# Optimizing a Trainium2 kernel written in Bass

```python
import jax, jax.numpy as jnp
from jax import lax
import numpy as np

D_MODEL = 1024
BATCH = 1
SEQ = 512
DEPTH = 1
DEC_BATCH = 8
DEC_SEQ = 16
PAST_LEN = 256

CHUNK = 64
N_MEM = 256
H_A = 8
HD_A = 128
H_KV = 2
H_IDX = 16
D_IDX = 64
TOPK_MAX = 256
Q_BLOCK = 128
H_G = 4
DK_G = 128
DV_G = 256
GATE_RANK = 16
GATE_TEMP = 16.0
H_M = 4
HD_M = 256
N_GROUPS = 4
E_PER_GROUP = 8
N_EXPERTS = N_GROUPS * E_PER_GROUP
D_EXPERT = 256
TOP_E = 2
MOE_BLOCK = 128
N_BRANCH = 3
EPS = 1e-6
NEG_INF = -1e30
SPLITS = (H_A * HD_A, H_KV * HD_A, H_KV * HD_A,
          H_IDX * D_IDX, D_IDX, H_IDX,
          H_G * DK_G, H_G * DK_G, H_G * DV_G,
          GATE_RANK, H_G * DV_G,
          H_M * HD_M,
          N_BRANCH * D_MODEL)
D_IN = sum(SPLITS)

kernel_name = 'hybrid_stream_dsa_gla_hmoe'

def rmsnorm(x, g):
    xf = x.astype(jnp.float32)
    y = xf * lax.rsqrt(jnp.mean(xf * xf, axis=-1, keepdims=True) + EPS)
    return (y * g).astype(x.dtype)

def split_cols(p):
    parts = []
    off = 0
    for n in SPLITS:
        parts.append(p[..., off:off + n])
        off += n
    return parts

def dsa_attend(q, qi, wi, k, v, ki, q_pos, k_pos, top_k):
    B, Tq = q.shape[:2]
    rel = jax.nn.relu(jnp.einsum('bthd,bsd->bths', qi, ki) * D_IDX ** -0.5)
    score = jnp.einsum('bth,bths->bts', wi, rel).astype(jnp.float32)
    adm = (k_pos[None, :] // CHUNK) <= (q_pos[:, None] // CHUNK)
    score = jnp.where(adm[None], score, NEG_INF)
    sel_score, sel_idx = lax.top_k(score, top_k)
    valid = sel_score > NEG_INF * 0.5
    k_sel = jax.vmap(lambda kb, ib: kb[ib])(k, sel_idx)
    v_sel = jax.vmap(lambda vb, ib: vb[ib])(v, sel_idx)
    qg = q.reshape(B, Tq, H_KV, H_A // H_KV, HD_A)
    logits = jnp.einsum('btgrd,btkgd->btgrk', qg, k_sel).astype(jnp.float32) * HD_A ** -0.5
    logits = jnp.where(valid[:, :, None, None, :], logits, NEG_INF)
    prob = jax.nn.softmax(logits, axis=-1).astype(v.dtype)
    o = jnp.einsum('btgrk,btkgd->btgrd', prob, v_sel)
    return o.reshape(B, Tq, H_A * HD_A)

def gla_chunked(q, k, v, log_a, s0, chunk):
    B, T, H, DK = q.shape
    DV = v.shape[-1]
    n = T // chunk
    r = lambda t: t.reshape(B, n, chunk, H, t.shape[-1])
    q, k, v = r(q), r(k), r(v)
    b = jnp.cumsum(r(log_a.astype(jnp.float32)), axis=2)
    b_last = b[:, :, -1:]
    qe = q * jnp.exp(b).astype(q.dtype)
    ke = k * jnp.exp(-b).astype(k.dtype)
    kd = k * jnp.exp(b_last - b).astype(k.dtype)
    causal = jnp.tril(jnp.ones((chunk, chunk), dtype=bool))
    att = jnp.where(causal, jnp.einsum('bnihk,bnjhk->bnhij', qe, ke), 0.0).astype(v.dtype)
    o_intra = jnp.einsum('bnhij,bnjhv->bnihv', att, v)
    decay = jnp.exp(b_last[:, :, 0]).astype(s0.dtype)

    def step(S, xs):
        qe_c, kd_c, v_c, dec_c, oi_c = xs
        o = oi_c + jnp.einsum('bihk,bhkv->bihv', qe_c, S)
        S = S * dec_c[..., None] + jnp.einsum('bjhk,bjhv->bhkv', kd_c, v_c)
        return S, o

    xs = (jnp.moveaxis(qe, 1, 0), jnp.moveaxis(kd, 1, 0), jnp.moveaxis(v, 1, 0),
          jnp.moveaxis(decay, 1, 0), jnp.moveaxis(o_intra, 1, 0))
    s_fin, o = lax.scan(step, s0, xs)
    return jnp.moveaxis(o, 0, 1).reshape(B, T, H, DV), s_fin

def memory_kv(mem, mem_norm_g, w_mem_kv, mem_k_norm_g):
    B, M, _ = mem.shape
    kv = rmsnorm(mem, mem_norm_g) @ w_mem_kv
    mk = rmsnorm(kv[..., :H_M * HD_M].reshape(B, M, H_M, HD_M), mem_k_norm_g)
    mv = kv[..., H_M * HD_M:].reshape(B, M, H_M, HD_M)
    return mk, mv

def mem_attend(q, mk, mv):
    B, T = q.shape[:2]
    logits = jnp.einsum('bthd,bmhd->bhtm', q, mk).astype(jnp.float32) * HD_M ** -0.5
    prob = jax.nn.softmax(logits, axis=-1).astype(mv.dtype)
    return jnp.einsum('bhtm,bmhd->bthd', prob, mv).reshape(B, T, H_M * HD_M)

def hmoe(x, ffn_norm_g, w_group_router, b_group_router, w_expert_router, b_expert_router,
         w_exp_gate, w_exp_up, w_exp_down):
    B, T, D = x.shape
    n = B * T
    blk = MOE_BLOCK if n % MOE_BLOCK == 0 else n
    h = rmsnorm(x, ffn_norm_g).reshape(n // blk, blk, D)

    def mix(hb):
        g_logit = (hb @ w_group_router + b_group_router).astype(jnp.float32)
        g_prob = jax.nn.softmax(g_logit, axis=-1)
        g_idx = jnp.argmax(g_logit, axis=-1)
        g_w = jnp.take_along_axis(g_prob, g_idx[:, None], axis=-1)
        e_logit = (hb @ w_expert_router + b_expert_router).astype(jnp.float32)
        e_logit = e_logit.reshape(-1, N_GROUPS, E_PER_GROUP)
        e_logit = jnp.take_along_axis(e_logit, g_idx[:, None, None], axis=1)[:, 0]
        top_p, top_i = lax.top_k(jax.nn.softmax(e_logit, axis=-1), TOP_E)
        top_p = top_p / jnp.sum(top_p, axis=-1, keepdims=True)
        expert_id = g_idx[:, None] * E_PER_GROUP + top_i
        combine = jnp.sum(jax.nn.one_hot(expert_id, N_EXPERTS, dtype=jnp.float32)
                          * (g_w * top_p)[..., None], axis=1)
        hid = jax.nn.silu(jnp.einsum('nd,edf->nef', hb, w_exp_gate)) * jnp.einsum('nd,edf->nef', hb, w_exp_up)
        return jnp.einsum('nef,efd->nd', hid * combine[..., None].astype(hid.dtype), w_exp_down)

    return lax.map(mix, h).reshape(B, T, D)

def layer_forward(x, mem_k, mem_v, past_k, past_v, past_ki, s0, top_k,
                  attn_norm_g, w_in, q_norm_g, k_norm_g, idx_k_norm_g,
                  w_gla_gate_up, b_gla_gate_up, gla_out_norm_g, mem_q_norm_g,
                  w_branch_a, w_branch_g, w_branch_m, w_out, ffn_norm_g,
                  w_group_router, b_group_router, w_expert_router, b_expert_router,
                  w_exp_gate, w_exp_up, w_exp_down):
    B, T, _ = x.shape
    past = 0 if past_k is None else past_k.shape[1]
    h = rmsnorm(x, attn_norm_g)
    (qa, ka, va, qi, ki, wi, qg, kg, vg, g_lr, g_out, qm, g_branch) = split_cols(h @ w_in)

    qa = rmsnorm(qa.reshape(B, T, H_A, HD_A), q_norm_g)
    ka = rmsnorm(ka.reshape(B, T, H_KV, HD_A), k_norm_g)
    va = va.reshape(B, T, H_KV, HD_A)
    qi = qi.reshape(B, T, H_IDX, D_IDX)
    ki = rmsnorm(ki, idx_k_norm_g)
    wi = wi * H_IDX ** -0.5
    if past_k is None:
        k_all, v_all, ki_all = ka, va, ki
    else:
        k_all = jnp.concatenate([past_k, ka], axis=1)
        v_all = jnp.concatenate([past_v, va], axis=1)
        ki_all = jnp.concatenate([past_ki, ki], axis=1)
    q_pos = past + jnp.arange(T)
    k_pos = jnp.arange(past + T)
    if T % Q_BLOCK == 0:
        nb = T // Q_BLOCK
        to_blocks = lambda t: jnp.moveaxis(t.reshape((B, nb, Q_BLOCK) + t.shape[2:]), 1, 0)
        o_a = lax.map(lambda xs: dsa_attend(xs[0], xs[1], xs[2], k_all, v_all, ki_all, xs[3], k_pos, top_k),
                      (to_blocks(qa), to_blocks(qi), to_blocks(wi), q_pos.reshape(nb, Q_BLOCK)))
        o_a = jnp.moveaxis(o_a, 0, 1).reshape(B, T, H_A * HD_A)
    else:
        o_a = dsa_attend(qa, qi, wi, k_all, v_all, ki_all, q_pos, k_pos, top_k)

    qg = qg.reshape(B, T, H_G, DK_G) * DK_G ** -0.5
    kg = kg.reshape(B, T, H_G, DK_G)
    vg = vg.reshape(B, T, H_G, DV_G)
    log_a = jax.nn.log_sigmoid((g_lr @ w_gla_gate_up + b_gla_gate_up).astype(jnp.float32)) / GATE_TEMP
    log_a = log_a.reshape(B, T, H_G, DK_G)
    chunk = CHUNK if T % CHUNK == 0 else T
    o_g, s_new = gla_chunked(qg, kg, vg, log_a, s0, chunk)
    o_g = rmsnorm(o_g, gla_out_norm_g).reshape(B, T, H_G * DV_G) * jax.nn.silu(g_out)

    qm = rmsnorm(qm.reshape(B, T, H_M, HD_M), mem_q_norm_g)
    o_m = mem_attend(qm, mem_k, mem_v)

    gt = jax.nn.sigmoid(g_branch.reshape(B, T, N_BRANCH, D_MODEL))
    merged = (gt[:, :, 0] * (o_a @ w_branch_a) + gt[:, :, 1] * (o_g @ w_branch_g)
              + gt[:, :, 2] * (o_m @ w_branch_m))
    x1 = x + merged @ w_out
    y = x1 + hmoe(x1, ffn_norm_g, w_group_router, b_group_router, w_expert_router, b_expert_router,
                  w_exp_gate, w_exp_up, w_exp_down)
    return y, ka, va, ki, s_new

def setup_inputs(seed: int = 0) -> dict:
    key = jax.random.key(seed)
    ks = iter(jax.random.split(key, 48))
    nrm = lambda shape, scale=1.0: jax.random.normal(next(ks), shape, jnp.float32) * scale
    gain = lambda shape: 1.0 + 0.1 * nrm(shape)
    D = D_MODEL
    return {
        'x_prompt': nrm((BATCH, SEQ, D)),
        'x_sample': nrm((DEC_BATCH, DEC_SEQ, D)),
        'mem_prompt': nrm((BATCH, N_MEM, D)),
        'cache_k': nrm((DEPTH, DEC_BATCH, PAST_LEN, H_KV, HD_A)),
        'cache_v': nrm((DEPTH, DEC_BATCH, PAST_LEN, H_KV, HD_A)),
        'cache_idx_k': nrm((DEPTH, DEC_BATCH, PAST_LEN, D_IDX)),
        'state_gla': nrm((DEPTH, DEC_BATCH, H_G, DK_G, DV_G)),
        'cache_mem_k': nrm((DEPTH, DEC_BATCH, N_MEM, H_M, HD_M)),
        'cache_mem_v': nrm((DEPTH, DEC_BATCH, N_MEM, H_M, HD_M)),
        'attn_norm_g': gain((DEPTH, D)),
        'w_in': nrm((DEPTH, D, D_IN), D ** -0.5),
        'q_norm_g': gain((DEPTH, HD_A)),
        'k_norm_g': gain((DEPTH, HD_A)),
        'idx_k_norm_g': gain((DEPTH, D_IDX)),
        'w_gla_gate_up': nrm((DEPTH, GATE_RANK, H_G * DK_G), GATE_RANK ** -0.5),
        'b_gla_gate_up': nrm((DEPTH, H_G * DK_G), 0.1),
        'gla_out_norm_g': gain((DEPTH, DV_G)),
        'mem_norm_g': gain((DEPTH, D)),
        'w_mem_kv': nrm((DEPTH, D, 2 * H_M * HD_M), D ** -0.5),
        'mem_q_norm_g': gain((DEPTH, HD_M)),
        'mem_k_norm_g': gain((DEPTH, HD_M)),
        'w_branch_a': nrm((DEPTH, H_A * HD_A, D), (H_A * HD_A) ** -0.5),
        'w_branch_g': nrm((DEPTH, H_G * DV_G, D), (H_G * DV_G) ** -0.5),
        'w_branch_m': nrm((DEPTH, H_M * HD_M, D), (H_M * HD_M) ** -0.5),
        'w_out': nrm((DEPTH, D, D), D ** -0.5),
        'ffn_norm_g': gain((DEPTH, D)),
        'w_group_router': nrm((DEPTH, D, N_GROUPS), D ** -0.5),
        'b_group_router': nrm((DEPTH, N_GROUPS), 0.01),
        'w_expert_router': nrm((DEPTH, D, N_EXPERTS), D ** -0.5),
        'b_expert_router': nrm((DEPTH, N_EXPERTS), 0.01),
        'w_exp_gate': nrm((DEPTH, N_EXPERTS, D, D_EXPERT), D ** -0.5),
        'w_exp_up': nrm((DEPTH, N_EXPERTS, D, D_EXPERT), D ** -0.5),
        'w_exp_down': nrm((DEPTH, N_EXPERTS, D_EXPERT, D), D_EXPERT ** -0.5),
    }

def reference(x_prompt, x_sample, mem_prompt, cache_k, cache_v, cache_idx_k, state_gla,
              cache_mem_k, cache_mem_v, attn_norm_g, w_in, q_norm_g, k_norm_g, idx_k_norm_g,
              w_gla_gate_up, b_gla_gate_up, gla_out_norm_g, mem_norm_g, w_mem_kv,
              mem_q_norm_g, mem_k_norm_g, w_branch_a, w_branch_g, w_branch_m, w_out,
              ffn_norm_g, w_group_router, b_group_router, w_expert_router, b_expert_router,
              w_exp_gate, w_exp_up, w_exp_down):
    top_k_prompt = min(TOPK_MAX, x_prompt.shape[1] // 4)
    top_k_sample = min(TOPK_MAX, (cache_k.shape[2] + x_sample.shape[1]) // 4)
    y_p, y_s = x_prompt, x_sample
    kp, vp, kip, sp, mkp, mvp = [], [], [], [], [], []
    ks_, vs_, kis, ss = [], [], [], []
    for l in range(DEPTH):
        lw = (attn_norm_g[l], w_in[l], q_norm_g[l], k_norm_g[l], idx_k_norm_g[l],
              w_gla_gate_up[l], b_gla_gate_up[l], gla_out_norm_g[l], mem_q_norm_g[l],
              w_branch_a[l], w_branch_g[l], w_branch_m[l], w_out[l], ffn_norm_g[l],
              w_group_router[l], b_group_router[l], w_expert_router[l], b_expert_router[l],
              w_exp_gate[l], w_exp_up[l], w_exp_down[l])
        mk_p, mv_p = memory_kv(mem_prompt, mem_norm_g[l], w_mem_kv[l], mem_k_norm_g[l])
        s0 = jnp.zeros((x_prompt.shape[0], H_G, DK_G, DV_G), x_prompt.dtype)
        y_p, k_new, v_new, ki_new, s_new = layer_forward(y_p, mk_p, mv_p, None, None, None, s0,
                                                          top_k_prompt, *lw)
        kp.append(k_new); vp.append(v_new); kip.append(ki_new); sp.append(s_new)
        mkp.append(mk_p); mvp.append(mv_p)
        y_s, k_new, v_new, ki_new, s_new = layer_forward(y_s, cache_mem_k[l], cache_mem_v[l], cache_k[l],
                                                          cache_v[l], cache_idx_k[l], state_gla[l],
                                                          top_k_sample, *lw)
        ks_.append(k_new); vs_.append(v_new); kis.append(ki_new); ss.append(s_new)
    new_k_prompt = jnp.stack(kp)
    new_v_prompt = jnp.stack(vp)
    new_idx_k_prompt = jnp.stack(kip)
    new_state_gla_prompt = jnp.stack(sp)
    new_mem_k_prompt = jnp.stack(mkp)
    new_mem_v_prompt = jnp.stack(mvp)
    new_k_sample = jnp.stack(ks_)
    new_v_sample = jnp.stack(vs_)
    new_idx_k_sample = jnp.stack(kis)
    new_state_gla_sample = jnp.stack(ss)
    return (y_p, y_s, new_k_prompt, new_v_prompt, new_idx_k_prompt, new_state_gla_prompt,
            new_mem_k_prompt, new_mem_v_prompt, new_k_sample, new_v_sample, new_idx_k_sample,
            new_state_gla_sample)


_drawn_inputs = setup_inputs


def setup_inputs(seed=0):
    import zlib

    import numpy as np

    out = dict(_drawn_inputs(seed))
    spreads = {}
    factors = {}
    for name, (base, spread) in spreads.items():
        noise = np.random.default_rng([zlib.crc32(name.encode()), seed]).standard_normal(out[name].shape)
        drawn = base * np.exp(spread * noise) if base else spread * noise
        out[name] = __import__('jax').numpy.asarray(drawn.astype(out[name].dtype))
    for name, factor in factors.items():
        out[name] = (out[name] * factor).astype(out[name].dtype)
    return out
```

```python
from contextlib import ExitStack

import concourse.bass as bass
from concourse import mybir

F32 = mybir.dt.float32
I32 = mybir.dt.int32
U32 = mybir.dt.uint32
ALU = mybir.AluOpType
ACT = mybir.ActivationFunctionType
AX_X = mybir.AxisListType.X

P = 128
BANK = 512
CHUNK = 64
EPS = 1e-6
NEG = -1e30
TAKEN = -3e38
GATE_TEMP = 16.0
TOPK_MAX = 256


def build(nc, a, o):
    _, TP, D = a["x_prompt"].shape
    B, TB, _ = a["x_sample"].shape
    TS = B * TB
    PAST = a["cache_k"].shape[2]
    KV, HD = a["cache_k"].shape[3:]
    DI = a["cache_idx_k"].shape[3]
    M, HM, HDM = a["cache_mem_k"].shape[2:]
    HG, DK, DV = a["state_gla"].shape[2:]
    RANK = a["w_gla_gate_up"].shape[1]
    HA = a["w_branch_a"].shape[1] // HD
    NG = a["w_group_router"].shape[2]
    NE, _, DF = a["w_exp_gate"].shape[1:]
    EPG = NE // NG
    D_IN = a["w_in"].shape[2]
    HI = (D_IN - (HA + 2 * KV) * HD - DI - 2 * HG * DK - 2 * HG * DV - RANK - HM * HDM - 3 * D) // (DI + 1)
    KD = D // P
    T = TP + TS
    NTP = TP // P
    NT = T // P
    NM = M // P
    TOPK_P = min(TOPK_MAX, TP // 4)
    TOPK_S = min(TOPK_MAX, (PAST + TB) // 4)
    GQ = HA // KV
    PB = PAST // P
    KS = PAST + TS
    assert TS == P and TP == 4 * P and D == 8 * P and HD == P and DK == P and GQ == 4 and HM * HDM == D
    assert DI == 64 and HI == 16 and HG == 4 and DV == 256 and NM == 2 and PB == 2 and 4 * DF == D
    sizes = [HA * HD, KV * HD, KV * HD, HI * DI, DI, HI, HG * DK, HG * DK, HG * DV, RANK, HG * DV, HM * HDM, 3 * D]
    offs = [sum(sizes[:n]) for n in range(len(sizes))]
    (C_QA, C_KA, C_VA, C_QI, C_KI, C_WI, C_QG, C_KG, C_VG, C_LR, C_GO, C_QM, C_GB) = offs
    assert offs[-1] + sizes[-1] == D_IN

    CAP = 64
    N_PAIR = 2 * T
    N_OVER = N_PAIR // (CAP + 1)
    N_SLOT = NE + N_OVER
    M_OVER = (T - 1) // CAP
    slot_rows = nc.dram_tensor("slot_rows", [N_SLOT * CAP, D], F32, kind="Internal").ap()

    w_in = a["w_in"][0].rearrange("(k p) c -> p k c", p=P)
    w_mem = a["w_mem_kv"][0].rearrange("(k p) c -> p k c", p=P)
    w_out = a["w_out"][0].rearrange("(k p) c -> p k c", p=P)
    w_br = [a["w_branch_" + n][0].rearrange("(k p) c -> p k c", p=P) for n in "gma"]
    w_gate, w_up = (a[n][0].rearrange("e (k p) f -> e p k f", p=P) for n in ("w_exp_gate", "w_exp_up"))
    w_down = a["w_exp_down"][0].rearrange("e (f p) c -> e p f c", p=P)
    xp = a["x_prompt"][0].rearrange("(t p) d -> t p d", p=P)
    xs = a["x_sample"].rearrange("b t d -> (b t) d")
    memx = a["mem_prompt"][0].rearrange("(t p) d -> t p d", p=P)
    x_tile = [xp[t] for t in range(NTP)] + [xs]

    with ExitStack() as ctx:
        def sb(name, words, dt=F32):
            return ctx.enter_context(nc.sbuf_tensor(name, [P, words], dt))

        def sem(name):
            return ctx.enter_context(nc.semaphore(name))

        HTW, MGW, RGW, TWW = KD * (T + M), KD * T, 2 * KD * BANK, 4 * KD * P
        EW = 3 * KD * DF
        NES = 4
        bulk = sb("bulk", HTW + MGW + RGW + TWW)
        assert HTW + MGW + RGW + TWW == NES * EW
        hT = bulk[:, 0:HTW].rearrange("p (k t) -> p k t", k=KD)
        region_m = bulk[:, HTW:HTW + MGW]
        merged = region_m.rearrange("p (k t) -> p k t", k=KD)
        region_r = bulk[:, HTW + MGW:HTW + MGW + RGW]
        ring = [region_r[:, s * KD * BANK:(s + 1) * KD * BANK].rearrange("p (k c) -> p k c", k=KD) for s in range(2)]
        region_t = bulk[:, HTW + MGW + RGW:]
        tw = [region_t[:, s * KD * P:(s + 1) * KD * P].rearrange("p (k c) -> p k c", k=KD) for s in range(4)]
        ew = [bulk[:, s * EW:(s + 1) * EW] for s in range(NES)]
        ew_gate = [w[:, 0:KD * DF].rearrange("p (k f) -> p k f", k=KD) for w in ew]
        ew_up = [w[:, KD * DF:2 * KD * DF].rearrange("p (k f) -> p k f", k=KD) for w in ew]
        ew_down = [w[:, 2 * KD * DF:].rearrange("p (f c) -> p f c", f=DF // P) for w in ew]

        arena = sb("arena", 80 * 256)

        def cut(region, kib, words):
            w0 = int(kib * 256)
            return region[:, w0:w0 + words]

        work_w = [(t + 1) * P for t in range(NTP)] + [KS]
        work_all = sb("work_all", sum(work_w))
        work = [work_all[:, sum(work_w[:t]):sum(work_w[:t + 1])] for t in range(NT)]
        mix = sb("mix", 4 * T)
        sg = [mix[:, q * T:(q + 1) * T] for q in range(2)]
        prod = [mix[:, (2 + q) * T:(3 + q) * T] for q in range(2)]
        sq = [mix[:, q * BANK:(q + 1) * BANK] for q in range(2)]
        qn = [mix[:, (2 + q) * BANK:(3 + q) * BANK] for q in range(2)]
        cst = sb("cst", 8 * P)
        ident, cum_p, suf_p, cum_s, suf_s, before, ones, other = (cst[:, n * P:(n + 1) * P] for n in range(8))
        bsel = sb("bsel", B)
        g_ki = sb("g_ki", DI)
        g_ka = sb("g_ka", HD)
        g_mk = sb("g_mk", HDM)
        gcols = sb("gcols", 8)
        gcol_q, gcol_o, gcol_qm = gcols[:, 0:1], gcols[:, 1:3], gcols[:, 3:5]
        wsm = sb("wsm", KD * (DI + HI + RANK))
        wsm = wsm[:, :].rearrange("p (k c) -> p k c", k=KD)
        wga = sb("wga", HG * DK)
        wi = sb("wi", NT * HI)
        wi = wi[:, :].rearrange("p (t h) -> p t h", t=NT)
        st = sb("st", 256)
        ss0, rs0 = st[:, 0:8], st[:, 8:16]
        ssk, rsk = st[:, 16:24], st[:, 24:32]
        ssn, rsn = st[:, 32:36], st[:, 36:40]
        sso, rso = st[:, 40:44], st[:, 44:48]
        dec = st[:, 48:80].rearrange("p (h c) -> p h c", h=HG)
        mx, nmx, sm, rsm = (st[:, 80 + 8 * n:88 + 8 * n] for n in range(4))
        top8 = st[:, 112:120]
        top8s = st[:, 120:128]
        newton = st[:, 144:152]
        ssf, rsf = st[:, 128:136], st[:, 136:144]

        ps = [ctx.enter_context(nc.psum_tensor(f"ps{n}", [P, BANK], F32)) for n in range(8)]

        xt = cut(arena, 0, (NT + NM) * D).rearrange("p (t d) -> p t d", d=D)
        qiT = cut(arena, 28, KD * T).rearrange("p (k t) -> p k t", k=KD)
        ci = cut(arena, 48, B * PB * P).rearrange("p (b s d) -> p b s d", b=B, s=PB)
        ciT = cut(arena, 56, B * PAST).rearrange("p (b s) -> p b s", b=B)
        wdiag = cut(arena, 0, HI * TS).rearrange("p (h t) -> p h t", h=HI)
        g_x, g_mem = cut(arena, 64, D), cut(arena, 68, D)
        kiT = cut(arena, 72.5, T)
        zrow = cut(arena, 76, D)
        wB = cut(region_m, 0, HI * TS).rearrange("p (h t) -> p h t", h=HI)
        rel = [cut(region_m, 8 + 2 * n, BANK) for n in range(3)]
        sT = cut(region_m, 14, PB * TS).rearrange("p (s t) -> p s t", s=PB)
        sct = [cut(region_m, 15 + n, HI * TB) for n in range(2)]
        kid = cut(region_m, 17, NT * P).rearrange("p (t d) -> p t d", t=NT)
        qkT = cut(arena, 0, 2 * HG * T).rearrange("p (h t) -> p h t", h=2 * HG)
        goT = cut(arena, 20, KD * T).rearrange("p (k t) -> p k t", k=KD)
        vg = cut(arena, 40, NT * HG * DV).rearrange("p (t c) -> p t c", t=NT)
        la = cut(arena, 60, NT * HG * DK).rearrange("p (t c) -> p t c", t=NT)
        glrT = cut(arena, 70, T)
        zabs = cut(region_m, 0, NT * HG * DK).rearrange("p (t c) -> p t c", t=NT)
        state = cut(region_m, 0, HG * DV).rearrange("p (h v) -> p h v", h=HG)
        state_s = [cut(region_m, 4 + 4 * n, HG * DV).rearrange("p (h v) -> p h v", h=HG) for n in range(3)]
        on = cut(region_m, 16, HG * DV)
        qem = cut(region_r, 0, B * (HG * P + TB))
        glt = [cut(region_r, 17 + 2 * n, BANK) for n in range(7)] + [cut(arena, 76.5, BANK)]
        eb, enb, qe, ke, kd, attm_p, attm_s, kdf = (v.rearrange("p (h t) -> p h t", h=HG) for v in glt)
        kdm = [v.rearrange("p (h t) -> p h t", h=HG) for v in (cut(arena, 72.5, BANK), cut(arena, 74.5, BANK))]
        mv = cut(arena, 0, NM * D).rearrange("p (m c) -> p m c", m=NM)
        mkT = cut(arena, 8, KD * M).rearrange("p (k m) -> p k m", k=KD)
        qmT = cut(arena, 16, KD * T).rearrange("p (k t) -> p k t", k=KD)
        pmT = cut(arena, 36, NM * HM * T).rearrange("p (m h t) -> p m h t", m=NM, h=HM)
        kmT = [cut(arena, 36 + 8 * n, KD * M).rearrange("p (k m) -> p k m", k=KD) for n in range(2)]
        mkn = cut(arena, 56, NM * D).rearrange("p (m c) -> p m c", m=NM)
        pm = [cut(arena, 56 + 4 * n, HM * M) for n in range(2)]
        kvb = [cut(arena, 64 + 8 * n, NM * D).rearrange("p (m c) -> p m c", m=NM) for n in range(2)]
        lmT = cut(arena, 52, NM * HM * TS).rearrange("p (m h t) -> p m h t", m=NM, h=HM)
        qaT = cut(arena, 0, KD * T).rearrange("p (k t) -> p k t", k=KD)
        kT = cut(arena, 20, KV * T).rearrange("p (k t) -> p k t", k=KV)
        va = cut(arena, 25, NT * KV * HD).rearrange("p (t c) -> p t c", t=NT)
        kn = cut(arena, 30, NT * KV * HD).rearrange("p (t c) -> p t c", t=NT)
        kc = cut(arena, 35, B * PB * KV * HD).rearrange("p (b s c) -> p b s c", b=B, s=PB)
        kcT = cut(arena, 51, B * KV * PAST).rearrange("p (b k s) -> p b k s", b=B, k=KV)
        paT = [cut(arena, 51 + 8 * n, 4 * BANK).rearrange("p (s h t) -> p s h t", s=4, h=GQ) for n in range(2)]
        lsT = cut(arena, 67, KV * PB * BANK).rearrange("p (k s h t) -> p k s h t", k=KV, s=PB, h=GQ)
        lg = [mix[:, q * BANK:(q + 1) * BANK] for q in range(2)]
        pr = [mix[:, (2 + q) * BANK:(3 + q) * BANK] for q in range(2)]
        xr = cut(arena, 0, NT * D).rearrange("p (t d) -> p t d", t=NT)
        x1 = cut(arena, 20, NT * D).rearrange("p (t d) -> p t d", t=NT)
        h2 = cut(arena, 40, NT * D).rearrange("p (t d) -> p t d", t=NT)
        h2T = cut(arena, 60, KD * T).rearrange("p (k t) -> p k t", k=KD)
        g_ffn = tw[0].rearrange("p k c -> p (k c)")
        NR = NG + NE
        w_rt = tw[1].rearrange("p k c -> p (k c)")[:, 0:KD * NR].rearrange("p (k c) -> p k c", k=KD)
        b_rt = tw[2].rearrange("p k c -> p (k c)")[:, 0:NR]
        rti = sb("rti", 64, I32)
        rt = ew[3]
        rt3 = [rt[:, n * NT * NE:(n + 1) * NT * NE].rearrange("p (t e) -> p t e", t=NT) for n in range(8)]
        hot0, hot1, hot_both, el, elm, r_tmp, iota_e, iota_g = rt3
        r0 = 8 * NT * NE
        lt = rt[:, r0:r0 + NT * NR].rearrange("p (t c) -> p t c", t=NT)
        r1 = r0 + NT * NR
        nov_t = rt[:, r1:r1 + NE * M_OVER].rearrange("p (e m) -> p e m", e=NE)
        assert r1 + NE * M_OVER <= 2048
        rs = sb("rs", 512)
        rs5 = [rs[:, n * NT:(n + 1) * NT] for n in range(24)]
        rsE = [rs[:, 128 + n * NE:128 + (n + 1) * NE] for n in range(6)]
        gs5 = rs[:, 320:320 + NT * NG].rearrange("p (t g) -> p t g", t=NT)
        ge5 = rs[:, 340:340 + NT * NG].rearrange("p (t g) -> p t g", t=NT)
        thr = rs[:, 360:360 + M_OVER]
        ovs = rs[:, 380:380 + N_OVER]
        rowi = rs[:, 400:400 + N_OVER]
        rows = rti[:, 24:24 + 2 * NT].rearrange("p (t j) -> p t j", j=2)
        hs = [cut(arena, 4 * n, D) for n in range(NES)]
        hsT = [cut(arena, 16 + 2 * n, KD * CAP).rearrange("p (k t) -> p k t", k=KD) for n in range(2)]
        hid = [cut(arena, 68 + n, DF // P * CAP) for n in range(2)]
        act_g = [cut(arena, 70 + n, DF // P * CAP) for n in range(2)]
        oT = [cut(arena, 40 + 2 * n, KD * CAP).rearrange("p (k t) -> p k t", k=KD) for n in range(2)]
        ysl = [cut(arena, 44 + 4 * n, D) for n in range(2)]
        yg = [cut(arena, 52 + 4 * n, D) for n in range(4)]

        x_in = [sem(f"x_in{t}") for t in range(3)]
        ring_in = [sem(f"ring_in{s}") for s in range(2)]
        tw_in = [sem(f"tw_in{s}") for s in range(4)]
        wsm_in, gain_in, ci_in, kc_in, vc_in, xr_in, rtw_in = (
            sem(n) for n in ("wsm_in", "gain_in", "ci_in", "kc_in", "vc_in", "xr_in", "rtw_in"))
        const_ok, zero_ok = sem("const_ok"), sem("zero_ok")
        dve_step, act_step, pool_step = sem("dve_step"), sem("act_step"), sem("pool_step")
        ss_ok, xn_ok, xT_full, hT_ok = sem("ss_ok"), sem("xn_ok"), sem("xT_full"), sem("hT_ok")
        kiw_full, kiss_ok, kid_ok, glr_full, glr_ok, kidT_full, kiT_ok = (
            sem(n) for n in ("kiw_full", "kiss_ok", "kid_ok", "glr_full", "glr_ok", "kidT_full", "kiT_ok"))
        t_full = [sem(f"t_full{s}") for s in range(4)]
        t_free = [sem(f"t_free{s}") for s in range(4)]
        sc_full = [sem(f"sc_full{n}") for n in range(3)]
        rel_ok = [sem(f"rel_ok{n}") for n in range(3)]
        acc_ok = sem("acc_ok")
        ciT_full, ciT_ok, wd_ok = (sem(n) for n in ("ciT_full", "ciT_ok", "wd_ok"))
        scs_full, scs_ok = sem("scs_full"), sem("scs_ok")
        n_full, n_free_act = sem("n_full"), sem("n_free_act")
        sq_ok, qn_ok, qT_full, qT_ok, kv_ok = (sem(n) for n in ("sq_ok", "qn_ok", "qT_full", "qT_ok", "kv_ok"))
        z_full, z_ok, la_ok = (sem(n) for n in ("z_full", "z_ok", "la_ok"))
        bT_full, suf_full, kt_full, eb_ok, kdf_ok, qe_ok, kd_ok, att_full, attm_ok = (
            sem(n) for n in ("bT_full", "suf_full", "kt_full", "eb_ok", "kdf_ok", "qe_ok", "kd_ok", "att_full", "attm_ok"))
        kv_full, state_ok, o_full, oss_ok, on_ok, oT_full, og_ok = (
            sem(n) for n in ("kv_full", "state_ok", "o_full", "oss_ok", "on_ok", "oT_full", "og_ok"))
        st_in = [sem(f"st_in{n}") for n in range(3)]
        st_out = [sem(f"st_out{n}") for n in range(3)]
        kdm_ok, qem_ok, kvs_full, states_ok = sem("kdm_ok"), sem("qem_ok"), sem("kvs_full"), sem("states_ok")
        sg_ok = [sem(f"sg_ok{q}") for q in range(2)]
        m_prod = [sem(f"m_prod{q}") for q in range(2)]
        merged_ok = sem("merged_ok")
        kvb_in = [sem(f"kvb_in{n}") for n in range(2)]
        kmT_full, kmT_ok, lmT_full, lmT_ok, mk_used = (
            sem(n) for n in ("kmT_full", "kmT_ok", "lmT_full", "lmT_ok", "mk_used"))
        lm_full, mmx_ok, pm_ok, pmn_ok, pmT_full, pmT_ok, om_full, om_ok = (
            sem(n) for n in ("lm_full", "mmx_ok", "pm_ok", "pmn_ok", "pmT_full", "pmT_ok", "om_full", "om_ok"))
        kcT_full, kcT_ok, lsT_full, lsT_ok = (sem(n) for n in ("kcT_full", "kcT_ok", "lsT_full", "lsT_ok"))
        lg_full, lg_ok, pr_ok, prn_ok, prT_full, prT_ok, oa_full, oa_ok = (
            sem(n) for n in ("lg_full", "lg_ok", "pr_ok", "prn_ok", "prT_full", "prT_ok", "oa_full", "oa_ok"))
        x1_ok, ssf_ok, h2_ok, h2T_full, h2T_ok, rt_full, rt_step = (
            sem(n) for n in ("x1_ok", "ssf_ok", "h2_ok", "h2T_full", "h2T_ok", "rt_full", "rt_step"))
        rank_full, pos_ok, scat = sem("rank_full"), sem("pos_ok"), sem("scat")
        ew_in = [sem(f"ew_in{s}") for s in range(NES)]
        (hsT_full, hsT_ok, gu_full, silu_ok, hid_ok, dn_full, oTs_ok, y_full, ysl_ok) = (
            sem(n) for n in ("hsT_full", "hsT_ok", "gu_full", "silu_ok", "hid_ok", "dn_full", "oTs_ok", "y_full", "ysl_ok"))
        ysl_out = [sem(f"ysl_out{n}") for n in range(2)]
        early_out, mem_out, kv_out, fill_ok = (sem(n) for n in ("early_out", "mem_out", "kv_out", "fill_ok"))
        yg_in, yg_used = [sem(f"yg_in{n}") for n in range(2)], sem("yg_used")
        pe_seen = sem("pe_seen")
        out_done = sem("out_done")

        fills, items = [], []

        def plan(kind, weights, col, n_fill, tiles):
            for c in range(n_fill):
                for t in tiles:
                    items.append((kind, len(fills), t, c))
                fills.append((weights, col + c * BANK))

        every, mems = list(range(NT)), list(range(NM))
        plan("vg", w_in, C_VG, HG * DV // BANK, every)
        plan("mk", w_mem, 0, D // BANK, mems)
        plan("mv", w_mem, D, D // BANK, mems)
        plan("qm", w_in, C_QM, HM * HDM // BANK, every)
        plan("kv", w_in, C_KA, 1, every)
        plan("qa", w_in, C_QA, HA * HD // BANK, every)
        plan("out", w_out, 0, D // BANK, every)
        NORMED = ("mk", "qm", "kv", "qa")
        index = {kind: [n for n, it in enumerate(items) if it[0] == kind] for kind in ("vg", "mk", "mv", "qm", "kv", "qa", "out")}
        normed = [n for n, it in enumerate(items) if it[0] in NORMED]
        by_act = [n for n, it in enumerate(items) if it[0] in ("vg", "mv")]

        last_item = [max(n for n, it in enumerate(items) if it[1] == f) for f in range(len(fills))]
        N_CONST, N_GAINS, N_TABLES = 24, 10, 1
        N_REL = (NT - 1) * HI

        def item_out(n):
            if n in normed:
                return qn_ok, normed.index(n) + 1
            if n in by_act:
                return n_free_act, by_act.index(n) + 1
            return x1_ok, index["out"].index(n) + 1

        def normed_before(kind):
            return normed.index(index[kind][-1]) + 1

        U_QI, U_QK, U_GO, U_MERGE = 0, 2, 4, [6, 10, 14]

        BR_GATE = [1, 2, 0]
        s_tiles = [NT - 1] + list(range(NTP))

        block = ctx.enter_context(nc.Block())

        @block.sync
        def _(sp):
            for t in range(NT):
                sp.dma_start(xt[:, t, :], x_tile[t]).then_inc(x_in[min(t, 2)], 16)
            for m in range(NM):
                sp.dma_start(xt[:, NT + m, :], memx[m]).then_inc(x_in[2], 16)
            sp.dma_start(wsm[:, :, 0:DI + HI], w_in[:, :, C_KI:C_KI + DI + HI]).then_inc(wsm_in, 16)
            sp.dma_start(wsm[:, :, DI + HI:], w_in[:, :, C_LR:C_LR + RANK]).then_inc(wsm_in, 16)

            def narrow_job(col, u):
                with sp.Fori(0, 2) as i:
                    for s in range(4):
                        at = sp.snap(i * (4 * P) + (col + s * P))
                        sp.wait_ge(t_full[s], i + u)
                        sp.dma_start(tw[s], w_in[:, :, bass.ds(at, P)]).then_inc(tw_in[s], 16)

            def merge_job(br, u):
                with sp.Fori(0, 4) as i:
                    for q in range(2):
                        sp.wait_ge(t_full[2 * q + 1], i + u)
                        sp.dma_start(tw[2 * q + 1], w_br[br][:, :, bass.ds(i * (2 * P) + q * P, P)]).then_inc(tw_in[2 * q + 1], 16)
                        sp.wait_ge(t_full[2 * q], i + u)
                        sp.dma_start(tw[2 * q], w_in[:, :, bass.ds(i * (2 * P) + (C_GB + BR_GATE[br] * D + q * P), P)])\
                          .then_inc(tw_in[2 * q], 16)

            def wide_fill(f):
                if f >= 2:
                    sp.wait_ge(n_full, last_item[f - 2] + 1)
                src, col = fills[f]
                sp.dma_start(ring[f % 2], src[:, :, col:col + BANK]).then_inc(ring_in[f % 2], 16)

            narrow_job(C_QI, U_QI)
            wide_fill(0)
            wide_fill(1)
            narrow_job(C_QG, U_QK)
            narrow_job(C_GO, U_GO)
            merge_job(0, U_MERGE[0])
            sp.wait_ge(og_ok, NT)
            for f in range(2, 8):
                wide_fill(f)
            merge_job(1, U_MERGE[1])
            for f in range(8, 11):
                wide_fill(f)
            merge_job(2, U_MERGE[2])
            for f in range(11, 13):
                wide_fill(f)
            for s in range(4):
                sp.wait_ge(t_full[s], U_MERGE[2] + 4)
            sp.dma_start(g_ffn, a["ffn_norm_g"].partition_broadcast(P)).then_inc(rtw_in, 16)
            sp.dma_start(w_rt[:, :, 0:NG], a["w_group_router"][0].rearrange("(k p) g -> p k g", p=P)).then_inc(rtw_in, 16)
            sp.dma_start(w_rt[:, :, NG:NR], a["w_expert_router"][0].rearrange("(k p) g -> p k g", p=P)).then_inc(rtw_in, 16)
            sp.dma_start(b_rt[:, 0:NG], a["b_group_router"].partition_broadcast(P)).then_inc(rtw_in, 16)
            sp.dma_start(b_rt[:, NG:NR], a["b_expert_router"].partition_broadcast(P)).then_inc(rtw_in, 16)

            def load_expert(s, e, done):
                sp.dma_start(ew_gate[s], w_gate[e] if isinstance(e, int) else w_gate[bass.ds(e, 1)].squeeze(0)).then_inc(done, 16)
                sp.dma_start(ew_up[s], w_up[e] if isinstance(e, int) else w_up[bass.ds(e, 1)].squeeze(0)).then_inc(done, 16)
                sp.dma_start(ew_down[s], w_down[e] if isinstance(e, int) else w_down[bass.ds(e, 1)].squeeze(0)).then_inc(done, 16)

            def load_rows(s, row, done):
                sp.dma_start(hs[s][0:CAP, :], slot_rows[bass.ds(row, CAP), :]).then_inc(done, 16)

            sp.wait_ge(x1_ok, 2 * NT)
            for s in range(3):
                load_expert(s, s, ew_in[s])
            sp.wait_ge(pos_ok, 1)
            load_expert(3, 3, ew_in[3])
            sp.wait_ge(scat, 32 * NT)
            for s in range(NES):
                load_rows(s, s * CAP, ew_in[s])
            with sp.Fori(1, NE // NES) as i:
                for s in range(NES):
                    e = sp.snap(i * NES + s)
                    row = sp.snap(i * (NES * CAP) + s * CAP)
                    sp.wait_ge(dn_full, i * NES + (s + 1 - NES))
                    load_expert(s, e, ew_in[s])
                    load_rows(s, row, ew_in[s])

            over = sp.value_load(rti[0:1, N_OVER:N_OVER + 1], min_val=0, max_val=N_OVER)
            sp.wait_ge(dn_full, NE)
            with sp.If(over > 0):
                with sp.Fori(0, N_OVER) as i:
                    sp.wait_ge(dn_full, i + NE)
                    e = sp.value_load(rti[0:1, bass.ds(i, 1)], min_val=0, max_val=NE - 1)
                    load_expert(0, e, ew_in[0])
                    load_rows(0, i * CAP + NE * CAP, ew_in[0])

        @block.tensor
        def _(pe):
            mm, tr = nc.tensor.matmul, nc.tensor.transpose

            pe.wait_ge(const_ok, N_CONST)
            for t in range(NT + NM):
                pe.wait_ge(xn_ok, t + 1)
                for h in range(2):
                    n = 2 * t + h
                    if n >= 2:
                        pe.wait_ge(hT_ok, n - 1)
                    for k in range(4):
                        last = tr(ps[n % 2][:, k * P:(k + 1) * P], xt[:, t, (4 * h + k) * P:(4 * h + k + 1) * P], ident)
                    last.then_inc(xT_full, 1)

            pe.wait_ge(hT_ok, 2 * (NT + NM))
            pe.wait_ge(wsm_in, 32)
            for t in range(NT):
                if t >= 2:
                    pe.wait_ge(kid_ok, t - 1)
                for k in range(KD):
                    last = mm(ps[2 + t % 2][:, 0:DI + HI], hT[:, k, t * P:(t + 1) * P], wsm[:, k, 0:DI + HI],
                              start=k == 0, stop=k == KD - 1)
                last.then_inc(kiw_full, 1)
            for k in range(KD):
                mm(ps[4][0:RANK, 0:TP], wsm[:, k, DI + HI:], hT[:, k, 0:TP], start=k == 0, stop=k == KD - 1)
            for k in range(KD):
                last = mm(ps[5][0:RANK, 0:TS], wsm[:, k, DI + HI:], hT[:, k, TP:T], start=k == 0, stop=k == KD - 1)
            last.then_inc(glr_full, 1)
            pe.wait_ge(kid_ok, NT)
            for t in range(NT):
                last = tr(ps[6 + t // 4][:, (t % 4) * P:(t % 4 + 1) * P], kid[:, t, :], ident)
            last.then_inc(kidT_full, 1)

            def narrow_job(u):
                with pe.Fori(0, 2) as i:
                    for s in range(4):
                        b = 2 * (s % 2)
                        pe.wait_ge(tw_in[s], i * 16 + (u + 1) * 16)
                        if s >= 2:
                            pe.wait_ge(t_free[s - 2], i + (u + 1))
                        else:
                            pe.wait_ge(t_free[s + 2], i + u)
                        for k in range(KD):
                            mm(ps[b][:, 0:TP], tw[s][:, k, :], hT[:, k, 0:TP], start=k == 0, stop=k == KD - 1)
                            last = mm(ps[b + 1][:, 0:TS], tw[s][:, k, :], hT[:, k, TP:T], start=k == 0, stop=k == KD - 1)
                        last.then_inc(t_full[s], 1)

            def merge_job(u, m):
                src = (goT, qmT, qaT)[m]
                with pe.Fori(0, 4) as i:
                    for q in range(2):
                        pe.wait_ge(m_prod[q], i + 4 * m)
                        pe.wait_ge(tw_in[2 * q], i * 16 + (u + 1) * 16)
                        for k in range(KD):
                            mm(ps[4 * q + 1][:, 0:TP], tw[2 * q][:, k, :], hT[:, k, 0:TP], start=k == 0, stop=k == KD - 1)
                            last = mm(ps[4 * q + 3][:, 0:TS], tw[2 * q][:, k, :], hT[:, k, TP:T],
                                      start=k == 0, stop=k == KD - 1)
                        last.then_inc(t_full[2 * q], 1)
                        pe.wait_ge(tw_in[2 * q + 1], i * 16 + (u + 1) * 16)
                        for k in range(KD):
                            mm(ps[4 * q][:, 0:TP], tw[2 * q + 1][:, k, :], src[:, k, 0:TP], start=k == 0, stop=k == KD - 1)
                            last = mm(ps[4 * q + 2][:, 0:TS], tw[2 * q + 1][:, k, :], src[:, k, TP:T],
                                      start=k == 0, stop=k == KD - 1)
                        last.then_inc(t_full[2 * q + 1], 1)

            def item_transposes(n):
                kind, _, t, c = items[n]
                j = normed.index(n)
                src = {"mk": mkn[:, t % NM, c * BANK:(c + 1) * BANK], "kv": kn[:, t, :]}.get(kind, qn[j % 2])
                pe.wait_ge(qn_ok, j + 1)
                if j >= 2:
                    pe.wait_ge(qT_ok, j - 1)
                for k in range(KV if kind == "kv" else 4):
                    last = tr(ps[6 + j % 2][:, k * P:(k + 1) * P], src[:, k * P:(k + 1) * P], ident)
                last.then_inc(qT_full, 1)

            def project(kinds):
                lag = None
                for n, (kind, f, t, c) in enumerate(items):
                    if kind not in kinds:
                        continue
                    lhs, tok = (merged, t * P) if kind == "out" else (hT, t * P + T * (kind in ("mk", "mv")))
                    if f != items[n - 1][1] or n == 0:
                        pe.wait_ge(ring_in[f % 2], 16 * (f // 2 + 1))
                    if n >= 2:
                        pe.wait_ge(*item_out(n - 2))
                    for k in range(KD):
                        last = mm(ps[4 + n % 2][:, :], lhs[:, k, tok:tok + P], ring[f % 2][:, k, :],
                                  start=k == 0, stop=k == KD - 1)
                    last.then_inc(n_full, 1)
                    if lag is not None:
                        item_transposes(lag)
                    lag = n if n in normed else None
                if lag is not None:
                    item_transposes(lag)

            narrow_job(U_QI)

            pe.wait_ge(kiT_ok, 1)
            pe.wait_ge(glr_ok, 1)
            for s in (2, 3):
                pe.wait_ge(t_free[s], U_QI + 2)
            n = 0
            for t in range(1, NT):
                lo, hi = (TP, T) if t == NTP else (0, (t + 1) * P)
                for h in range(HI):
                    r = DI * (h % 2)
                    if n >= 3:
                        pe.wait_ge(rel_ok[n % 3], n // 3)
                    mm(ps[4 + n % 3][:, 0:hi - lo], qiT[r:r + DI, h // 2, t * P:(t + 1) * P], kiT[r:r + DI, lo:hi],
                       start=True, stop=True).then_inc(sc_full[n % 3], 1)
                    n += 1

            pe.wait_ge(ci_in, 16 * 2 * B)
            for g in range(4):
                if g >= 2:
                    pe.wait_ge(ciT_ok, g - 1)
                for j in range(4):
                    b, s = (4 * g + j) // PB, (4 * g + j) % PB
                    last = tr(ps[g % 2][:, j * P:(j + 1) * P], ci[:, b, s, :], ident)
                last.then_inc(ciT_full, 1)
            pe.wait_ge(wd_ok, 1)
            for g in range(4):
                if g >= 2:
                    pe.wait_ge(ciT_ok, 4 + g - 1)
                mm(ps[2 + g % 2][:, :], ones, wdiag[:, 4 * g:4 * g + 4, :], start=True, stop=True).then_inc(ciT_full, 1)
            pe.wait_ge(ciT_ok, 8)
            for b in range(B):
                if b >= 2:
                    pe.wait_ge(scs_ok, b - 1)
                for s in range(PB):
                    for par in range(2):
                        r = DI * par
                        c0 = s * HI * TB // 2
                        last = mm(ps[2 * (b % 2) + par][:, c0:c0 + HI * TB // 2], ciT[r:r + DI, b, s * P:(s + 1) * P],
                                  qiT[r:r + DI, :, TP + b * TB:TP + (b + 1) * TB], start=True, stop=True)
                last.then_inc(scs_full, 1)
            pe.wait_ge(scs_ok, B)
            for s in range(PB):
                last = tr(ps[2][:, s * P:(s + 1) * P], sT[:, s, :], ident)
            last.then_inc(scs_full, 1)
            pe.wait_ge(scs_ok, B + 1)

            narrow_job(U_QK)
            narrow_job(U_GO)
            for r in range(3):
                pe.wait_ge(rel_ok[r], (N_REL + 2 - r) // 3)
            pe.wait_ge(gain_in, 16 * N_GAINS)
            for t in range(NT):
                if t >= 2:
                    pe.wait_ge(z_ok, t - 1)
                mm(ps[6 + t % 2][:, :], glrT[0:RANK + 1, t * P:(t + 1) * P], wga[0:RANK + 1, :], start=True, stop=True)\
                    .then_inc(z_full, 1)
            project(("vg",))

            pe.wait_ge(la_ok, 1)
            pe.wait_ge(n_free_act, len(index["vg"]))
            for s in range(4):
                pe.wait_ge(t_free[s], U_GO + 2)
            pe.wait_ge(z_ok, NT)
            for t in range(NT):
                tok = slice(t * P, (t + 1) * P)
                cum, suf = (cum_p, suf_p) if t < NTP else (cum_s, suf_s)
                if t:
                    pe.wait_ge(og_ok, t)
                for h in range(HG):
                    last = mm(ps[0][:, h * P:(h + 1) * P], la[:, t, h * P:(h + 1) * P], cum, start=True, stop=True)
                last.then_inc(bT_full, 1)
                mm(ps[1][:, :], suf, la[:, t, :], start=True, stop=True).then_inc(suf_full, 1)
                if t:
                    pe.wait_ge(state_ok, 2 * t + 1)
                for h in range(HG):
                    last = tr(ps[2][:, h * P:(h + 1) * P], qkT[:, HG + h, tok], ident)
                last.then_inc(kt_full, 1)
                pe.wait_ge(qe_ok, t + 1)
                for h in range(HG):
                    last = mm(ps[3][:, h * P:(h + 1) * P], ke[:, h, :], qe[:, h, :], start=True, stop=True)
                last.then_inc(att_full, 1)
                pe.wait_ge(attm_ok, t + 1)
                pe.wait_ge(kd_ok, t + 1)
                attm = attm_p if t < NTP else attm_s
                for h in range(HG):
                    mm(ps[4 + h][:, 0:DV], attm[:, h, :], vg[:, t, h * DV:(h + 1) * DV], start=True, stop=False)
                if t < NTP:
                    for c in range(2):
                        r = slice(c * CHUNK, (c + 1) * CHUNK)
                        pe.wait_ge(state_ok, 2 * t + c + 1)
                        for h in range(HG):
                            last = mm(ps[4 + h][r, 0:DV], qe[:, h, r], state[:, h, :], start=False, stop=True)
                        if c:
                            last.then_inc(o_full, 1)
                        for h in range(HG):
                            last = mm(ps[2 + h // 2][:, (h % 2) * DV:(h % 2 + 1) * DV], kd[r, h, :],
                                      vg[r, t, h * DV:(h + 1) * DV], start=True, stop=True)
                        last.then_inc(kv_full, 1)
                else:
                    pe.wait_ge(qem_ok, 1)
                    for b in range(B):
                        pe.wait_ge(st_in[b % 3], 16 * (b // 3 + 1))
                        for h in range(HG):
                            c0 = b * HG * P + h * P
                            last = mm(ps[4 + h][:, 0:DV], qem[:, c0:c0 + P], state_s[b % 3][:, h, :],
                                      start=False, stop=b == B - 1)
                        if b == B - 1:
                            last.then_inc(o_full, 1)
                        pe.wait_ge(kdm_ok, b + 1)
                        if b:
                            pe.wait_ge(states_ok, b)
                        for h in range(HG):
                            last = mm(ps[2 + h // 2][:, (h % 2) * DV:(h % 2 + 1) * DV], kdm[b % 2][:, h, :],
                                      vg[:, t, h * DV:(h + 1) * DV], start=True, stop=True)
                        last.then_inc(kvs_full, 1)
                pe.wait_ge(on_ok, t + 1)
                for k in range(KD):
                    last = tr(ps[k // 4][:, (k % 4) * P:(k % 4 + 1) * P], on[:, k * P:(k + 1) * P], ident)
                last.then_inc(oT_full, 1)
            pe.wait_ge(og_ok, NT)
            pe.wait_ge(states_ok, B)
            merge_job(U_MERGE[0], 0)

            for q in range(2):
                pe.wait_ge(m_prod[q], 4)
            project(("mk", "mv", "qm"))
            pe.wait_ge(qT_ok, normed_before("qm"))
            pe.wait_ge(n_free_act, len(by_act))

            n = 0
            for b in range(B):
                pe.wait_ge(kvb_in[b % 2], 16 * (b // 2 + 1))
                for g in range(4):
                    if n >= 2:
                        pe.wait_ge(kmT_ok, n - 1)
                    for j in range(4):
                        k, m = 2 * g + j // 2, j % 2
                        last = tr(ps[n % 2][:, j * P:(j + 1) * P], kvb[b % 2][:, m, k * P:(k + 1) * P], ident)
                    last.then_inc(kmT_full, 1)
                    n += 1
                pe.wait_ge(kmT_ok, n)
                for m in range(NM):
                    for h in range(HM):
                        for d in range(2):
                            last = mm(ps[2 + m][:, h * TS + b * TB:h * TS + (b + 1) * TB],
                                      kmT[b % 2][:, 2 * h + d, m * P:(m + 1) * P],
                                      qmT[:, 2 * h + d, TP + b * TB:TP + (b + 1) * TB], start=d == 0, stop=d == 1)
                last.then_inc(lmT_full, 1)
            pe.wait_ge(lmT_ok, 1)

            def mem_transposes(j, t):
                pe.wait_ge(pmn_ok, j + 1)
                if j:
                    pe.wait_ge(pmT_ok, j)
                for m in range(NM):
                    for h in range(HM):
                        last = tr(ps[6 + m][:, h * P:(h + 1) * P], pm[j % 2][:, h * M + m * P:h * M + (m + 1) * P], ident)
                last.then_inc(pmT_full, 1)

            for j, t in enumerate(s_tiles):
                b = 2 * (j % 2)
                if j >= 2:
                    pe.wait_ge(pm_ok, j - 1)
                for h in range(HM):
                    dst = ps[b + h // 2][:, (h % 2) * M:(h % 2 + 1) * M]
                    if t == NTP:
                        for m in range(NM):
                            last = tr(dst[:, m * P:(m + 1) * P], lmT[:, m, h, :], ident)
                    else:
                        for d in range(2):
                            last = mm(dst, qmT[:, 2 * h + d, t * P:(t + 1) * P], mkT[:, 2 * h + d, :], start=d == 0, stop=d == 1)
                last.then_inc(lm_full, 1)
                if j:
                    mem_transposes(j - 1, s_tiles[j - 1])
            mem_transposes(NT - 1, s_tiles[-1])
            pe.wait_ge(pmT_ok, NT)
            for n in range(KD):
                h, d = n // 2, n % 2
                if n >= 4:
                    pe.wait_ge(om_ok, n - 3)
                for m in range(NM):
                    last = mm(ps[n % 4][:, :], mv[:, m, n * P:(n + 1) * P], pmT[:, m, h, 0:TP], start=m == 0, stop=m == NM - 1)
                last.then_inc(om_full, 1)
            for b in range(B):
                pe.wait_ge(kvb_in[b % 2], 16 * ((B + b) // 2 + 1))
                for k in range(KD):
                    for m in range(NM):
                        last = mm(ps[4 + k // 4][:, (k % 4) * TS + b * TB:(k % 4) * TS + (b + 1) * TB],
                                  kvb[b % 2][:, m, k * P:(k + 1) * P],
                                  pmT[:, m, k // 2, TP + b * TB:TP + (b + 1) * TB], start=m == 0, stop=m == NM - 1)
                last.then_inc(mk_used, 1)
            pe.wait_ge(om_ok, KD + 2)
            merge_job(U_MERGE[1], 1)

            for q in range(2):
                pe.wait_ge(m_prod[q], 8)
            project(("kv", "qa"))
            pe.wait_ge(qT_ok, normed_before("qa"))

            pe.wait_ge(kc_in, 16 * B)
            for b in range(B):
                if b >= 2:
                    pe.wait_ge(kcT_ok, b - 1)
                for k in range(KV):
                    for s in range(PB):
                        last = tr(ps[b % 2][:, (k * PB + s) * P:(k * PB + s + 1) * P], kc[:, b, s, k * P:(k + 1) * P], ident)
                last.then_inc(kcT_full, 1)
            pe.wait_ge(kcT_ok, B)
            for k in range(KV):
                for s in range(PB):
                    n = k * PB + s
                    dst = ps[2 + n][:, :].rearrange("p (h t) -> p h t", h=GQ)
                    for b in range(B):
                        last = mm(dst[:, :, b * TB:(b + 1) * TB], kcT[:, b, k, s * P:(s + 1) * P],
                                  qaT[:, k * GQ:(k + 1) * GQ, TP + b * TB:TP + (b + 1) * TB], start=True, stop=True)
                    last.then_inc(lsT_full, 1)
            pe.wait_ge(lsT_ok, KV * PB)
            pe.wait_ge(vc_in, 16 * B)

            def attend_transposes(n):
                j, h = n // HA, n % HA
                t = s_tiles[j]
                nb = work_w[t] // P
                pe.wait_ge(prn_ok, n + 1)
                if n >= 2:
                    pe.wait_ge(prT_ok, n - 1)
                for s in range(nb):
                    last = tr(ps[2 + n % 2][:, s * P:(s + 1) * P], pr[n % 2][:, s * P:(s + 1) * P], ident)
                last.then_inc(prT_full, 1)
                if h % GQ < GQ - 1:
                    return
                k, w = h // GQ, n // GQ
                pe.wait_ge(prT_ok, n + 1)
                if w >= 2:
                    pe.wait_ge(oa_ok, w - 1)
                dst = ps[4 + w % 2]
                pT = paT[w % 2]
                if t < NTP:
                    for s in range(nb):
                        last = mm(dst[:, :], va[:, s, k * P:(k + 1) * P], pT[:, s, :, :], start=s == 0, stop=s == nb - 1)
                else:
                    mm(dst[:, :], va[:, NTP, k * P:(k + 1) * P], pT[:, PB, :, :], start=True, stop=False)
                    out = dst[:, :].rearrange("p (h t) -> p h t", h=GQ)
                    for b in range(B):
                        for s in range(PB):
                            last = mm(out[:, :, b * TB:(b + 1) * TB], kc[:, b, s, k * P:(k + 1) * P],
                                      pT[:, s, :, b * TB:(b + 1) * TB], start=False, stop=(b, s) == (B - 1, PB - 1))
                last.then_inc(oa_full, 1)

            n = 0
            for j, t in enumerate(s_tiles):
                for h in range(HA):
                    k = h // GQ
                    dst = ps[n % 2]
                    if n >= 2:
                        pe.wait_ge(lg_ok, n - 1)
                    if t < NTP:
                        last = mm(dst[:, 0:work_w[t]], qaT[:, h, t * P:(t + 1) * P], kT[:, k, 0:work_w[t]], start=True, stop=True)
                    else:
                        for s in range(PB):
                            tr(dst[:, s * P:(s + 1) * P], lsT[:, k, s, h % GQ, :], ident)
                        last = mm(dst[:, PAST:KS], qaT[:, h, TP:T], kT[:, k, TP:T], start=True, stop=True)
                    last.then_inc(lg_full, 1)
                    if n:
                        attend_transposes(n - 1)
                    n += 1
            attend_transposes(n - 1)
            pe.wait_ge(oa_ok, NT * KV)
            merge_job(U_MERGE[2], 2)

            for q in range(2):
                pe.wait_ge(m_prod[q], 12)
            pe.wait_ge(merged_ok, 16)
            project(("out",))
            n = 0
            for t in range(NT):
                pe.wait_ge(h2_ok, t + 1)
                for h in range(2):
                    if n >= 2:
                        pe.wait_ge(h2T_ok, n - 1)
                    for k in range(4):
                        last = tr(ps[n % 2][:, k * P:(k + 1) * P], h2[:, t, (4 * h + k) * P:(4 * h + k + 1) * P], ident)
                    last.then_inc(h2T_full, 1)
                    n += 1
            pe.wait_ge(h2T_ok, 2 * NT)
            pe.wait_ge(rtw_in, 5 * 16)
            for t in range(NT):
                for k in range(KD):
                    last = mm(ps[2][:, t * NR:(t + 1) * NR], h2T[:, k, t * P:(t + 1) * P], w_rt[:, k, :],
                              start=k == 0, stop=k == KD - 1)
            last.then_inc(rt_full, 1)
            pe.wait_ge(rt_step, 2)
            for t in range(NT):
                for s in range(t + 1):
                    mm(ps[3][:, t * NE:(t + 1) * NE], before if s == t else ones, hot_both[:, s, :], start=s == 0, stop=s == t)
            for s in range(NT):
                last = mm(ps[3][:, NT * NE:(NT + 1) * NE], ones, hot_both[:, s, :], start=s == 0, stop=s == NT - 1)
            last.then_inc(rank_full, 1)
            pe.wait_ge(pos_ok, 1)

            def expert(n, s, wait_w, sems, at):
                f_hsT, f_hsTok, f_gu, f_hid, f_dn, f_oT, f_y = sems
                pe.wait_ge(*wait_w)
                pe.sem_inc(pe_seen, 1)
                for k in range(KD):
                    last = tr(ps[0][:, k * CAP:(k + 1) * CAP], hs[s][0:CAP, k * P:(k + 1) * P], ident[0:CAP, 0:CAP])
                last.then_inc(f_hsT, 1)
                pe.wait_ge(f_hsTok, at(0))
                for g, w in enumerate((ew_gate[s], ew_up[s])):
                    for f in range(DF // P):
                        c0 = (g * (DF // P) + f) * CAP
                        for k in range(KD):
                            last = mm(ps[1][:, c0:c0 + CAP], w[:, k, f * P:(f + 1) * P], hsT[n % 2][:, k, :],
                                      start=k == 0, stop=k == KD - 1)
                last.then_inc(f_gu, 1)
                pe.wait_ge(f_hid, at(0))
                for k in range(KD):
                    for f in range(DF // P):
                        last = mm(ps[2][:, k * CAP:(k + 1) * CAP], ew_down[s][:, f, k * P:(k + 1) * P],
                                  hid[n % 2][:, f * CAP:(f + 1) * CAP], start=f == 0, stop=f == DF // P - 1)
                last.then_inc(f_dn, 1)
                pe.wait_ge(f_oT, at(0))
                pe.sem_inc(pe_seen, 1)
                for k in range(KD):
                    last = tr(ps[4 + k // 4][0:CAP, (k % 4) * P:(k % 4 + 1) * P], oT[n % 2][:, k, :], ident)
                last.then_inc(f_y, 1)

            main = (hsT_full, hsT_ok, gu_full, hid_ok, dn_full, oTs_ok, y_full)
            with pe.Fori(0, NE // NES) as i:
                for s in range(NES):
                    if s:
                        pe.wait_ge(ysl_ok, i * NES + s)
                    else:
                        pe.wait_ge(ysl_ok, i * NES)
                    expert(s, s, (ew_in[s], i * 64 + 64), main, lambda x, s=s: i * NES + (s + 1 - x))
            over = pe.value_load(rti[0:1, N_OVER:N_OVER + 1], min_val=0, max_val=N_OVER)
            pe.wait_ge(ysl_ok, NE)
            with pe.If(over > 0):
                with pe.Fori(0, N_OVER) as i:
                    pe.wait_ge(ysl_ok, i + NE)
                    expert(0, 0, (ew_in[0], i * 64 + (64 * NE // NES + 64)), main, lambda x: i + (NE + 1 - x))

        @block.scalar
        def _(act):
            go = nc.scalar.activation
            junk = cut(region_m, 0, D)

            for t in range(NT + NM):
                act.wait_ge(x_in[min(t, 2)], 16 if t < 2 else 16 * (NT + NM - 2))
                if t:
                    act.wait_ge(ss_ok, t)
                go(junk, xt[:, t, :], ACT.Square, accum_out=ss0[:, t:t + 1]).then_inc(ss_ok, 1)
            for n in range(2 * (NT + NM)):
                act.wait_ge(xT_full, n + 1)
                t, h = n // 2, n % 2
                go(hT[:, 4 * h:4 * h + 4, t * P:(t + 1) * P], ps[n % 2][:, :].rearrange("p (k t) -> p k t", k=4),
                   ACT.Copy).then_inc(hT_ok, 1)
            for t in range(NT):
                act.wait_ge(kiw_full, t + 1)
                if t:
                    act.wait_ge(kiss_ok, t)
                go(junk[:, 0:DI], ps[2 + t % 2][:, 0:DI], ACT.Square, accum_out=ssk[:, t:t + 1]).then_inc(kiss_ok, 1)
            act.wait_ge(glr_full, 1)
            act.wait_ge(zero_ok, 1)
            go(glrT[0:RANK, 0:TP], ps[4][0:RANK, 0:TP], ACT.Copy)
            go(glrT[0:RANK, TP:T], ps[5][0:RANK, 0:TS], ACT.Copy).then_inc(glr_ok, 1)
            act.wait_ge(kidT_full, 1)
            go(kiT[:, 0:TP], ps[6][:, :], ACT.Copy)
            go(kiT[:, TP:T], ps[7][:, 0:TS], ACT.Copy).then_inc(kiT_ok, 1)

            def narrow_out(dst, func, u):
                with act.Fori(0, 2) as i:
                    for s in range(4):
                        b = 2 * (s % 2)
                        act.wait_ge(t_full[s], i + (u + 1))
                        go(dst[:, bass.ds(i * 4 + s, 1), 0:TP], ps[b][:, 0:TP].unsqueeze(1), func)
                        go(dst[:, bass.ds(i * 4 + s, 1), TP:T], ps[b + 1][:, 0:TS].unsqueeze(1), func).then_inc(t_free[s], 1)

            def gates(u, m):
                with act.Fori(0, 4) as i:
                    for q in range(2):
                        act.wait_ge(m_prod[q], i + 4 * m)
                        act.wait_ge(t_full[2 * q], i + (u + 1))
                        go(sg[q][:, 0:TP], ps[4 * q + 1][:, 0:TP], ACT.Sigmoid)
                        go(sg[q][:, TP:T], ps[4 * q + 3][:, 0:TS], ACT.Sigmoid).then_inc(sg_ok[q], 1)

            def item_transposed(n):
                kind, _, t, c = items[n]
                j = normed.index(n)
                act.wait_ge(qT_full, j + 1)
                src = ps[6 + j % 2][:, :].rearrange("p (k t) -> p k t", t=P)
                tok = slice(t * P, (t + 1) * P)
                if kind == "mk":
                    last = go(mkT[:, 4 * c:4 * c + 4, tok], src, ACT.Copy)
                elif kind == "kv":
                    last = go(kT[:, :, tok], src[:, 0:KV, :], ACT.Copy)
                elif kind == "qa":
                    last = go(qaT[:, 4 * c:4 * c + 4, tok], src, ACT.Copy, scale=gcol_q)
                else:
                    for d in range(2):
                        last = go(qmT[:, 4 * c + d:4 * c + 4:2, tok], src[:, d::2, :], ACT.Copy, scale=gcol_qm[:, d:d + 1])
                last.then_inc(qT_ok, 1)

            def project_out(kinds):
                lag = None
                for n, (kind, f, t, c) in enumerate(items):
                    if kind not in kinds:
                        continue
                    act.wait_ge(n_full, n + 1)
                    src = ps[4 + n % 2]
                    if n in by_act:
                        dst = (vg if kind == "vg" else mv)[:, t, c * BANK:(c + 1) * BANK]
                        go(dst, src[:, :], ACT.Copy).then_inc(n_free_act, 1)
                    else:
                        j = normed.index(n)
                        if j >= 2:
                            act.wait_ge(qn_ok, j - 1)
                        if kind == "kv":
                            go(va[:, t, :], src[:, KV * HD:], ACT.Copy)
                        w = KV * HD if kind == "kv" else BANK
                        go(sq[j % 2][:, 0:w], src[:, 0:w], ACT.Square).then_inc(sq_ok, 1)
                    if lag is not None:
                        item_transposed(lag)
                    lag = n if n in normed else None
                if lag is not None:
                    item_transposed(lag)

            narrow_out(qiT, ACT.Copy, U_QI)
            n = 0
            for t in range(1, NT):
                w = TS if t == NTP else (t + 1) * P
                for h in range(HI):
                    act.wait_ge(sc_full[n % 3], n // 3 + 1)
                    if n >= 3:
                        act.wait_ge(acc_ok, n - 2)
                    go(rel[n % 3][:, 0:w], ps[4 + n % 3][:, 0:w], ACT.Relu).then_inc(rel_ok[n % 3], 1)
                    n += 1
            for g in range(4):
                act.wait_ge(ciT_full, g + 1)
                go(ciT[:, 2 * g:2 * g + 2, :], ps[g % 2][:, :].rearrange("p (b s) -> p b s", b=2), ACT.Copy).then_inc(ciT_ok, 1)
            for g in range(4):
                act.wait_ge(ciT_full, 4 + g + 1)
                go(wB[:, 4 * g:4 * g + 4, :], ps[2 + g % 2][:, :].rearrange("p (h t) -> p h t", h=4), ACT.Copy).then_inc(ciT_ok, 1)

            narrow_out(qkT, ACT.Copy, U_QK)
            narrow_out(goT, ACT.Silu, U_GO)
            act.wait_ge(z_ok, NT)
            go(zabs, zabs, ACT.Exp, scale=-1.0).then_inc(act_step, 1)
            act.wait_ge(act_step, 1)
            go(zabs, zabs, ACT.Ln, bias=1.0).then_inc(act_step, 1)
            project_out(("vg",))

            act.wait_ge(fill_ok, 16)
            for t in range(NT):
                act.wait_ge(bT_full, t + 1)
                if t:
                    act.wait_ge(attm_ok, t)
                go(eb, ps[0][:, :].rearrange("p (h t) -> p h t", h=HG), ACT.Exp)
                go(enb, ps[0][:, :].rearrange("p (h t) -> p h t", h=HG), ACT.Exp, scale=-1.0).then_inc(eb_ok, 1)
                act.wait_ge(suf_full, t + 1)
                go(kdf, ps[1][:, :].rearrange("p (h t) -> p h t", h=HG), ACT.Exp).then_inc(kdf_ok, 1)
                if t == NTP:
                    act.wait_ge(kd_ok, NT)
                    for b in range(B):
                        if b >= 2:
                            act.wait_ge(kvs_full, b - 1)
                        go(kdm[b % 2], kd, ACT.Copy, scale=bsel[:, b:b + 1]).then_inc(kdm_ok, 1)
                act.wait_ge(o_full, t + 1)
                if t:
                    act.wait_ge(on_ok, t)
                for h in range(HG):
                    last = go(mix[:, h * DV:(h + 1) * DV], ps[4 + h][:, 0:DV], ACT.Square, accum_out=sso[:, h:h + 1])
                last.then_inc(oss_ok, 1)
            gates(U_MERGE[0], 0)

            for q in range(2):
                act.wait_ge(m_prod[q], 4)
            project_out(("mk", "mv", "qm"))
            n = 0
            for b in range(B):
                if b >= 2:
                    act.wait_ge(lmT_full, b - 1)
                for g in range(4):
                    act.wait_ge(kmT_full, n + 1)
                    go(kmT[b % 2][:, 2 * g:2 * g + 2, :], ps[n % 2][:, :].rearrange("p (k m) -> p k m", k=2), ACT.Copy)\
                        .then_inc(kmT_ok, 1)
                    n += 1
            act.wait_ge(lmT_full, B)
            for m in range(NM):
                last = go(lmT[:, m, :, :], ps[2 + m][:, :].rearrange("p (h t) -> p h t", h=HM), ACT.Copy)
            last.then_inc(lmT_ok, 1)
            act.wait_ge(mem_out, 48)

            def mem_transposed(j, t):
                act.wait_ge(pmT_full, j + 1)
                for m in range(NM):
                    last = go(pmT[:, m, :, t * P:(t + 1) * P], ps[6 + m][:, :].rearrange("p (h t) -> p h t", h=HM), ACT.Copy)
                last.then_inc(pmT_ok, 1)

            for j, t in enumerate(s_tiles):
                b = 2 * (j % 2)
                act.wait_ge(mmx_ok, j + 1)
                if j >= 2:
                    act.wait_ge(pmT_full, j - 1)
                for h in range(HM):
                    last = go(pm[j % 2][:, h * M:(h + 1) * M], ps[b + h // 2][:, (h % 2) * M:(h % 2 + 1) * M], ACT.Exp,
                              bias=nmx[:, h:h + 1], scale=HDM ** -0.5, accum_out=sm[:, 4 * (j % 2) + h:4 * (j % 2) + h + 1])
                last.then_inc(pm_ok, 1)
                if j:
                    mem_transposed(j - 1, s_tiles[j - 1])
            mem_transposed(NT - 1, s_tiles[-1])
            for n in range(KD):
                act.wait_ge(om_full, n + 1)
                go(qmT[:, n, 0:TP], ps[n % 4][:, :], ACT.Copy).then_inc(om_ok, 1)
            act.wait_ge(mk_used, B)
            for g in range(2):
                go(qmT[:, 4 * g:4 * g + 4, TP:T], ps[4 + g][:, :].rearrange("p (k t) -> p k t", k=4), ACT.Copy).then_inc(om_ok, 1)
            gates(U_MERGE[1], 1)

            for q in range(2):
                act.wait_ge(m_prod[q], 8)
            project_out(("kv", "qa"))
            for b in range(B):
                act.wait_ge(kcT_full, b + 1)
                go(kcT[:, b, :, :], ps[b % 2][:, :].rearrange("p (k s) -> p k s", k=KV), ACT.Copy).then_inc(kcT_ok, 1)
            for n in range(KV * PB):
                act.wait_ge(lsT_full, n + 1)
                go(lsT[:, n // PB, n % PB, :, :], ps[2 + n][:, :].rearrange("p (h t) -> p h t", h=GQ), ACT.Copy)\
                    .then_inc(lsT_ok, 1)

            def attend_transposed(n):
                nb, w = work_w[s_tiles[n // HA]] // P, n // GQ
                act.wait_ge(prT_full, n + 1)
                if w >= 2:
                    act.wait_ge(oa_full, w - 1)
                go(paT[w % 2][:, 0:nb, n % GQ, :], ps[2 + n % 2][:, 0:nb * P].rearrange("p (s t) -> p s t", t=P), ACT.Copy)\
                    .then_inc(prT_ok, 1)

            for n in range(NT * HA):
                w = work_w[s_tiles[n // HA]]
                act.wait_ge(lg_ok, n + 1)
                if n >= 2:
                    act.wait_ge(prT_full, n - 1)
                go(pr[n % 2][:, 0:w], lg[n % 2][:, 0:w], ACT.Exp, bias=nmx[:, n % 4:n % 4 + 1], scale=HD ** -0.5,
                   accum_out=sm[:, n % 4:n % 4 + 1]).then_inc(pr_ok, 1)
                if n:
                    attend_transposed(n - 1)
            attend_transposed(NT * HA - 1)
            gates(U_MERGE[2], 2)

            act.wait_ge(x1_ok, 2 * NT)
            for t in range(NT):
                go(h2[:, t, :], x1[:, t, :], ACT.Square, accum_out=ssf[:, t:t + 1]).then_inc(ssf_ok, 1)
            n = 0
            for t in range(NT):
                for h in range(2):
                    act.wait_ge(h2T_full, n + 1)
                    go(h2T[:, 4 * h:4 * h + 4, t * P:(t + 1) * P], ps[n % 2][:, :].rearrange("p (k t) -> p k t", k=4),
                       ACT.Copy).then_inc(h2T_ok, 1)
                    n += 1
            act.wait_ge(rt_step, 1)
            go(ge5, gs5, ACT.Exp).then_inc(act_step, 1)
            act.wait_ge(rt_step, 3)
            go(rs5[7], rs5[6], ACT.Exp).then_inc(act_step, 1)

            def expert(q, at, sems):
                f_hsT, f_hsTok, f_gu, f_silu, f_dn, f_oT = sems
                act.wait_ge(f_hsT, at)
                go(hsT[q], ps[0][:, :].rearrange("p (k t) -> p k t", k=KD), ACT.Copy).then_inc(f_hsTok, 1)
                act.wait_ge(f_gu, at)
                go(act_g[q], ps[1][:, 0:DF // P * CAP], ACT.Silu).then_inc(f_silu, 1)
                act.wait_ge(f_dn, at)
                go(oT[q], ps[2][:, :].rearrange("p (k t) -> p k t", k=KD), ACT.Copy).then_inc(f_oT, 1)

            with act.Fori(0, NE // NES) as i:
                for s in range(NES):
                    expert(s % 2, i * NES + (s + 1), (hsT_full, hsT_ok, gu_full, silu_ok, dn_full, oTs_ok))
            over = act.value_load(rti[0:1, N_OVER:N_OVER + 1], min_val=0, max_val=N_OVER)
            with act.If(over > 0):
                with act.Fori(0, N_OVER) as i:
                    expert(0, i + (NE + 1), (hsT_full, hsT_ok, gu_full, silu_ok, dn_full, oTs_ok))

        @block.vector
        def _(dve):
            v = nc.vector
            steps = [0]

            def link(ins):
                steps[0] += 1
                ins.then_inc(dve_step, 1)
                dve.wait_ge(dve_step, steps[0])

            def rstd(out, total, width):
                x, y, w = total, out, newton[:, 0:out.shape[1]]
                link(v.tensor_scalar(x, x, 1.0 / width, EPS, ALU.mult, ALU.add))
                link(v.tensor_scalar(y.bitcast(I32), x.bitcast(I32), 1, None, ALU.logical_shift_right))
                link(v.tensor_scalar(y.bitcast(I32), y.bitcast(I32), -1.0, float(0x5f3759df), ALU.mult, ALU.add))
                for _ in range(3):
                    link(v.scalar_tensor_tensor(w, y, -0.5, y, ALU.mult, ALU.mult))
                    link(v.tensor_tensor(w, w, x, ALU.mult))
                    link(v.scalar_tensor_tensor(y, w, 1.5, y, ALU.add, ALU.mult))

            dve.wait_ge(gain_in, 16 * N_GAINS)
            for t in range(NT + NM):
                if t in (0, 2):
                    t1 = 2 if t == 0 else NT + NM
                    dve.wait_ge(ss_ok, t1)
                    rstd(rs0[:, t:t1], ss0[:, t:t1], D)
                v.scalar_tensor_tensor(xt[:, t, :], xt[:, t, :], rs0[:, t:t + 1], g_x if t < NT else g_mem,
                                       ALU.mult, ALU.mult).then_inc(xn_ok, 1)
            dve.wait_ge(xn_ok, NT + NM)
            v.memset(glrT[0:32, :], 1.0).then_inc(zero_ok, 1)

            for t in range(NT):
                dve.wait_ge(kiss_ok, t + 1)
                rstd(rsk[:, t:t + 1], ssk[:, t:t + 1], DI)
                src = ps[2 + t % 2]
                for r in range(2):
                    v.scalar_tensor_tensor(kid[:, t, r * DI:(r + 1) * DI], src[:, 0:DI], rsk[:, t:t + 1], g_ki[:, 0:DI],
                                           ALU.mult, ALU.mult)
                v.tensor_scalar(wi[:, t, :], src[:, DI:DI + HI], HI ** -0.5 * DI ** -0.5, None, ALU.mult).then_inc(kid_ok, 1)
            dve.wait_ge(kid_ok, NT)
            dve.wait_ge(hT_ok, 2 * (NT + NM))
            dve.wait_ge(const_ok, N_CONST)
            for par in range(2):
                n8 = HI // 2
                last = v.tensor_tensor(wdiag[:, par * n8:(par + 1) * n8, :], ident.unsqueeze(1).to_broadcast([P, n8, P]),
                                       wi[:, NTP, par::2].unsqueeze(2).to_broadcast([P, n8, P]), ALU.mult)
            last.then_inc(wd_ok, 1)

            n = 0
            for t in range(1, NT):
                dst = work[t][:, PAST:KS] if t == NTP else work[t]
                w = TS if t == NTP else (t + 1) * P
                for h in range(HI):
                    dve.wait_ge(rel_ok[n % 3], n // 3 + 1)
                    if h == 0:
                        v.tensor_scalar(dst, rel[n % 3][:, 0:w], wi[:, t, 0:1], None, ALU.mult).then_inc(acc_ok, 1)
                    else:
                        dve.wait_ge(acc_ok, n)
                        v.scalar_tensor_tensor(dst, rel[n % 3][:, 0:w], wi[:, t, h:h + 1], dst, ALU.mult, ALU.add)\
                            .then_inc(acc_ok, 1)
                    n += 1
            dve.wait_ge(ciT_ok, 8)
            for b in range(B):
                dve.wait_ge(scs_full, b + 1)
                if b:
                    dve.wait_ge(scs_ok, b)
                for s in range(PB):
                    for par in range(2):
                        h8 = slice(par * HI // 2, (par + 1) * HI // 2)
                        src = ps[2 * (b % 2) + par][:, s * HI * TB // 2:(s + 1) * HI * TB // 2]
                        last = v.scalar_tensor_tensor(sct[s].rearrange("p (h t) -> p h t", h=HI)[:, h8, :],
                                                      src.rearrange("p (h t) -> p h t", t=TB),
                                                      0.0, wB[:, h8, b * TB:(b + 1) * TB], ALU.max, ALU.mult)
                link(last)
                for s in range(PB):
                    last = v.tensor_reduce(sT[:, s, b * TB:(b + 1) * TB], sct[s].rearrange("p (h t) -> p t h", h=HI), AX_X, ALU.add)
                last.then_inc(scs_ok, 1)
            dve.wait_ge(scs_full, B + 1)
            v.tensor_copy(work[NTP][:, 0:PAST], ps[2][:, 0:PAST]).then_inc(scs_ok, 1)

            dve.wait_ge(acc_ok, n)
            link(v.memset(work[0], 0.0))
            for t in range(NTP):
                v.memset(work[t][0:CHUNK, t * P + CHUNK:(t + 1) * P], NEG)
            link(v.tensor_tensor(work[NTP][:, PAST:KS], work[NTP][:, PAST:KS], other, ALU.add))
            dve.wait_ge(scs_ok, B + 1)

            for t in range(1, NT):
                left = TOPK_S if t == NTP else TOPK_P
                while left > 0:
                    link(v.max(top8, work[t]))
                    if left < 8:
                        link(v.memset(top8[:, left:8], TAKEN))
                    link(v.match_replace(work[t], top8, work[t], TAKEN))
                    left -= 8
                link(v.tensor_scalar(work[t], work[t], TAKEN / 2, NEG, ALU.is_gt, ALU.mult))

            for t in range(NT):
                dve.wait_ge(z_full, t + 1)
                link(v.tensor_scalar(la[:, t, :], ps[6 + t % 2][:, :], 0.0, None, ALU.min))
                v.scalar_tensor_tensor(zabs[:, t, :], la[:, t, :], -2.0, ps[6 + t % 2][:, :], ALU.mult, ALU.add)\
                    .then_inc(z_ok, 1)
            dve.wait_ge(act_step, 2)
            v.tensor_tensor(la, la, zabs, ALU.subtract).then_inc(la_ok, 1)
            dve.wait_ge(la_ok, 1)
            v.memset(state, 0.0).then_inc(state_ok, 1)

            dve.wait_ge(pool_step, 3)
            dve.wait_ge(early_out, 32)
            for t in range(NT):
                tok = slice(t * P, (t + 1) * P)
                cum, attm = (cum_p, attm_p) if t < NTP else (cum_s, attm_s)
                dve.wait_ge(eb_ok, t + 1)
                if t < NTP:
                    v.tensor_copy(dec[:, :, 0:2], eb[:, :, CHUNK - 1::CHUNK])
                else:
                    v.tensor_copy(dec[:, :, 0:B], eb[:, :, TB - 1::TB])
                v.scalar_tensor_tensor(qe, qkT[:, 0:HG, tok], DK ** -0.5, eb, ALU.mult, ALU.mult)
                v.tensor_tensor(ke, qkT[:, HG:2 * HG, tok], enb, ALU.mult).then_inc(qe_ok, 1)
                if t == NTP:
                    dve.wait_ge(qe_ok, t + 1)
                    diag = qem.rearrange("p (b x) -> p b x", b=B)[:, :, 0:HG * P].rearrange("p b (h c) -> p h b c", h=HG)
                    v.tensor_copy(diag[:, :, :, 0:TB], qe.rearrange("p h (b c) -> p h b c", b=B)).then_inc(qem_ok, 1)
                dve.wait_ge(kdf_ok, t + 1)
                dve.wait_ge(kt_full, t + 1)
                v.tensor_tensor(kd, ps[2][:, :].rearrange("p (h t) -> p h t", h=HG), kdf, ALU.mult).then_inc(kd_ok, 1)
                dve.wait_ge(att_full, t + 1)
                v.copy_predicated(attm, cum.bitcast(U32).unsqueeze(1).to_broadcast([P, HG, P]),
                                  ps[3][:, :].rearrange("p (h t) -> p h t", h=HG)).then_inc(attm_ok, 1)
                if t < NTP:
                    dve.wait_ge(qe_ok, t + 1)
                    for c in range(2):
                        dve.wait_ge(kv_full, 2 * t + c + 1)
                        dve.wait_ge(state_ok, 2 * t + c + 1)
                        for h in range(HG):
                            last = v.scalar_tensor_tensor(state[:, h, :], state[:, h, :], dec[:, h, c:c + 1],
                                                          ps[2 + h // 2][:, (h % 2) * DV:(h % 2 + 1) * DV], ALU.mult, ALU.add)
                        last.then_inc(state_ok, 1)
                else:
                    for b in range(B):
                        dve.wait_ge(kvs_full, b + 1)
                        for h in range(HG):
                            last = v.scalar_tensor_tensor(state_s[b % 3][:, h, :], state_s[b % 3][:, h, :], dec[:, h, b:b + 1],
                                                          ps[2 + h // 2][:, (h % 2) * DV:(h % 2 + 1) * DV], ALU.mult, ALU.add)
                        last.then_inc(states_ok, 1)
                dve.wait_ge(oss_ok, t + 1)
                rstd(rso[:, 0:HG], sso[:, 0:HG], DV)
                for h in range(HG):
                    last = v.tensor_scalar(on[:, h * DV:(h + 1) * DV], ps[4 + h][:, 0:DV], rso[:, h:h + 1], None, ALU.mult)
                last.then_inc(on_ok, 1)
                dve.wait_ge(oT_full, t + 1)
                for g in range(2):
                    for d in range(2):
                        dst = goT[:, 4 * g + d:4 * g + 4:2, tok]
                        last = v.scalar_tensor_tensor(dst, ps[g][:, :].rearrange("p (k t) -> p k t", k=4)[:, d::2, :],
                                                      gcol_o[:, d:d + 1], dst, ALU.mult, ALU.mult)
                last.then_inc(og_ok, 1)

            def merge(u, m):
                with dve.Fori(0, 4) as i:
                    for q in range(2):
                        dve.wait_ge(sg_ok[q], i + (4 * m + 1))
                        dve.wait_ge(t_full[2 * q + 1], i + (u + 1))
                        sum_ = merged[:, bass.ds(i * 2 + q, 1), :]
                        dst = prod[q].unsqueeze(1) if m else sum_
                        v.tensor_tensor(dst[:, :, 0:TP], sg[q][:, 0:TP].unsqueeze(1), ps[4 * q][:, 0:TP].unsqueeze(1), ALU.mult)
                        v.tensor_tensor(dst[:, :, TP:T], sg[q][:, TP:T].unsqueeze(1), ps[4 * q + 2][:, 0:TS].unsqueeze(1), ALU.mult)\
                            .then_inc(m_prod[q], 1)
                        if m:
                            dve.wait_ge(m_prod[q], i + (4 * m + 1))
                            v.tensor_tensor(sum_, sum_, prod[q].unsqueeze(1), ALU.add).then_inc(merged_ok, 1)

            for n in range(3):
                dve.wait_ge(st_out[n], 16 * ((B + 2 - n) // 3))
            dve.wait_ge(early_out, 48)
            merge(U_MERGE[0], 0)

            def project_norm(kinds):
                for n in normed:
                    kind, f, t, c = items[n]
                    if kind not in kinds:
                        continue
                    j = normed.index(n)
                    hd = HDM if kind in ("mk", "qm") else HD
                    w = KV * HD if kind == "kv" else BANK
                    nh = w // hd
                    dve.wait_ge(sq_ok, j + 1)
                    link(v.tensor_reduce(ssn[:, 0:nh], sq[j % 2][:, 0:w].rearrange("p (h d) -> p h d", d=hd), AX_X, ALU.add))
                    rstd(rsn[:, 0:nh], ssn[:, 0:nh], hd)
                    if j >= 2:
                        dve.wait_ge(qT_full, j - 1)
                    q3 = qn[j % 2][:, 0:w].rearrange("p (h d) -> p h d", d=hd)
                    x = v.tensor_tensor(q3, ps[4 + n % 2][:, 0:w].rearrange("p (h d) -> p h d", d=hd),
                                        rsn[:, 0:nh].unsqueeze(2).to_broadcast([P, nh, hd]), ALU.mult)
                    if kind in ("qm", "qa"):
                        x.then_inc(qn_ok, 1)
                        continue
                    link(x)
                    dst, g = (mkn[:, t, c * BANK:(c + 1) * BANK], g_mk) if kind == "mk" else (kn[:, t, :], g_ka)
                    v.tensor_tensor(dst.rearrange("p (h d) -> p h d", d=hd), q3, g[:, 0:hd].unsqueeze(1).to_broadcast([P, nh, hd]),
                                    ALU.mult).then_inc(qn_ok, 1)

            project_norm(("mk", "qm"))

            def mem_max(j):
                dve.wait_ge(lm_full, j + 1)
                if j:
                    dve.wait_ge(pm_ok, j)
                for g in range(2):
                    last = v.tensor_reduce(mx[:, 2 * g:2 * g + 2], ps[2 * (j % 2) + g][:, :].rearrange("p (h m) -> p h m", h=2),
                                           AX_X, ALU.max)
                link(last)
                v.tensor_scalar(nmx[:, 0:HM], mx[:, 0:HM], -HDM ** -0.5, None, ALU.mult).then_inc(mmx_ok, 1)

            mem_max(0)
            for j in range(NT):
                if j + 1 < NT:
                    mem_max(j + 1)
                dve.wait_ge(pm_ok, j + 1)
                r = 4 * (j % 2)
                link(v.reciprocal(rsm[:, r:r + HM], sm[:, r:r + HM]))
                for h in range(HM):
                    last = v.tensor_scalar(pm[j % 2][:, h * M:(h + 1) * M], pm[j % 2][:, h * M:(h + 1) * M],
                                           rsm[:, r + h:r + h + 1], None, ALU.mult)
                last.then_inc(pmn_ok, 1)
            merge(U_MERGE[1], 1)

            project_norm(("kv", "qa"))

            def attend_max(n):
                t = s_tiles[n // HA]
                dve.wait_ge(lg_full, n + 1)
                if n >= 2:
                    dve.wait_ge(pr_ok, n - 1)
                link(v.tensor_tensor_reduce(lg[n % 2][:, 0:work_w[t]], ps[n % 2][:, 0:work_w[t]], work[t], 1.0, TAKEN,
                                            ALU.add, ALU.max, mx[:, n % 4:n % 4 + 1]))
                v.tensor_scalar(nmx[:, n % 4:n % 4 + 1], mx[:, n % 4:n % 4 + 1], -HD ** -0.5, None, ALU.mult).then_inc(lg_ok, 1)

            def attend_out(w):
                t, k = s_tiles[w // KV], w % KV
                dve.wait_ge(oa_full, w + 1)
                v.tensor_copy(qaT[:, k * GQ:(k + 1) * GQ, t * P:(t + 1) * P], ps[4 + w % 2][:, :].rearrange("p (h t) -> p h t", h=GQ))\
                    .then_inc(oa_ok, 1)

            attend_max(0)
            for n in range(NT * HA):
                w = work_w[s_tiles[n // HA]]
                if n + 1 < NT * HA:
                    attend_max(n + 1)
                dve.wait_ge(pr_ok, n + 1)
                link(v.reciprocal(rsm[:, n % 4:n % 4 + 1], sm[:, n % 4:n % 4 + 1]))
                v.tensor_scalar(pr[n % 2][:, 0:w], pr[n % 2][:, 0:w], rsm[:, n % 4:n % 4 + 1], None, ALU.mult).then_inc(prn_ok, 1)
                if n >= GQ and n % GQ == 1:
                    attend_out(n // GQ - 1)
            attend_out(NT * KV - 1)
            merge(U_MERGE[2], 2)

            dve.wait_ge(kv_out, 64)
            dve.wait_ge(xr_in, 32)
            for n in index["out"]:
                _, f, t, c = items[n]
                dve.wait_ge(n_full, n + 1)
                v.tensor_tensor(x1[:, t, c * BANK:(c + 1) * BANK], ps[4 + n % 2][:, :], xr[:, t, c * BANK:(c + 1) * BANK], ALU.add)\
                    .then_inc(x1_ok, 1)
            dve.wait_ge(rtw_in, 80)
            dve.wait_ge(ssf_ok, NT)
            rstd(rsf[:, 0:NT], ssf[:, 0:NT], D)
            for t in range(NT):
                v.scalar_tensor_tensor(h2[:, t, :], x1[:, t, :], rsf[:, t:t + 1], g_ffn, ALU.mult, ALU.mult).then_inc(h2_ok, 1)

            def per(x, w):
                return x.unsqueeze(2).to_broadcast([P, NT, w])

            def first_index(out, x, top, w):
                c = r_tmp[:, :, 0:w]
                link(v.tensor_tensor(c, x, per(top, w), ALU.not_equal))
                link(v.scalar_tensor_tensor(c, c, 1000.0, iota_e[:, :, 0:w], ALU.mult, ALU.add))
                link(v.tensor_reduce(out, c, AX_X, ALU.min))

            dve.wait_ge(rt_full, 1)
            link(v.tensor_tensor(lt, ps[2][:, 0:NT * NR].rearrange("p (t c) -> p t c", t=NT),
                                 b_rt.unsqueeze(1).to_broadcast([P, NT, NR]), ALU.add))
            gmax, gsum, gw, gidx, m1, m2, dm, e2, i1, i2, den, rden, w0, w1, p0, p1 = rs5[0:16]
            link(v.tensor_reduce(gmax, lt[:, :, 0:NG], AX_X, ALU.max))
            v.tensor_tensor(gs5, lt[:, :, 0:NG], per(gmax, NG), ALU.subtract).then_inc(rt_step, 1)
            dve.wait_ge(pool_step, 3 + N_TABLES)
            first_index(gidx, lt[:, :, 0:NG], gmax, NG)
            link(v.tensor_tensor(r_tmp, iota_g, per(gidx, NE), ALU.not_equal))
            link(v.scalar_tensor_tensor(elm, r_tmp, NEG, lt[:, :, NG:NR], ALU.mult, ALU.add))
            link(v.tensor_reduce(m1, elm, AX_X, ALU.max))
            first_index(i1, elm, m1, NE)
            link(v.tensor_tensor(hot0, iota_e, per(i1, NE), ALU.is_equal))
            link(v.scalar_tensor_tensor(elm, hot0, 3 * NEG, elm, ALU.mult, ALU.add))
            link(v.tensor_reduce(m2, elm, AX_X, ALU.max))
            first_index(i2, elm, m2, NE)
            link(v.tensor_tensor(hot1, iota_e, per(i2, NE), ALU.is_equal))
            v.tensor_tensor(hot_both, hot0, hot1, ALU.add).then_inc(rt_step, 1)
            v.tensor_tensor(dm, m2, m1, ALU.subtract).then_inc(rt_step, 1)
            dve.wait_ge(act_step, 3)
            link(v.tensor_reduce(gsum, ge5, AX_X, ALU.add))
            link(v.reciprocal(gw, gsum))
            dve.wait_ge(act_step, 4)
            link(v.tensor_scalar(den, e2, 1.0, None, ALU.add))
            link(v.reciprocal(rden, den))
            link(v.tensor_tensor(w0, gw, rden, ALU.mult))
            link(v.tensor_tensor(w1, w0, e2, ALU.mult))

            dve.wait_ge(rank_full, 1)
            rank = ps[3][:, 0:NT * NE].rearrange("p (t e) -> p t e", t=NT)
            total = ps[3][:, NT * NE:(NT + 1) * NE]
            nov, incl, delta, zero_e = rsE[0], rsE[1], rsE[2], rsE[3]
            v.memset(zero_e, 0.0)
            link(v.tensor_tensor(nov_t, total.unsqueeze(2).to_broadcast([P, NE, M_OVER]),
                                 thr.unsqueeze(1).to_broadcast([P, NE, M_OVER]), ALU.is_gt))
            link(v.tensor_reduce(nov, nov_t, AX_X, ALU.add))
            link(v.tensor_tensor_scan(incl, nov, zero_e, 0.0, ALU.add, ALU.add))
            link(v.tensor_tensor(delta, incl, nov, ALU.subtract))
            link(v.tensor_tensor(delta, delta, iota_e[:, 0, :], ALU.subtract))
            link(v.tensor_scalar(delta, delta, float(NE - 1), float(CAP), ALU.add, ALU.mult))
            link(v.tensor_scalar(elm, rank, float(CAP), None, ALU.is_ge))
            link(v.tensor_tensor(elm, elm, delta.unsqueeze(1).to_broadcast([P, NT, NE]), ALU.mult))
            link(v.tensor_tensor(elm, elm, rank, ALU.add))
            link(v.scalar_tensor_tensor(elm, iota_e, float(CAP), elm, ALU.mult, ALU.add))
            for j, (hot, p) in enumerate(((hot0, p0), (hot1, p1))):
                link(v.tensor_tensor(r_tmp, hot, elm, ALU.mult))
                link(v.tensor_reduce(p, r_tmp, AX_X, ALU.add))
                link(v.tensor_copy(rows[:, :, j], p))
            big = rt[:, 0:N_OVER * NE].rearrange("p (s e) -> p s e", e=NE)
            link(v.tensor_tensor(big, incl.unsqueeze(1).to_broadcast([P, N_OVER, NE]),
                                 rowi.unsqueeze(2).to_broadcast([P, N_OVER, NE]), ALU.is_le))
            link(v.tensor_reduce(ovs, big, AX_X, ALU.add))
            link(v.tensor_scalar(ovs, ovs, float(NE - 1), None, ALU.min))
            v.tensor_copy(rti[0:1, 0:N_OVER], ovs[0:1, :])
            v.tensor_copy(rti[0:1, N_OVER:N_OVER + 1], incl[0:1, NE - 1:NE]).then_inc(pos_ok, 1)

            def expert(q, at, out_wait, f_silu, f_hid, f_y, f_ysl):
                dve.wait_ge(f_silu, at)
                v.tensor_tensor(hid[q], act_g[q], ps[1][:, DF // P * CAP:2 * (DF // P) * CAP], ALU.mult).then_inc(f_hid, 1)
                dve.wait_ge(*out_wait)
                dve.wait_ge(f_y, at)
                v.tensor_copy(ysl[q][0:CAP, 0:BANK], ps[4][0:CAP, :])
                v.tensor_copy(ysl[q][0:CAP, BANK:D], ps[5][0:CAP, :]).then_inc(f_ysl, 1)

            with dve.Fori(0, NE // NES) as i:
                for s in range(NES):
                    expert(s % 2, i * NES + (s + 1), (ysl_out[s % 2], i * 32 + s // 2 * 16), silu_ok, hid_ok, y_full, ysl_ok)
            for q in range(2):
                dve.wait_ge(ysl_out[q], 16 * NE // 2)
            over = dve.value_load(rti[0:1, N_OVER:N_OVER + 1], min_val=0, max_val=N_OVER)
            with dve.If(over > 0):
                with dve.Fori(0, N_OVER) as i:
                    expert(0, i + (NE + 1), (ysl_out[0], i * 16 + 8 * NE), silu_ok, hid_ok, y_full, ysl_ok)

            for t in range(NT):
                q = t % 2
                dve.wait_ge(yg_in[q], 32 * (t // 2 + 1))
                link(v.scalar_tensor_tensor(x1[:, t, :], yg[2 * q], w0[:, t:t + 1], x1[:, t, :], ALU.mult, ALU.add))
                v.scalar_tensor_tensor(x1[:, t, :], yg[2 * q + 1], w1[:, t:t + 1], x1[:, t, :], ALU.mult, ALU.add)\
                    .then_inc(yg_used, 1)

        @block.gpsimd
        def _(pool):
            g = nc.gpsimd
            made = [0]

            def made_const(ins):
                made[0] += 1
                ins.then_inc(const_ok, 1)
                pool.wait_ge(const_ok, made[0])

            gains = [(g_x, "attn_norm_g"), (g_mem, "mem_norm_g"), (g_ki[:, :], "idx_k_norm_g"), (g_ka[:, :], "k_norm_g"),
                     (g_mk[:, :], "mem_k_norm_g")]
            for dst, name in gains:
                g.dma_start(dst, a[name].partition_broadcast(P)).then_inc(gain_in, 16)
            with nc.allow_non_contiguous_dma(reason="a few gains, one per partition"):
                g.dma_start(gcol_q, a["q_norm_g"].rearrange("l d -> d l")).then_inc(gain_in, 16)
                g.dma_start(gcol_o, a["gla_out_norm_g"][0].rearrange("(c d) -> d c", d=P)).then_inc(gain_in, 16)
                g.dma_start(gcol_qm, a["mem_q_norm_g"][0].rearrange("(c d) -> d c", d=P)).then_inc(gain_in, 16)

            g.dma_start(wga[0:RANK, :], a["w_gla_gate_up"][0]).then_inc(gain_in, 16)
            g.dma_start(wga[RANK:RANK + 1, :], a["b_gla_gate_up"]).then_inc(gain_in, 16)

            def result(t):
                pool.wait_ge(yg_used, t + 1)
                dst = o["y_s"].rearrange("b t d -> (b t) d") if t == NTP else o["y_p"][0, t * P:(t + 1) * P, :]
                g.dma_start(dst, x1[:, t, :]).then_inc(out_done, 16)

            def band(dst, value, tests, fill=0.0):
                made_const(g.memset(dst, value))
                for pattern, base, mult in tests:
                    made_const(g.affine_select(out=dst, in_=dst, compare_op=ALU.is_ge, fill=fill, base=base,
                                               pattern=pattern, channel_multiplier=mult))

            band(ident, 1.0, [([[-1, P]], 0, 1), ([[1, P]], 0, -1)])
            band(ones, 1.0, [])
            for cum, suf, n in ((cum_p, suf_p, P // CHUNK), (cum_s, suf_s, B)):
                w = P // n
                band(cum, 1.0 / GATE_TEMP, [([[1, P]], 0, -1), ([[-w, n], [0, w]], 0, 1)])
                band(suf, 1.0 / GATE_TEMP, [([[-1, P]], -1, 1), ([[w, n], [0, w]], w - 1, -1)])
            band(before, 1.0, [([[1, P]], -1, -1)])
            band(other, 0.0, [([[-TB, B], [0, TB]], 0, 1), ([[TB, B], [0, TB]], TB - 1, -1)], NEG)
            band(bsel[:, :], 1.0, [([[-TB, B]], 0, 1), ([[TB, B]], TB - 1, -1)])
            assert made[0] == N_CONST

            for half in range(2):
                for b in range(B):
                    g.dma_start(ci[:, b, :, half * DI:(half + 1) * DI], a["cache_idx_k"][0, b].rearrange("(s p) d -> p s d", p=P))\
                     .then_inc(ci_in, 16)

            g.memset(zrow, 0.0).then_inc(pool_step, 1)
            pool.wait_ge(pool_step, 1)
            g.dma_start(slot_rows.rearrange("(p n) d -> p n d", p=CAP), zrow[0:CAP, :].unsqueeze(1).to_broadcast([CAP, N_SLOT, D]))\
             .then_inc(fill_ok, 16)

            pool.wait_ge(kid_ok, NT)
            g.dma_start(o["ki_p"][0, 0].rearrange("(t p) d -> p t d", p=P), kid[:, 0:NTP, 0:DI]).then_inc(early_out, 16)
            g.dma_start(o["ki_s"][0].rearrange("b t d -> (b t) d"), kid[:, NTP, 0:DI]).then_inc(early_out, 16)

            pool.wait_ge(n_full, len(index["vg"]))
            g.memset(qem, 0.0)
            g.memset(attm_p, 0.0).then_inc(pool_step, 1)
            g.memset(attm_s, 0.0).then_inc(pool_step, 1)
            pool.wait_ge(la_ok, 1)

            def state_in(b):
                g.dma_start(state_s[b % 3], a["state_gla"][0, b].rearrange("h k v -> k h v")).then_inc(st_in[b % 3], 16)

            for b in range(3):
                state_in(b)
            pool.wait_ge(state_ok, 2 * NTP + 1)
            g.dma_start(o["state_p"][0, 0].rearrange("h k v -> k h v"), state).then_inc(early_out, 16)
            for b in range(B):
                pool.wait_ge(states_ok, b + 1)
                g.dma_start(o["state_s"][0, b].rearrange("h k v -> k h v"), state_s[b % 3]).then_inc(st_out[b % 3], 16)
                if b + 3 < B:
                    pool.wait_ge(st_out[b % 3], 16 * (b // 3 + 1))
                    state_in(b + 3)

            def cached(name, b):
                g.dma_start(kvb[b % 2], a[name][0, b].rearrange("(m p) h d -> p m (h d)", p=P)).then_inc(kvb_in[b % 2], 16)

            pool.wait_ge(og_ok, NT)
            pool.wait_ge(kvs_full, B)
            for b in range(2):
                cached("cache_mem_k", b)
            pool.wait_ge(n_free_act, len(by_act))
            g.dma_start(o["mv_p"][0, 0].rearrange("(m p) h d -> p m (h d)", p=P), mv).then_inc(mem_out, 16)
            pool.wait_ge(qn_ok, normed_before("mk"))
            for m in range(NM):
                g.dma_start(o["mk_p"][0, 0].rearrange("(m p) h d -> m p (h d)", p=P)[m], mkn[:, m, :]).then_inc(mem_out, 16)
            for b in range(2, B):
                pool.wait_ge(kmT_full, 4 * (b - 1))
                cached("cache_mem_k", b)
            for b in range(B):
                if b < 2:
                    pool.wait_ge(kmT_full, 4 * (B - 1 + b))
                else:
                    pool.wait_ge(mk_used, b - 1)
                cached("cache_mem_v", b)

            for s in range(4):
                pool.wait_ge(t_full[s], U_MERGE[1] + 4)
            for b in range(B):
                g.dma_start(kc[:, b, :, :], a["cache_k"][0, b].rearrange("(s p) k d -> p s (k d)", p=P)).then_inc(kc_in, 16)
            pool.wait_ge(qn_ok, normed_before("kv"))
            for src, dp, ds in ((kn, "k_p", "k_s"), (va, "v_p", "v_s")):
                g.dma_start(o[dp][0, 0].rearrange("(t p) k d -> p t (k d)", p=P), src[:, 0:NTP, :]).then_inc(kv_out, 16)
                g.dma_start(o[ds][0].rearrange("b t k d -> (b t) (k d)"), src[:, NTP, :]).then_inc(kv_out, 16)
            pool.wait_ge(kcT_full, B)
            for b in range(B):
                g.dma_start(kc[:, b, :, :], a["cache_v"][0, b].rearrange("(s p) k d -> p s (k d)", p=P)).then_inc(vc_in, 16)

            for s in range(4):
                pool.wait_ge(t_full[s], U_MERGE[2] + 4)
            g.dma_start(xr[:, 0:NTP, :], a["x_prompt"][0].rearrange("(t p) d -> p t d", p=P)).then_inc(xr_in, 16)
            g.dma_start(xr[:, NTP, :], xs).then_inc(xr_in, 16)

            pool.wait_ge(x1_ok, 2 * NT)
            f32 = dict(allow_small_or_imprecise_dtypes=True)
            g.iota(iota_e, [[0, NT], [1, NE]], base=0, channel_multiplier=0, **f32)
            g.iota(iota_g, [[0, NT], [1, NG], [0, EPG]], base=0, channel_multiplier=0, **f32)
            g.iota(thr, [[CAP, M_OVER]], base=CAP, channel_multiplier=0, **f32)
            g.iota(rowi, [[1, N_OVER]], base=0, channel_multiplier=0, **f32).then_inc(pool_step, 1)

            pool.wait_ge(pos_ok, 1)
            pool.wait_ge(fill_ok, 16)
            for t in range(NT):
                for j in range(2):
                    g.indirect_dma_start(slot_rows, bass.IndirectOffsetOnAxis(ap=rows[:, t, j:j + 1].bitcast(U32), axis=0),
                                         h2[:, t, :], None).then_inc(scat, 16)

            with pool.Fori(0, NE // NES) as i:
                for s in range(NES):
                    pool.wait_ge(ysl_ok, i * NES + (s + 1))
                    g.dma_start(slot_rows[bass.ds(i * (NES * CAP) + s * CAP, CAP), :], ysl[s % 2][0:CAP, :]).then_inc(ysl_out[s % 2], 16)
            over = pool.value_load(rti[0:1, N_OVER:N_OVER + 1], min_val=0, max_val=N_OVER)
            with pool.If(over > 0):
                with pool.Fori(0, N_OVER) as i:
                    pool.wait_ge(ysl_ok, i + (NE + 1))
                    g.dma_start(slot_rows[bass.ds(i * CAP + NE * CAP, CAP), :], ysl[0][0:CAP, :]).then_inc(ysl_out[0], 16)
                pool.wait_ge(ysl_out[0], 16 * (NE // 2 + N_OVER))
            for q in range(2):
                pool.wait_ge(ysl_out[q], 16 * NE // 2)
            for t in range(NT):
                q = t % 2
                if t >= 2:
                    pool.wait_ge(yg_used, t - 1)
                for j in range(2):
                    g.indirect_dma_start(yg[2 * q + j], None, slot_rows,
                                         bass.IndirectOffsetOnAxis(ap=rows[:, t, j:j + 1].bitcast(U32), axis=0)).then_inc(yg_in[q], 16)
                if t:
                    result(t - 1)
            result(NT - 1)
            pool.wait_ge(out_done, 16 * NT)
            pool.wait_ge(mem_out, 48)
            pool.wait_ge(kv_out, 64)


_INS = ["x_prompt", "x_sample", "mem_prompt", "cache_k", "cache_v", "cache_idx_k", "state_gla", "cache_mem_k",
        "cache_mem_v", "attn_norm_g", "w_in", "q_norm_g", "k_norm_g", "idx_k_norm_g", "w_gla_gate_up", "b_gla_gate_up",
        "gla_out_norm_g", "mem_norm_g", "w_mem_kv", "mem_q_norm_g", "mem_k_norm_g", "w_branch_a", "w_branch_g",
        "w_branch_m", "w_out", "ffn_norm_g", "w_group_router", "b_group_router", "w_expert_router",
        "b_expert_router", "w_exp_gate", "w_exp_up", "w_exp_down"]
_OUTS = [("y_p", "x_prompt"), ("y_s", "x_sample"), ("k_p", None), ("v_p", None), ("ki_p", None), ("state_p", None),
         ("mk_p", None), ("mv_p", None), ("k_s", None), ("v_s", None), ("ki_s", None), ("state_s", "state_gla")]


def kernel(**inputs):
    import numpy as np
    import concourse.bacc as bacc
    from concourse.bass_utils import run_bass_kernel_spmd

    arrays = {n: np.ascontiguousarray(inputs[n]) for n in _INS}
    depth, db, past, kv, hd = arrays["cache_k"].shape
    _, tp, _ = arrays["x_prompt"].shape
    _, tb, _ = arrays["x_sample"].shape
    di = arrays["cache_idx_k"].shape[-1]
    hg, dk, dv = arrays["state_gla"].shape[2:]
    m, hm, hdm = arrays["cache_mem_k"].shape[2:]
    shapes = {"k_p": (depth, 1, tp, kv, hd), "v_p": (depth, 1, tp, kv, hd), "ki_p": (depth, 1, tp, di),
              "state_p": (depth, 1, hg, dk, dv), "mk_p": (depth, 1, m, hm, hdm), "mv_p": (depth, 1, m, hm, hdm),
              "k_s": (depth, db, tb, kv, hd), "v_s": (depth, db, tb, kv, hd), "ki_s": (depth, db, tb, di)}
    nc = bacc.Bacc("TRN2", target_bir_lowering=False, num_devices=1)
    a = {n: nc.dram_tensor(f"in_{n}", arrays[n].shape, F32, kind="ExternalInput").ap() for n in _INS}
    o = {}
    for n, like in _OUTS:
        shape = arrays[like].shape if like else shapes[n]
        o[n] = nc.dram_tensor(f"out_{n}", shape, F32, kind="ExternalOutput").ap()
    build(nc, a, o)
    r = run_bass_kernel_spmd(nc, [{f"in_{n}": x for n, x in arrays.items()}], core_ids=[0])
    return tuple(r.results[0][f"out_{n}"] for n, _ in _OUTS)
```

```python
from contextlib import ExitStack

import concourse.bass as bass
from concourse import mybir

F32 = mybir.dt.float32
I32 = mybir.dt.int32
U32 = mybir.dt.uint32
ALU = mybir.AluOpType
ACT = mybir.ActivationFunctionType
AX_X = mybir.AxisListType.X

P = 128
BANK = 512
CHUNK = 64
EPS = 1e-6
NEG = -1e30
TAKEN = -3e38
GATE_TEMP = 16.0
TOPK_MAX = 256


def build(nc, a, o):
    _, TP, D = a["x_prompt"].shape
    B, TB, _ = a["x_sample"].shape
    TS = B * TB
    PAST = a["cache_k"].shape[2]
    KV, HD = a["cache_k"].shape[3:]
    DI = a["cache_idx_k"].shape[3]
    M, HM, HDM = a["cache_mem_k"].shape[2:]
    HG, DK, DV = a["state_gla"].shape[2:]
    RANK = a["w_gla_gate_up"].shape[1]
    HA = a["w_branch_a"].shape[1] // HD
    NG = a["w_group_router"].shape[2]
    NE, _, DF = a["w_exp_gate"].shape[1:]
    EPG = NE // NG
    D_IN = a["w_in"].shape[2]
    HI = (D_IN - (HA + 2 * KV) * HD - DI - 2 * HG * DK - 2 * HG * DV - RANK - HM * HDM - 3 * D) // (DI + 1)
    KD = D // P
    T = TP + TS
    NTP = TP // P
    NT = T // P
    NM = M // P
    TOPK_P = min(TOPK_MAX, TP // 4)
    TOPK_S = min(TOPK_MAX, (PAST + TB) // 4)
    GQ = HA // KV
    PB = PAST // P
    KS = PAST + TS
    assert TS == P and TP == 4 * P and D == 8 * P and HD == P and DK == P and GQ == 4 and HM * HDM == D
    assert DI == 64 and HI == 16 and HG == 4 and DV == 256 and NM == 2 and PB == 2 and 4 * DF == D
    sizes = [HA * HD, KV * HD, KV * HD, HI * DI, DI, HI, HG * DK, HG * DK, HG * DV, RANK, HG * DV, HM * HDM, 3 * D]
    offs = [sum(sizes[:n]) for n in range(len(sizes))]
    (C_QA, C_KA, C_VA, C_QI, C_KI, C_WI, C_QG, C_KG, C_VG, C_LR, C_GO, C_QM, C_GB) = offs
    assert offs[-1] + sizes[-1] == D_IN

    CAP = 64
    N_PAIR = 2 * T
    N_OVER = N_PAIR // (CAP + 1)
    N_SLOT = NE + N_OVER
    M_OVER = (T - 1) // CAP
    slot_rows = nc.dram_tensor("slot_rows", [N_SLOT * CAP, D], F32, kind="Internal").ap()

    w_in = a["w_in"][0].rearrange("(k p) c -> p k c", p=P)
    w_mem = a["w_mem_kv"][0].rearrange("(k p) c -> p k c", p=P)
    w_out = a["w_out"][0].rearrange("(k p) c -> p k c", p=P)
    w_br = [a["w_branch_" + n][0].rearrange("(k p) c -> p k c", p=P) for n in "gma"]
    w_gate, w_up = (a[n][0].rearrange("e (k p) f -> e p k f", p=P) for n in ("w_exp_gate", "w_exp_up"))
    w_down = a["w_exp_down"][0].rearrange("e (f p) c -> e p f c", p=P)
    xp = a["x_prompt"][0].rearrange("(t p) d -> t p d", p=P)
    xs = a["x_sample"].rearrange("b t d -> (b t) d")
    memx = a["mem_prompt"][0].rearrange("(t p) d -> t p d", p=P)
    x_tile = [xp[t] for t in range(NTP)] + [xs]

    with ExitStack() as ctx:
        def sb(name, words, dt=F32):
            return ctx.enter_context(nc.sbuf_tensor(name, [P, words], dt))

        def sem(name):
            return ctx.enter_context(nc.semaphore(name))

        HTW, MGW, RGW, TWW = KD * (T + M), KD * T, 2 * KD * BANK, 4 * KD * P
        EW = 3 * KD * DF
        NES = 4
        bulk = sb("bulk", HTW + MGW + RGW + TWW)
        assert HTW + MGW + RGW + TWW == NES * EW
        hT = bulk[:, 0:HTW].rearrange("p (k t) -> p k t", k=KD)
        region_m = bulk[:, HTW:HTW + MGW]
        merged = region_m.rearrange("p (k t) -> p k t", k=KD)
        region_r = bulk[:, HTW + MGW:HTW + MGW + RGW]
        ring = [region_r[:, s * KD * BANK:(s + 1) * KD * BANK].rearrange("p (k c) -> p k c", k=KD) for s in range(2)]
        region_t = bulk[:, HTW + MGW + RGW:]
        tw = [region_t[:, s * KD * P:(s + 1) * KD * P].rearrange("p (k c) -> p k c", k=KD) for s in range(4)]
        ew = [bulk[:, s * EW:(s + 1) * EW] for s in range(NES)]
        ew_gate = [w[:, 0:KD * DF].rearrange("p (k f) -> p k f", k=KD) for w in ew]
        ew_up = [w[:, KD * DF:2 * KD * DF].rearrange("p (k f) -> p k f", k=KD) for w in ew]
        ew_down = [w[:, 2 * KD * DF:].rearrange("p (f c) -> p f c", f=DF // P) for w in ew]

        arena = sb("arena", 80 * 256)

        def cut(region, kib, words):
            w0 = int(kib * 256)
            return region[:, w0:w0 + words]

        work_w = [(t + 1) * P for t in range(NTP)] + [KS]
        work_all = sb("work_all", sum(work_w))
        work = [work_all[:, sum(work_w[:t]):sum(work_w[:t + 1])] for t in range(NT)]
        mix = sb("mix", 4 * T)
        sg = [mix[:, q * T:(q + 1) * T] for q in range(2)]
        prod = [mix[:, (2 + q) * T:(3 + q) * T] for q in range(2)]
        sq = [mix[:, q * BANK:(q + 1) * BANK] for q in range(2)]
        qn = [mix[:, (2 + q) * BANK:(3 + q) * BANK] for q in range(2)]
        cst = sb("cst", 8 * P)
        ident, cum_p, suf_p, cum_s, suf_s, before, ones, other = (cst[:, n * P:(n + 1) * P] for n in range(8))
        bsel = sb("bsel", B)
        g_ki = sb("g_ki", DI)
        g_ka = sb("g_ka", HD)
        g_mk = sb("g_mk", HDM)
        gcols = sb("gcols", 8)
        gcol_q, gcol_o, gcol_qm = gcols[:, 0:1], gcols[:, 1:3], gcols[:, 3:5]
        wsm = sb("wsm", KD * (DI + HI + RANK))
        wsm = wsm[:, :].rearrange("p (k c) -> p k c", k=KD)
        wga = sb("wga", HG * DK)
        wi = sb("wi", NT * HI)
        wi = wi[:, :].rearrange("p (t h) -> p t h", t=NT)
        st = sb("st", 256)
        ss0, rs0 = st[:, 0:8], st[:, 8:16]
        ssk, rsk = st[:, 16:24], st[:, 24:32]
        ssn, rsn = st[:, 32:36], st[:, 36:40]
        sso, rso = st[:, 40:44], st[:, 44:48]
        dec = st[:, 48:80].rearrange("p (h c) -> p h c", h=HG)
        mx, nmx, sm, rsm = (st[:, 80 + 8 * n:88 + 8 * n] for n in range(4))
        top8 = st[:, 112:120]
        top8s = st[:, 120:128]
        newton = st[:, 144:152]
        ssf, rsf = st[:, 128:136], st[:, 136:144]

        ps = [ctx.enter_context(nc.psum_tensor(f"ps{n}", [P, BANK], F32)) for n in range(8)]

        xt = cut(arena, 0, (NT + NM) * D).rearrange("p (t d) -> p t d", d=D)
        qiT = cut(arena, 28, KD * T).rearrange("p (k t) -> p k t", k=KD)
        ci = cut(arena, 48, B * PB * P).rearrange("p (b s d) -> p b s d", b=B, s=PB)
        ciT = cut(arena, 56, B * PAST).rearrange("p (b s) -> p b s", b=B)
        wdiag = cut(arena, 0, HI * TS).rearrange("p (h t) -> p h t", h=HI)
        g_x, g_mem = cut(arena, 64, D), cut(arena, 68, D)
        kiT = cut(arena, 72.5, T)
        zrow = cut(arena, 76, D)
        wB = cut(region_m, 0, HI * TS).rearrange("p (h t) -> p h t", h=HI)
        rel = [cut(region_m, 8 + 2 * n, BANK) for n in range(3)]
        sT = cut(region_m, 14, PB * TS).rearrange("p (s t) -> p s t", s=PB)
        sct = [cut(region_m, 15 + n, HI * TB) for n in range(2)]
        kid = cut(region_m, 17, NT * P).rearrange("p (t d) -> p t d", t=NT)
        qkT = cut(arena, 0, 2 * HG * T).rearrange("p (h t) -> p h t", h=2 * HG)
        goT = cut(arena, 20, KD * T).rearrange("p (k t) -> p k t", k=KD)
        vg = cut(arena, 40, NT * HG * DV).rearrange("p (t c) -> p t c", t=NT)
        la = cut(arena, 60, NT * HG * DK).rearrange("p (t c) -> p t c", t=NT)
        glrT = cut(arena, 70, T)
        zabs = cut(region_m, 0, NT * HG * DK).rearrange("p (t c) -> p t c", t=NT)
        state = cut(region_m, 0, HG * DV).rearrange("p (h v) -> p h v", h=HG)
        state_s = [cut(region_m, 4 + 4 * n, HG * DV).rearrange("p (h v) -> p h v", h=HG) for n in range(3)]
        on = cut(region_m, 16, HG * DV)
        qem = cut(region_r, 0, B * (HG * P + TB))
        glt = [cut(region_r, 17 + 2 * n, BANK) for n in range(7)] + [cut(arena, 76.5, BANK)]
        eb, enb, qe, ke, kd, attm_p, attm_s, kdf = (v.rearrange("p (h t) -> p h t", h=HG) for v in glt)
        kdm = [v.rearrange("p (h t) -> p h t", h=HG) for v in (cut(arena, 72.5, BANK), cut(arena, 74.5, BANK))]
        mv = cut(arena, 0, NM * D).rearrange("p (m c) -> p m c", m=NM)
        mkT = cut(arena, 8, KD * M).rearrange("p (k m) -> p k m", k=KD)
        qmT = cut(arena, 16, KD * T).rearrange("p (k t) -> p k t", k=KD)
        pmT = cut(arena, 36, NM * HM * T).rearrange("p (m h t) -> p m h t", m=NM, h=HM)
        kmT = [cut(arena, 36 + 8 * n, KD * M).rearrange("p (k m) -> p k m", k=KD) for n in range(2)]
        mkn = cut(arena, 56, NM * D).rearrange("p (m c) -> p m c", m=NM)
        pm = [cut(arena, 56 + 4 * n, HM * M) for n in range(2)]
        kvb = [x.rearrange("p (m c) -> p m c", m=NM)
               for x in (cut(arena, 64, NM * D), cut(arena, 72, NM * D), mix[:, 0:NM * D])]
        lmT = cut(arena, 52, NM * HM * TS).rearrange("p (m h t) -> p m h t", m=NM, h=HM)
        qaT = cut(arena, 0, KD * T).rearrange("p (k t) -> p k t", k=KD)
        kT = cut(arena, 20, KV * T).rearrange("p (k t) -> p k t", k=KV)
        va = cut(arena, 25, NT * KV * HD).rearrange("p (t c) -> p t c", t=NT)
        kn = cut(arena, 30, NT * KV * HD).rearrange("p (t c) -> p t c", t=NT)
        kc = cut(arena, 35, B * PB * KV * HD).rearrange("p (b s c) -> p b s c", b=B, s=PB)
        kcT = cut(arena, 51, B * KV * PAST).rearrange("p (b k s) -> p b k s", b=B, k=KV)
        paT = [cut(arena, 51 + 8 * n, 4 * BANK).rearrange("p (s h t) -> p s h t", s=4, h=GQ) for n in range(2)]
        lsT = cut(arena, 67, KV * PB * BANK).rearrange("p (k s h t) -> p k s h t", k=KV, s=PB, h=GQ)
        lg = [mix[:, q * BANK:(q + 1) * BANK] for q in range(3)]
        pr = [mix[:, (3 + q) * BANK:(4 + q) * BANK] for q in range(2)] + [cut(arena, 75, BANK)]
        lg_bank, prT_bank = (0, 1, 6), (2, 3, 7)
        xr = cut(arena, 0, NT * D).rearrange("p (t d) -> p t d", t=NT)
        x1 = cut(arena, 20, NT * D).rearrange("p (t d) -> p t d", t=NT)
        h2 = cut(arena, 40, NT * D).rearrange("p (t d) -> p t d", t=NT)
        h2T = cut(arena, 60, KD * T).rearrange("p (k t) -> p k t", k=KD)
        g_ffn = tw[0].rearrange("p k c -> p (k c)")
        NR = NG + NE
        w_rt = tw[1].rearrange("p k c -> p (k c)")[:, 0:KD * NR].rearrange("p (k c) -> p k c", k=KD)
        b_rt = tw[2].rearrange("p k c -> p (k c)")[:, 0:NR]
        rti = sb("rti", 64, I32)
        rt = ew[3]
        rt3 = [rt[:, n * NT * NE:(n + 1) * NT * NE].rearrange("p (t e) -> p t e", t=NT) for n in range(8)]
        hot0, hot1, hot_both, el, elm, r_tmp, iota_e, iota_g = rt3
        r0 = 8 * NT * NE
        lt = rt[:, r0:r0 + NT * NR].rearrange("p (t c) -> p t c", t=NT)
        r1 = r0 + NT * NR
        nov_t = rt[:, r1:r1 + NE * M_OVER].rearrange("p (e m) -> p e m", e=NE)
        assert r1 + NE * M_OVER <= 2048
        rs = sb("rs", 512)
        rs5 = [rs[:, n * NT:(n + 1) * NT] for n in range(24)]
        rsE = [rs[:, 128 + n * NE:128 + (n + 1) * NE] for n in range(6)]
        gs5 = rs[:, 320:320 + NT * NG].rearrange("p (t g) -> p t g", t=NT)
        ge5 = rs[:, 340:340 + NT * NG].rearrange("p (t g) -> p t g", t=NT)
        thr = rs[:, 360:360 + M_OVER]
        ovs = rs[:, 380:380 + N_OVER]
        rowi = rs[:, 400:400 + N_OVER]
        rows = rti[:, 24:24 + 2 * NT].rearrange("p (t j) -> p t j", j=2)
        hs = [cut(arena, 4 * n, D) for n in range(NES)]
        hsT = [cut(arena, 16 + 2 * n, KD * CAP).rearrange("p (k t) -> p k t", k=KD) for n in range(2)]
        hid = [cut(arena, 68 + n, DF // P * CAP) for n in range(2)]
        act_g = [cut(arena, 70 + n, DF // P * CAP) for n in range(2)]
        oT = [cut(arena, 40 + 2 * n, KD * CAP).rearrange("p (k t) -> p k t", k=KD) for n in range(2)]
        ysl = [cut(arena, 44 + 4 * n, D) for n in range(2)]
        yg = [cut(arena, 52 + 4 * n, D) for n in range(4)]

        x_in = [sem(f"x_in{t}") for t in range(3)]
        ring_in = [sem(f"ring_in{s}") for s in range(2)]
        tw_in = [sem(f"tw_in{s}") for s in range(4)]
        wsm_in, gain_in, ci_in, kc_in, vc_in, xr_in, rtw_in = (
            sem(n) for n in ("wsm_in", "gain_in", "ci_in", "kc_in", "vc_in", "xr_in", "rtw_in"))
        g_norm_in = xr_in
        const_ok, zero_ok = sem("const_ok"), sem("zero_ok")
        dve_step, act_step, pool_step = sem("dve_step"), sem("act_step"), sem("pool_step")
        ss_ok, xn_ok, xT_full, hT_ok = sem("ss_ok"), sem("xn_ok"), sem("xT_full"), sem("hT_ok")
        kiw_full, kiss_ok, kid_ok, glr_full, glr_ok, kidT_full, kiT_ok = (
            sem(n) for n in ("kiw_full", "kiss_ok", "kid_ok", "glr_full", "glr_ok", "kidT_full", "kiT_ok"))
        t_full = [sem(f"t_full{s}") for s in range(4)]
        t_free = [sem(f"t_free{s}") for s in range(4)]
        sc_full = [sem(f"sc_full{n}") for n in range(3)]
        rel_ok = [sem(f"rel_ok{n}") for n in range(3)]
        acc_ok = sem("acc_ok")
        ciT_full, ciT_ok, wd_ok = (sem(n) for n in ("ciT_full", "ciT_ok", "wd_ok"))
        scs_full, scs_ok = sem("scs_full"), sem("scs_ok")
        n_full, n_free_act = sem("n_full"), sem("n_free_act")
        sq_ok, qn_ok, qT_full, qT_ok, kv_ok = (sem(n) for n in ("sq_ok", "qn_ok", "qT_full", "qT_ok", "kv_ok"))
        z_full, z_ok, la_ok = (sem(n) for n in ("z_full", "z_ok", "la_ok"))
        bT_full, suf_full, kt_full, eb_ok, kdf_ok, qe_ok, kd_ok, att_full, attm_ok = (
            sem(n) for n in ("bT_full", "suf_full", "kt_full", "eb_ok", "kdf_ok", "qe_ok", "kd_ok", "att_full", "attm_ok"))
        kv_full, state_ok, o_full, oss_ok, on_ok, oT_full, og_ok = (
            sem(n) for n in ("kv_full", "state_ok", "o_full", "oss_ok", "on_ok", "oT_full", "og_ok"))
        st_in = [sem(f"st_in{n}") for n in range(3)]
        st_out = [sem(f"st_out{n}") for n in range(3)]
        kdm_ok, qem_ok, kvs_full, states_ok = sem("kdm_ok"), sem("qem_ok"), sem("kvs_full"), sem("states_ok")
        sg_ok = [sem(f"sg_ok{q}") for q in range(2)]
        m_prod = [sem(f"m_prod{q}") for q in range(2)]
        merged_ok = sem("merged_ok")
        kvb_in = [sem("kvb_in0"), sem("kvb_in1"), kc_in]
        kmT_full, kmT_ok, lmT_full, lmT_ok, mk_used = (
            sem(n) for n in ("kmT_full", "kmT_ok", "lmT_full", "lmT_ok", "mk_used"))
        lm_full, mmx_ok, pm_ok, pmn_ok, pmT_full, pmT_ok, om_full, om_ok = (
            sem(n) for n in ("lm_full", "mmx_ok", "pm_ok", "pmn_ok", "pmT_full", "pmT_ok", "om_full", "om_ok"))
        kcT_full, kcT_ok, lsT_full, lsT_ok = (sem(n) for n in ("kcT_full", "kcT_ok", "lsT_full", "lsT_ok"))
        lg_full, lg_ok, pr_ok, prn_ok, prT_full, prT_ok, oa_full, oa_ok = (
            sem(n) for n in ("lg_full", "lg_ok", "pr_ok", "prn_ok", "prT_full", "prT_ok", "oa_full", "oa_ok"))
        x1_ok, ssf_ok, h2_ok, h2T_full, h2T_ok, rt_full, rt_step = (
            sem(n) for n in ("x1_ok", "ssf_ok", "h2_ok", "h2T_full", "h2T_ok", "rt_full", "rt_step"))
        rank_full, pos_ok, scat = sem("rank_full"), sem("pos_ok"), sem("scat")
        ew_in = [sem(f"ew_in{s}") for s in range(NES)]
        (hsT_full, hsT_ok, gu_full, silu_ok, hid_ok, dn_full, oTs_ok, y_full, ysl_ok) = (
            sem(n) for n in ("hsT_full", "hsT_ok", "gu_full", "silu_ok", "hid_ok", "dn_full", "oTs_ok", "y_full", "ysl_ok"))
        ysl_out = [sem(f"ysl_out{n}") for n in range(2)]
        early_out, mem_out, kv_out, fill_ok = (sem(n) for n in ("early_out", "mem_out", "kv_out", "fill_ok"))
        yg_in, yg_used = [sem(f"yg_in{n}") for n in range(2)], sem("yg_used")
        pe_seen = sem("pe_seen")
        out_done = sem("out_done")

        fills, items = [], []

        def plan(kind, weights, col, n_fill, tiles):
            for c in range(n_fill):
                for t in tiles:
                    items.append((kind, len(fills), t, c))
                fills.append((weights, col + c * BANK))

        every, mems = list(range(NT)), list(range(NM))
        plan("vg", w_in, C_VG, HG * DV // BANK, every)
        plan("mk", w_mem, 0, D // BANK, mems)
        plan("mv", w_mem, D, D // BANK, mems)
        plan("qm", w_in, C_QM, HM * HDM // BANK, every)
        plan("kv", w_in, C_KA, 1, every)
        plan("qa", w_in, C_QA, HA * HD // BANK, every)
        plan("out", w_out, 0, D // BANK, every)
        NORMED = ("mk", "qm", "kv", "qa")
        index = {kind: [n for n, it in enumerate(items) if it[0] == kind] for kind in ("vg", "mk", "mv", "qm", "kv", "qa", "out")}
        normed = [n for n, it in enumerate(items) if it[0] in NORMED]
        by_act = [n for n, it in enumerate(items) if it[0] in ("vg", "mv")]

        last_item = [max(n for n, it in enumerate(items) if it[1] == f) for f in range(len(fills))]
        N_CONST, N_GAINS, N_TABLES = 24, 8, 1
        N_IDENT = 3
        N_REL = (NT - 1) * HI

        def item_out(n):
            if n in normed:
                return qn_ok, normed.index(n) + 1
            if n in by_act:
                return n_free_act, by_act.index(n) + 1
            return x1_ok, index["out"].index(n) + 1

        def normed_before(kind):
            return normed.index(index[kind][-1]) + 1

        U_QI, U_QK, U_GO, U_MERGE = 1, 3, 5, [7, 11, 15]

        row_in, ROWS_IN = tw_in, 16 * (U_MERGE[2] + 3)
        BR_GATE = [1, 2, 0]
        s_tiles = [NT - 1] + list(range(NTP))

        block = ctx.enter_context(nc.Block())

        @block.sync
        def _(sp):
            for t in range(NT):
                sp.dma_start(xt[:, t, :], x_tile[t]).then_inc(x_in[min(t, 2)], 16)
            for m in range(NM):
                sp.dma_start(xt[:, NT + m, :], memx[m]).then_inc(x_in[2], 16)
            sp.dma_start(wsm[:, :, 0:DI + HI], w_in[:, :, C_KI:C_KI + DI + HI]).then_inc(wsm_in, 16)
            sp.dma_start(wsm[:, :, DI + HI:], w_in[:, :, C_LR:C_LR + RANK]).then_inc(wsm_in, 16)

            def narrow_job(col, u):
                with sp.Fori(0, 2) as i:
                    for s in range(4):
                        at = sp.snap(i * (4 * P) + (col + s * P))
                        sp.wait_ge(t_full[s], i + u)
                        sp.dma_start(tw[s], w_in[:, :, bass.ds(at, P)]).then_inc(tw_in[s], 16)

            def merge_job(br, u):
                with sp.Fori(0, 4) as i:
                    for q in range(2):
                        sp.wait_ge(t_full[2 * q + 1], i + u)
                        sp.dma_start(tw[2 * q + 1], w_br[br][:, :, bass.ds(i * (2 * P) + q * P, P)]).then_inc(tw_in[2 * q + 1], 16)
                        sp.wait_ge(t_full[2 * q], i + u)
                        sp.dma_start(tw[2 * q], w_in[:, :, bass.ds(i * (2 * P) + (C_GB + BR_GATE[br] * D + q * P), P)])\
                          .then_inc(tw_in[2 * q], 16)

            def wide_fill(f):
                if f >= 2:
                    sp.wait_ge(n_full, last_item[f - 2] + 1)
                src, col = fills[f]
                sp.dma_start(ring[f % 2], src[:, :, col:col + BANK]).then_inc(ring_in[f % 2], 16)

            narrow_job(C_QI, U_QI)
            wide_fill(0)
            wide_fill(1)
            narrow_job(C_QG, U_QK)
            narrow_job(C_GO, U_GO)
            merge_job(0, U_MERGE[0])
            sp.wait_ge(og_ok, NT)
            for f in range(2, 8):
                wide_fill(f)
            merge_job(1, U_MERGE[1])
            for f in range(8, 11):
                wide_fill(f)
            merge_job(2, U_MERGE[2])
            for f in range(11, 13):
                wide_fill(f)
            for s in range(4):
                sp.wait_ge(t_full[s], U_MERGE[2] + 4)
            sp.dma_start(g_ffn, a["ffn_norm_g"].partition_broadcast(P)).then_inc(rtw_in, 16)
            sp.dma_start(w_rt[:, :, 0:NG], a["w_group_router"][0].rearrange("(k p) g -> p k g", p=P)).then_inc(rtw_in, 16)
            sp.dma_start(w_rt[:, :, NG:NR], a["w_expert_router"][0].rearrange("(k p) g -> p k g", p=P)).then_inc(rtw_in, 16)
            sp.dma_start(b_rt[:, 0:NG], a["b_group_router"].partition_broadcast(P)).then_inc(rtw_in, 16)
            sp.dma_start(b_rt[:, NG:NR], a["b_expert_router"].partition_broadcast(P)).then_inc(rtw_in, 16)

            def load_expert(s, e, done):
                sp.dma_start(ew_gate[s], w_gate[e] if isinstance(e, int) else w_gate[bass.ds(e, 1)].squeeze(0)).then_inc(done, 16)
                sp.dma_start(ew_up[s], w_up[e] if isinstance(e, int) else w_up[bass.ds(e, 1)].squeeze(0)).then_inc(done, 16)
                sp.dma_start(ew_down[s], w_down[e] if isinstance(e, int) else w_down[bass.ds(e, 1)].squeeze(0)).then_inc(done, 16)

            def load_rows(s, row, done):
                sp.dma_start(hs[s][0:CAP, :], slot_rows[bass.ds(row, CAP), :]).then_inc(done, 16)

            sp.wait_ge(x1_ok, 2 * NT)
            for s in range(3):
                load_expert(s, s, ew_in[s])
            sp.wait_ge(pos_ok, 1)
            load_expert(3, 3, ew_in[3])
            sp.wait_ge(scat, 32 * NT)
            for s in range(NES):
                load_rows(s, s * CAP, row_in[s])
            with sp.Fori(1, NE // NES) as i:
                for s in range(NES):
                    e = sp.snap(i * NES + s)
                    row = sp.snap(i * (NES * CAP) + s * CAP)
                    sp.wait_ge(dn_full, i * NES + (s + 1 - NES))
                    load_expert(s, e, ew_in[s])
                    load_rows(s, row, row_in[s])

            over = sp.value_load(rti[0:1, N_OVER:N_OVER + 1], min_val=0, max_val=N_OVER)
            sp.wait_ge(dn_full, NE)
            with sp.If(over > 0):
                with sp.Fori(0, N_OVER) as i:
                    sp.wait_ge(dn_full, i + NE)
                    e = sp.value_load(rti[0:1, bass.ds(i, 1)], min_val=0, max_val=NE - 1)
                    load_expert(0, e, ew_in[0])
                    load_rows(0, i * CAP + NE * CAP, row_in[0])

        @block.tensor
        def _(pe):
            mm, tr = nc.tensor.matmul, nc.tensor.transpose

            for s in range(4):
                pe.sem_inc(t_full[s], 1)

            pe.wait_ge(const_ok, N_IDENT)
            for t in range(NT + NM):
                pe.wait_ge(xn_ok, t + 1)
                for h in range(2):
                    n = 2 * t + h
                    if n >= 2:
                        pe.wait_ge(hT_ok, n - 1)
                    for k in range(4):
                        last = tr(ps[n % 2][:, k * P:(k + 1) * P], xt[:, t, (4 * h + k) * P:(4 * h + k + 1) * P], ident)
                    last.then_inc(xT_full, 1)

            pe.wait_ge(hT_ok, 2 * (NT + NM))
            pe.wait_ge(wsm_in, 32)
            pe.wait_ge(const_ok, N_CONST)
            for t in range(NT):
                if t >= 2:
                    pe.wait_ge(kid_ok, t - 1)
                for k in range(KD):
                    last = mm(ps[2 + t % 2][:, 0:DI + HI], hT[:, k, t * P:(t + 1) * P], wsm[:, k, 0:DI + HI],
                              start=k == 0, stop=k == KD - 1)
                last.then_inc(kiw_full, 1)
            for k in range(KD):
                mm(ps[4][0:RANK, 0:TP], wsm[:, k, DI + HI:], hT[:, k, 0:TP], start=k == 0, stop=k == KD - 1)
            for k in range(KD):
                last = mm(ps[5][0:RANK, 0:TS], wsm[:, k, DI + HI:], hT[:, k, TP:T], start=k == 0, stop=k == KD - 1)
            last.then_inc(glr_full, 1)
            pe.wait_ge(kid_ok, NT)
            for t in range(NT):
                last = tr(ps[6 + t // 4][:, (t % 4) * P:(t % 4 + 1) * P], kid[:, t, :], ident)
            last.then_inc(kidT_full, 1)

            def narrow_job(u):
                with pe.Fori(0, 2) as i:
                    for s in range(4):
                        b = 2 * (s % 2)
                        pe.wait_ge(tw_in[s], i * 16 + u * 16)
                        if s >= 2:
                            pe.wait_ge(t_free[s - 2], i + (u + 1))
                        else:
                            pe.wait_ge(t_free[s + 2], i + u)
                        for k in range(KD):
                            mm(ps[b][:, 0:TP], tw[s][:, k, :], hT[:, k, 0:TP], start=k == 0, stop=k == KD - 1)
                            last = mm(ps[b + 1][:, 0:TS], tw[s][:, k, :], hT[:, k, TP:T], start=k == 0, stop=k == KD - 1)
                        last.then_inc(t_full[s], 1)

            def merge_job(u, m):
                src = (goT, qmT, qaT)[m]
                with pe.Fori(0, 4) as i:
                    for q in range(2):
                        pe.wait_ge(m_prod[q], i + (4 * m + 1))
                        pe.wait_ge(tw_in[2 * q], i * 16 + u * 16)
                        for k in range(KD):
                            mm(ps[4 * q + 1][:, 0:TP], tw[2 * q][:, k, :], hT[:, k, 0:TP], start=k == 0, stop=k == KD - 1)
                            last = mm(ps[4 * q + 3][:, 0:TS], tw[2 * q][:, k, :], hT[:, k, TP:T],
                                      start=k == 0, stop=k == KD - 1)
                        last.then_inc(t_full[2 * q], 1)
                        pe.wait_ge(tw_in[2 * q + 1], i * 16 + u * 16)
                        for k in range(KD):
                            mm(ps[4 * q][:, 0:TP], tw[2 * q + 1][:, k, :], src[:, k, 0:TP], start=k == 0, stop=k == KD - 1)
                            last = mm(ps[4 * q + 2][:, 0:TS], tw[2 * q + 1][:, k, :], src[:, k, TP:T],
                                      start=k == 0, stop=k == KD - 1)
                        last.then_inc(t_full[2 * q + 1], 1)

            def item_transposes(n):
                kind, _, t, c = items[n]
                j = normed.index(n)
                src = {"mk": mkn[:, t % NM, c * BANK:(c + 1) * BANK], "kv": kn[:, t, :]}.get(kind, qn[j % 2])
                pe.wait_ge(qn_ok, j + 1)
                if j >= 2:
                    pe.wait_ge(qT_ok, j - 1)
                for k in range(KV if kind == "kv" else 4):
                    last = tr(ps[6 + j % 2][:, k * P:(k + 1) * P], src[:, k * P:(k + 1) * P], ident)
                last.then_inc(qT_full, 1)

            def project(kinds):
                lag = None
                for n, (kind, f, t, c) in enumerate(items):
                    if kind not in kinds:
                        continue
                    lhs, tok = (merged, t * P) if kind == "out" else (hT, t * P + T * (kind in ("mk", "mv")))
                    if f != items[n - 1][1] or n == 0:
                        pe.wait_ge(ring_in[f % 2], 16 * (f // 2 + 1))
                    if n >= 2:
                        pe.wait_ge(*item_out(n - 2))
                    for k in range(KD):
                        last = mm(ps[4 + n % 2][:, :], lhs[:, k, tok:tok + P], ring[f % 2][:, k, :],
                                  start=k == 0, stop=k == KD - 1)
                    last.then_inc(n_full, 1)
                    if lag is not None:
                        item_transposes(lag)
                    lag = n if n in normed else None
                if lag is not None:
                    item_transposes(lag)

            narrow_job(U_QI)

            pe.wait_ge(kiT_ok, 1)
            pe.wait_ge(glr_ok, 1)
            for s in (2, 3):
                pe.wait_ge(t_free[s], U_QI + 2)
            n = 0
            for t in range(1, NT):
                lo, hi = (TP, T) if t == NTP else (0, (t + 1) * P)
                for h in range(HI):
                    r = DI * (h % 2)
                    if n >= 3:
                        pe.wait_ge(rel_ok[n % 3], n // 3)
                    mm(ps[4 + n % 3][:, 0:hi - lo], qiT[r:r + DI, h // 2, t * P:(t + 1) * P], kiT[r:r + DI, lo:hi],
                       start=True, stop=True).then_inc(sc_full[n % 3], 1)
                    n += 1

            pe.wait_ge(ci_in, 16 * 2 * B)
            for g in range(4):
                if g >= 2:
                    pe.wait_ge(ciT_ok, g - 1)
                for j in range(4):
                    b, s = (4 * g + j) // PB, (4 * g + j) % PB
                    last = tr(ps[g % 2][:, j * P:(j + 1) * P], ci[:, b, s, :], ident)
                last.then_inc(ciT_full, 1)
            pe.wait_ge(wd_ok, 1)
            for g in range(4):
                if g >= 2:
                    pe.wait_ge(ciT_ok, 4 + g - 1)
                mm(ps[2 + g % 2][:, :], ones, wdiag[:, 4 * g:4 * g + 4, :], start=True, stop=True).then_inc(ciT_full, 1)
            pe.wait_ge(ciT_ok, 8)
            for b in range(B):
                if b >= 2:
                    pe.wait_ge(scs_ok, b - 1)
                for s in range(PB):
                    for par in range(2):
                        r = DI * par
                        c0 = s * HI * TB // 2
                        last = mm(ps[2 * (b % 2) + par][:, c0:c0 + HI * TB // 2], ciT[r:r + DI, b, s * P:(s + 1) * P],
                                  qiT[r:r + DI, :, TP + b * TB:TP + (b + 1) * TB], start=True, stop=True)
                last.then_inc(scs_full, 1)
            pe.wait_ge(scs_ok, B)
            for s in range(PB):
                last = tr(ps[2][:, s * P:(s + 1) * P], sT[:, s, :], ident)
            last.then_inc(scs_full, 1)
            pe.wait_ge(scs_ok, B + 1)

            narrow_job(U_QK)
            narrow_job(U_GO)
            for r in range(3):
                pe.wait_ge(rel_ok[r], (N_REL + 2 - r) // 3)
            pe.wait_ge(gain_in, 16 * N_GAINS)
            for t in range(NT):
                if t >= 2:
                    pe.wait_ge(z_ok, t - 1)
                mm(ps[6 + t % 2][:, :], glrT[0:RANK + 1, t * P:(t + 1) * P], wga[0:RANK + 1, :], start=True, stop=True)\
                    .then_inc(z_full, 1)
            project(("vg",))

            pe.wait_ge(la_ok, 1)
            pe.wait_ge(n_free_act, len(index["vg"]))
            for s in range(4):
                pe.wait_ge(t_free[s], U_GO + 2)
            pe.wait_ge(z_ok, NT)
            def decays(t):
                cum, suf = (cum_p, suf_p) if t < NTP else (cum_s, suf_s)
                if t:
                    pe.wait_ge(kdf_ok, t)
                for h in range(HG):
                    last = mm(ps[0][:, h * P:(h + 1) * P], la[:, t, h * P:(h + 1) * P], cum, start=True, stop=True)
                last.then_inc(bT_full, 1)
                mm(ps[1][:, :], suf, la[:, t, :], start=True, stop=True).then_inc(suf_full, 1)
                if t:
                    pe.wait_ge(state_ok, 2 * t + 1)
                for h in range(HG):
                    last = tr(ps[2][:, h * P:(h + 1) * P], qkT[:, HG + h, t * P:(t + 1) * P], ident)
                last.then_inc(kt_full, 1)

            def gla_transposes(t):
                pe.wait_ge(on_ok, t + 1)
                for k in range(KD):
                    last = tr(ps[6 + k // 4][:, (k % 4) * P:(k % 4 + 1) * P], on[:, k * P:(k + 1) * P], ident)
                last.then_inc(oT_full, 1)

            for t in range(NT):
                decays(t)
                if t:
                    gla_transposes(t - 1)
                pe.wait_ge(qe_ok, t + 1)
                for h in range(HG):
                    last = mm(ps[3][:, h * P:(h + 1) * P], ke[:, h, :], qe[:, h, :], start=True, stop=True)
                last.then_inc(att_full, 1)
                pe.wait_ge(attm_ok, t + 1)
                pe.wait_ge(kd_ok, t + 1)
                if t:
                    pe.wait_ge(og_ok, t)
                attm = attm_p if t < NTP else attm_s
                for h in range(HG):
                    mm(ps[4 + h][:, 0:DV], attm[:, h, :], vg[:, t, h * DV:(h + 1) * DV], start=True, stop=False)
                if t < NTP:
                    for c in range(2):
                        r = slice(c * CHUNK, (c + 1) * CHUNK)
                        pe.wait_ge(state_ok, 2 * t + c + 1)
                        for h in range(HG):
                            last = mm(ps[4 + h][r, 0:DV], qe[:, h, r], state[:, h, :], start=False, stop=True)
                        if c:
                            last.then_inc(o_full, 1)
                        for h in range(HG):
                            last = mm(ps[2 + h // 2][:, (h % 2) * DV:(h % 2 + 1) * DV], kd[r, h, :],
                                      vg[r, t, h * DV:(h + 1) * DV], start=True, stop=True)
                        last.then_inc(kv_full, 1)
                else:
                    pe.wait_ge(qem_ok, 1)
                    for b in range(B):
                        pe.wait_ge(st_in[b % 3], 16 * (b // 3 + 1))
                        for h in range(HG):
                            c0 = b * HG * P + h * P
                            last = mm(ps[4 + h][:, 0:DV], qem[:, c0:c0 + P], state_s[b % 3][:, h, :],
                                      start=False, stop=b == B - 1)
                        if b == B - 1:
                            last.then_inc(o_full, 1)
                        pe.wait_ge(kdm_ok, b + 1)
                        if b:
                            pe.wait_ge(states_ok, b)
                        for h in range(HG):
                            last = mm(ps[2 + h // 2][:, (h % 2) * DV:(h % 2 + 1) * DV], kdm[b % 2][:, h, :],
                                      vg[:, t, h * DV:(h + 1) * DV], start=True, stop=True)
                        last.then_inc(kvs_full, 1)
            gla_transposes(NT - 1)
            pe.wait_ge(og_ok, NT)
            pe.wait_ge(states_ok, B)
            merge_job(U_MERGE[0], 0)

            for q in range(2):
                pe.wait_ge(m_prod[q], 4 + 1)
            project(("mk", "mv", "qm"))
            pe.wait_ge(qT_ok, normed_before("qm"))
            pe.wait_ge(n_free_act, len(by_act))

            n = 0
            for b in range(B):
                pe.wait_ge(kvb_in[b % 3], 16 * (b // 3 + 1))
                for g in range(4):
                    if n >= 2:
                        pe.wait_ge(kmT_ok, n - 1)
                    for j in range(4):
                        k, m = 2 * g + j // 2, j % 2
                        last = tr(ps[n % 2][:, j * P:(j + 1) * P], kvb[b % 3][:, m, k * P:(k + 1) * P], ident)
                    last.then_inc(kmT_full, 1)
                    n += 1
                pe.wait_ge(kmT_ok, n)
                for m in range(NM):
                    for h in range(HM):
                        for d in range(2):
                            last = mm(ps[2 + m][:, h * TS + b * TB:h * TS + (b + 1) * TB],
                                      kmT[b % 2][:, 2 * h + d, m * P:(m + 1) * P],
                                      qmT[:, 2 * h + d, TP + b * TB:TP + (b + 1) * TB], start=d == 0, stop=d == 1)
                last.then_inc(lmT_full, 1)
            pe.wait_ge(lmT_ok, 1)

            def mem_transposes(j, t):
                pe.wait_ge(pmn_ok, j + 1)
                if j:
                    pe.wait_ge(pmT_ok, j)
                for m in range(NM):
                    for h in range(HM):
                        last = tr(ps[6 + m][:, h * P:(h + 1) * P], pm[j % 2][:, h * M + m * P:h * M + (m + 1) * P], ident)
                last.then_inc(pmT_full, 1)

            for j, t in enumerate(s_tiles):
                b = 2 * (j % 2)
                if j >= 2:
                    pe.wait_ge(pm_ok, j - 1)
                for h in range(HM):
                    dst = ps[b + h // 2][:, (h % 2) * M:(h % 2 + 1) * M]
                    if t == NTP:
                        for m in range(NM):
                            last = tr(dst[:, m * P:(m + 1) * P], lmT[:, m, h, :], ident)
                    else:
                        for d in range(2):
                            last = mm(dst, qmT[:, 2 * h + d, t * P:(t + 1) * P], mkT[:, 2 * h + d, :], start=d == 0, stop=d == 1)
                last.then_inc(lm_full, 1)
                if j:
                    mem_transposes(j - 1, s_tiles[j - 1])
            mem_transposes(NT - 1, s_tiles[-1])
            pe.wait_ge(pmT_ok, NT)
            for n in range(KD):
                h, d = n // 2, n % 2
                if n >= 4:
                    pe.wait_ge(om_ok, n - 3)
                for m in range(NM):
                    last = mm(ps[n % 4][:, :], mv[:, m, n * P:(n + 1) * P], pmT[:, m, h, 0:TP], start=m == 0, stop=m == NM - 1)
                last.then_inc(om_full, 1)
            for b in range(B):
                n = B + b
                pe.wait_ge(kvb_in[n % 3], 16 * (n // 3 + 1))
                for k in range(KD):
                    for m in range(NM):
                        last = mm(ps[4 + k // 4][:, (k % 4) * TS + b * TB:(k % 4) * TS + (b + 1) * TB],
                                  kvb[n % 3][:, m, k * P:(k + 1) * P],
                                  pmT[:, m, k // 2, TP + b * TB:TP + (b + 1) * TB], start=m == 0, stop=m == NM - 1)
                last.then_inc(mk_used, 1)
            pe.wait_ge(om_ok, KD + 2)
            merge_job(U_MERGE[1], 1)

            for q in range(2):
                pe.wait_ge(m_prod[q], 8 + 1)
            project(("kv", "qa"))
            pe.wait_ge(qT_ok, normed_before("qa"))

            pe.wait_ge(kc_in, 16 * (B + 2 * B // 3))
            for b in range(B):
                if b >= 2:
                    pe.wait_ge(kcT_ok, b - 1)
                for k in range(KV):
                    for s in range(PB):
                        last = tr(ps[b % 2][:, (k * PB + s) * P:(k * PB + s + 1) * P], kc[:, b, s, k * P:(k + 1) * P], ident)
                last.then_inc(kcT_full, 1)
            pe.wait_ge(kcT_ok, B)
            for k in range(KV):
                for s in range(PB):
                    n = k * PB + s
                    dst = ps[2 + n][:, :].rearrange("p (h t) -> p h t", h=GQ)
                    for b in range(B):
                        last = mm(dst[:, :, b * TB:(b + 1) * TB], kcT[:, b, k, s * P:(s + 1) * P],
                                  qaT[:, k * GQ:(k + 1) * GQ, TP + b * TB:TP + (b + 1) * TB], start=True, stop=True)
                    last.then_inc(lsT_full, 1)
            pe.wait_ge(lsT_ok, KV * PB)
            pe.wait_ge(vc_in, 16 * B)

            def attend_transposes(n):
                j, h = n // HA, n % HA
                t = s_tiles[j]
                nb = work_w[t] // P
                pe.wait_ge(prn_ok, n + 1)
                if n >= 3:
                    pe.wait_ge(prT_ok, n - 2)
                for s in range(nb):
                    last = tr(ps[prT_bank[n % 3]][:, s * P:(s + 1) * P], pr[n % 3][:, s * P:(s + 1) * P], ident)
                last.then_inc(prT_full, 1)

            def attend_values(n):
                if n % GQ < GQ - 1:
                    return
                t, k, w = s_tiles[n // HA], n % HA // GQ, n // GQ
                nb = work_w[t] // P
                pe.wait_ge(prT_ok, n + 1)
                if w >= 2:
                    pe.wait_ge(oa_ok, w - 1)
                dst = ps[4 + w % 2]
                pT = paT[w % 2]
                if t < NTP:
                    for s in range(nb):
                        last = mm(dst[:, :], va[:, s, k * P:(k + 1) * P], pT[:, s, :, :], start=s == 0, stop=s == nb - 1)
                else:
                    mm(dst[:, :], va[:, NTP, k * P:(k + 1) * P], pT[:, PB, :, :], start=True, stop=False)
                    out = dst[:, :].rearrange("p (h t) -> p h t", h=GQ)
                    for b in range(B):
                        for s in range(PB):
                            last = mm(out[:, :, b * TB:(b + 1) * TB], kc[:, b, s, k * P:(k + 1) * P],
                                      pT[:, s, :, b * TB:(b + 1) * TB], start=False, stop=(b, s) == (B - 1, PB - 1))
                last.then_inc(oa_full, 1)

            n = 0
            for j, t in enumerate(s_tiles):
                for h in range(HA):
                    k = h // GQ
                    dst = ps[lg_bank[n % 3]]
                    if n >= 3:
                        pe.wait_ge(lg_ok, n - 2)
                    if t < NTP:
                        last = mm(dst[:, 0:work_w[t]], qaT[:, h, t * P:(t + 1) * P], kT[:, k, 0:work_w[t]], start=True, stop=True)
                    else:
                        for s in range(PB):
                            tr(dst[:, s * P:(s + 1) * P], lsT[:, k, s, h % GQ, :], ident)
                        last = mm(dst[:, PAST:KS], qaT[:, h, TP:T], kT[:, k, TP:T], start=True, stop=True)
                    last.then_inc(lg_full, 1)
                    if n >= 3:
                        attend_values(n - 3)
                    if n >= 2:
                        attend_transposes(n - 2)
                    n += 1
            attend_transposes(n - 2)
            attend_transposes(n - 1)
            attend_values(n - 1)
            pe.wait_ge(oa_ok, NT * KV)
            merge_job(U_MERGE[2], 2)

            for q in range(2):
                pe.wait_ge(m_prod[q], 12 + 1)
            pe.wait_ge(merged_ok, 16)
            project(("out",))
            n = 0
            for t in range(NT):
                pe.wait_ge(h2_ok, t + 1)
                for h in range(2):
                    if n >= 2:
                        pe.wait_ge(h2T_ok, n - 1)
                    for k in range(4):
                        last = tr(ps[n % 2][:, k * P:(k + 1) * P], h2[:, t, (4 * h + k) * P:(4 * h + k + 1) * P], ident)
                    last.then_inc(h2T_full, 1)
                    n += 1
            pe.wait_ge(h2T_ok, 2 * NT)
            pe.wait_ge(rtw_in, 5 * 16)
            for t in range(NT):
                for k in range(KD):
                    last = mm(ps[2][:, t * NR:(t + 1) * NR], h2T[:, k, t * P:(t + 1) * P], w_rt[:, k, :],
                              start=k == 0, stop=k == KD - 1)
            last.then_inc(rt_full, 1)
            pe.wait_ge(rt_step, 2)
            for t in range(NT):
                for s in range(t + 1):
                    mm(ps[3][:, t * NE:(t + 1) * NE], before if s == t else ones, hot_both[:, s, :], start=s == 0, stop=s == t)
            for s in range(NT):
                last = mm(ps[3][:, NT * NE:(NT + 1) * NE], ones, hot_both[:, s, :], start=s == 0, stop=s == NT - 1)
            last.then_inc(rank_full, 1)
            pe.wait_ge(pos_ok, 1)

            def wait(signal, value):
                if value is not None:
                    pe.wait_ge(signal, value)

            def rows_transposed(n, row_value, cnt):
                wait(hsT_ok, cnt(-1))
                pe.wait_ge(row_in[n % NES], row_value)
                pe.sem_inc(pe_seen, 1)
                for k in range(KD):
                    last = tr(ps[0][:, k * CAP:(k + 1) * CAP], hs[n % NES][0:CAP, k * P:(k + 1) * P], ident[0:CAP, 0:CAP])
                last.then_inc(hsT_full, 1)

            def gate_up(n, w_value, cnt):
                wait(hid_ok, cnt(-2))
                pe.wait_ge(ew_in[n % NES], w_value)
                pe.wait_ge(hsT_ok, cnt(0))
                for g, w in enumerate((ew_gate[n % NES], ew_up[n % NES])):
                    for f in range(DF // P):
                        c0 = (g * (DF // P) + f) * CAP
                        for k in range(KD):
                            last = mm(ps[1 + 2 * (n % 2)][:, c0:c0 + CAP], w[:, k, f * P:(f + 1) * P], hsT[n % 2][:, k, :],
                                      start=k == 0, stop=k == KD - 1)
                last.then_inc(gu_full, 1)

            def down(n, cnt):
                wait(oTs_ok, cnt(-1))
                pe.wait_ge(hid_ok, cnt(0))
                for k in range(KD):
                    for f in range(DF // P):
                        last = mm(ps[2][:, k * CAP:(k + 1) * CAP], ew_down[n % NES][:, f, k * P:(k + 1) * P],
                                  hid[n % 2][:, f * CAP:(f + 1) * CAP], start=f == 0, stop=f == DF // P - 1)
                last.then_inc(dn_full, 1)

            def outputs_transposed(n, cnt):
                wait(ysl_ok, cnt(-2))
                pe.wait_ge(oTs_ok, cnt(0))
                pe.sem_inc(pe_seen, 1)
                for k in range(KD):
                    last = tr(ps[4 + 2 * (n % 2) + k // 4][0:CAP, (k % 4) * P:(k % 4 + 1) * P], oT[n % 2][:, k, :], ident)
                last.then_inc(y_full, 1)

            def group(i):
                fixed = isinstance(i, int)
                for s in range(NES):
                    def count(n, s=s):
                        def cnt(x):
                            if fixed:
                                return i * NES + s + n + x + 1 if i * NES + s + n + x >= 0 else None
                            return i * NES + (s + n + x + 1)
                        return cnt
                    if not (fixed and i == NE // NES - 1 and s == NES - 1):
                        nxt = s + 1
                        turn = i * 16 + (ROWS_IN + 16 + 16 * (nxt // NES))
                        rows_transposed(nxt, turn, count(1))
                    gate_up(s, i * 48 + 48, count(0))
                    if not (fixed and i * NES + s < 2):
                        outputs_transposed(s - 2, count(-2))
                    if not (fixed and i * NES + s < 1):
                        down((s - 1) % NES, count(-1))

            rows_transposed(0, ROWS_IN + 16, lambda x: x + 1 if x >= 0 else None)
            group(0)
            with pe.Fori(1, NE // NES - 1) as i:
                group(i)
            group(NE // NES - 1)
            after = lambda n: lambda x: n + x + 1
            outputs_transposed(NE - 2, after(NE - 2))
            down(NE - 1, after(NE - 1))
            outputs_transposed(NE - 1, after(NE - 1))

            over = pe.value_load(rti[0:1, N_OVER:N_OVER + 1], min_val=0, max_val=N_OVER)
            pe.wait_ge(ysl_ok, NE)
            with pe.If(over > 0):
                with pe.Fori(0, N_OVER) as i:
                    cnt = lambda x: i + (NE + 1 + x)
                    pe.wait_ge(ysl_ok, i + NE)
                    rows_transposed(0, i * 16 + (ROWS_IN + 16 * NE // NES + 16), cnt)
                    gate_up(0, i * 48 + (48 * NE // NES + 48), cnt)
                    down(0, cnt)
                    outputs_transposed(0, cnt)
        @block.scalar
        def _(act):
            go = nc.scalar.activation
            junk = cut(region_m, 0, D)

            for s in range(4):
                act.sem_inc(t_free[s], 1)

            for t in range(NT + NM):
                act.wait_ge(x_in[min(t, 2)], 16 if t < 2 else 16 * (NT + NM - 2))
                if t:
                    act.wait_ge(ss_ok, t)
                go(junk, xt[:, t, :], ACT.Square, accum_out=ss0[:, t:t + 1]).then_inc(ss_ok, 1)
            for n in range(2 * (NT + NM)):
                act.wait_ge(xT_full, n + 1)
                t, h = n // 2, n % 2
                go(hT[:, 4 * h:4 * h + 4, t * P:(t + 1) * P], ps[n % 2][:, :].rearrange("p (k t) -> p k t", k=4),
                   ACT.Copy).then_inc(hT_ok, 1)
            for t in range(NT):
                act.wait_ge(kiw_full, t + 1)
                if t:
                    act.wait_ge(kiss_ok, t)
                go(junk[:, 0:DI], ps[2 + t % 2][:, 0:DI], ACT.Square, accum_out=ssk[:, t:t + 1]).then_inc(kiss_ok, 1)
            act.wait_ge(glr_full, 1)
            act.wait_ge(zero_ok, 1)
            go(glrT[0:RANK, 0:TP], ps[4][0:RANK, 0:TP], ACT.Copy)
            go(glrT[0:RANK, TP:T], ps[5][0:RANK, 0:TS], ACT.Copy).then_inc(glr_ok, 1)
            act.wait_ge(kidT_full, 1)
            go(kiT[:, 0:TP], ps[6][:, :], ACT.Copy)
            go(kiT[:, TP:T], ps[7][:, 0:TS], ACT.Copy).then_inc(kiT_ok, 1)

            def narrow_out(dst, func, u):
                with act.Fori(0, 2) as i:
                    for s in range(4):
                        b = 2 * (s % 2)
                        act.wait_ge(t_full[s], i + (u + 1))
                        go(dst[:, bass.ds(i * 4 + s, 1), 0:TP], ps[b][:, 0:TP].unsqueeze(1), func)
                        go(dst[:, bass.ds(i * 4 + s, 1), TP:T], ps[b + 1][:, 0:TS].unsqueeze(1), func).then_inc(t_free[s], 1)

            def gates(u, m):
                with act.Fori(0, 4) as i:
                    for q in range(2):
                        act.wait_ge(m_prod[q], i + (4 * m + 1))
                        act.wait_ge(t_full[2 * q], i + (u + 1))
                        go(sg[q][:, 0:TP], ps[4 * q + 1][:, 0:TP], ACT.Sigmoid)
                        go(sg[q][:, TP:T], ps[4 * q + 3][:, 0:TS], ACT.Sigmoid).then_inc(sg_ok[q], 1)

            def item_transposed(n):
                kind, _, t, c = items[n]
                j = normed.index(n)
                act.wait_ge(qT_full, j + 1)
                src = ps[6 + j % 2][:, :].rearrange("p (k t) -> p k t", t=P)
                tok = slice(t * P, (t + 1) * P)
                if kind == "mk":
                    last = go(mkT[:, 4 * c:4 * c + 4, tok], src, ACT.Copy)
                elif kind == "kv":
                    last = go(kT[:, :, tok], src[:, 0:KV, :], ACT.Copy)
                elif kind == "qa":
                    last = go(qaT[:, 4 * c:4 * c + 4, tok], src, ACT.Copy, scale=gcol_q)
                else:
                    for d in range(2):
                        last = go(qmT[:, 4 * c + d:4 * c + 4:2, tok], src[:, d::2, :], ACT.Copy, scale=gcol_qm[:, d:d + 1])
                last.then_inc(qT_ok, 1)

            def project_out(kinds):
                lag = None
                for n, (kind, f, t, c) in enumerate(items):
                    if kind not in kinds:
                        continue
                    act.wait_ge(n_full, n + 1)
                    src = ps[4 + n % 2]
                    if n in by_act:
                        dst = (vg if kind == "vg" else mv)[:, t, c * BANK:(c + 1) * BANK]
                        go(dst, src[:, :], ACT.Copy).then_inc(n_free_act, 1)
                    else:
                        j = normed.index(n)
                        if j >= 2:
                            act.wait_ge(qn_ok, j - 1)
                        if kind == "kv":
                            go(va[:, t, :], src[:, KV * HD:], ACT.Copy)
                        w = KV * HD if kind == "kv" else BANK
                        go(sq[j % 2][:, 0:w], src[:, 0:w], ACT.Square).then_inc(sq_ok, 1)
                    if lag is not None:
                        item_transposed(lag)
                    lag = n if n in normed else None
                if lag is not None:
                    item_transposed(lag)

            narrow_out(qiT, ACT.Copy, U_QI)
            n = 0
            for t in range(1, NT):
                w = TS if t == NTP else (t + 1) * P
                for h in range(HI):
                    act.wait_ge(sc_full[n % 3], n // 3 + 1)
                    if n >= 3:
                        act.wait_ge(acc_ok, n - 2)
                    go(rel[n % 3][:, 0:w], ps[4 + n % 3][:, 0:w], ACT.Relu).then_inc(rel_ok[n % 3], 1)
                    n += 1
            for g in range(4):
                act.wait_ge(ciT_full, g + 1)
                go(ciT[:, 2 * g:2 * g + 2, :], ps[g % 2][:, :].rearrange("p (b s) -> p b s", b=2), ACT.Copy).then_inc(ciT_ok, 1)
            for g in range(4):
                act.wait_ge(ciT_full, 4 + g + 1)
                go(wB[:, 4 * g:4 * g + 4, :], ps[2 + g % 2][:, :].rearrange("p (h t) -> p h t", h=4), ACT.Copy).then_inc(ciT_ok, 1)

            narrow_out(qkT, ACT.Copy, U_QK)
            narrow_out(goT, ACT.Silu, U_GO)
            act.wait_ge(z_ok, NT)
            go(zabs, zabs, ACT.Exp, scale=-1.0).then_inc(act_step, 1)
            act.wait_ge(act_step, 1)
            go(zabs, zabs, ACT.Ln, bias=1.0).then_inc(act_step, 1)
            project_out(("vg",))

            act.wait_ge(fill_ok, 16)
            for t in range(NT):
                act.wait_ge(bT_full, t + 1)
                if t:
                    act.wait_ge(attm_ok, t)
                go(eb, ps[0][:, :].rearrange("p (h t) -> p h t", h=HG), ACT.Exp)
                go(enb, ps[0][:, :].rearrange("p (h t) -> p h t", h=HG), ACT.Exp, scale=-1.0).then_inc(eb_ok, 1)
                act.wait_ge(suf_full, t + 1)
                go(kdf, ps[1][:, :].rearrange("p (h t) -> p h t", h=HG), ACT.Exp).then_inc(kdf_ok, 1)
                if t == NTP:
                    act.wait_ge(kd_ok, NT)
                    for b in range(B):
                        if b >= 2:
                            act.wait_ge(kvs_full, b - 1)
                        go(kdm[b % 2], kd, ACT.Copy, scale=bsel[:, b:b + 1]).then_inc(kdm_ok, 1)
                act.wait_ge(o_full, t + 1)
                if t:
                    act.wait_ge(on_ok, t)
                for h in range(HG):
                    last = go(mix[:, h * DV:(h + 1) * DV], ps[4 + h][:, 0:DV], ACT.Square, accum_out=sso[:, h:h + 1])
                last.then_inc(oss_ok, 1)
            gates(U_MERGE[0], 0)

            for q in range(2):
                act.wait_ge(m_prod[q], 4 + 1)
            project_out(("mk", "mv", "qm"))
            n = 0
            for b in range(B):
                if b >= 2:
                    act.wait_ge(lmT_full, b - 1)
                for g in range(4):
                    act.wait_ge(kmT_full, n + 1)
                    go(kmT[b % 2][:, 2 * g:2 * g + 2, :], ps[n % 2][:, :].rearrange("p (k m) -> p k m", k=2), ACT.Copy)\
                        .then_inc(kmT_ok, 1)
                    n += 1
            act.wait_ge(lmT_full, B)
            for m in range(NM):
                last = go(lmT[:, m, :, :], ps[2 + m][:, :].rearrange("p (h t) -> p h t", h=HM), ACT.Copy)
            last.then_inc(lmT_ok, 1)
            act.wait_ge(mem_out, 48)

            def mem_transposed(j, t):
                act.wait_ge(pmT_full, j + 1)
                for m in range(NM):
                    last = go(pmT[:, m, :, t * P:(t + 1) * P], ps[6 + m][:, :].rearrange("p (h t) -> p h t", h=HM), ACT.Copy)
                last.then_inc(pmT_ok, 1)

            for j, t in enumerate(s_tiles):
                b = 2 * (j % 2)
                act.wait_ge(mmx_ok, j + 1)
                if j >= 2:
                    act.wait_ge(pmT_full, j - 1)
                for h in range(HM):
                    last = go(pm[j % 2][:, h * M:(h + 1) * M], ps[b + h // 2][:, (h % 2) * M:(h % 2 + 1) * M], ACT.Exp,
                              bias=nmx[:, h:h + 1], scale=HDM ** -0.5, accum_out=sm[:, 4 * (j % 2) + h:4 * (j % 2) + h + 1])
                last.then_inc(pm_ok, 1)
                if j:
                    mem_transposed(j - 1, s_tiles[j - 1])
            mem_transposed(NT - 1, s_tiles[-1])
            for n in range(KD):
                act.wait_ge(om_full, n + 1)
                go(qmT[:, n, 0:TP], ps[n % 4][:, :], ACT.Copy).then_inc(om_ok, 1)
            act.wait_ge(mk_used, B)
            for g in range(2):
                go(qmT[:, 4 * g:4 * g + 4, TP:T], ps[4 + g][:, :].rearrange("p (k t) -> p k t", k=4), ACT.Copy).then_inc(om_ok, 1)
            gates(U_MERGE[1], 1)

            for q in range(2):
                act.wait_ge(m_prod[q], 8 + 1)
            project_out(("kv", "qa"))
            for b in range(B):
                act.wait_ge(kcT_full, b + 1)
                go(kcT[:, b, :, :], ps[b % 2][:, :].rearrange("p (k s) -> p k s", k=KV), ACT.Copy).then_inc(kcT_ok, 1)
            for n in range(KV * PB):
                act.wait_ge(lsT_full, n + 1)
                go(lsT[:, n // PB, n % PB, :, :], ps[2 + n][:, :].rearrange("p (h t) -> p h t", h=GQ), ACT.Copy)\
                    .then_inc(lsT_ok, 1)

            def attend_transposed(n):
                nb, w = work_w[s_tiles[n // HA]] // P, n // GQ
                act.wait_ge(prT_full, n + 1)
                if w >= 2:
                    act.wait_ge(oa_full, w - 1)
                go(paT[w % 2][:, 0:nb, n % GQ, :], ps[prT_bank[n % 3]][:, 0:nb * P].rearrange("p (s t) -> p s t", t=P), ACT.Copy)\
                    .then_inc(prT_ok, 1)

            for n in range(NT * HA):
                w = work_w[s_tiles[n // HA]]
                act.wait_ge(lg_ok, n + 1)
                if n >= 3:
                    act.wait_ge(prT_full, n - 2)
                go(pr[n % 3][:, 0:w], lg[n % 3][:, 0:w], ACT.Exp, bias=nmx[:, n % 4:n % 4 + 1], scale=HD ** -0.5,
                   accum_out=sm[:, n % 4:n % 4 + 1]).then_inc(pr_ok, 1)
                if n >= 2:
                    attend_transposed(n - 2)
            for n in (NT * HA - 2, NT * HA - 1):
                attend_transposed(n)
            gates(U_MERGE[2], 2)

            act.wait_ge(x1_ok, 2 * NT)
            for t in range(NT):
                go(h2[:, t, :], x1[:, t, :], ACT.Square, accum_out=ssf[:, t:t + 1]).then_inc(ssf_ok, 1)
            n = 0
            for t in range(NT):
                for h in range(2):
                    act.wait_ge(h2T_full, n + 1)
                    go(h2T[:, 4 * h:4 * h + 4, t * P:(t + 1) * P], ps[n % 2][:, :].rearrange("p (k t) -> p k t", k=4),
                       ACT.Copy).then_inc(h2T_ok, 1)
                    n += 1
            act.wait_ge(rt_step, 1)
            go(ge5, gs5, ACT.Exp).then_inc(act_step, 1)
            act.wait_ge(rt_step, 3)
            go(rs5[7], rs5[6], ACT.Exp).then_inc(act_step, 1)

            def rows_out(n, at):
                act.wait_ge(hsT_full, at)
                go(hsT[n % 2], ps[0][:, :].rearrange("p (k t) -> p k t", k=KD), ACT.Copy).then_inc(hsT_ok, 1)

            def silu(n, at):
                act.wait_ge(gu_full, at)
                go(act_g[n % 2], ps[1 + 2 * (n % 2)][:, 0:DF // P * CAP], ACT.Silu).then_inc(silu_ok, 1)

            def outputs_out(n, at, y_at):
                if y_at is not None:
                    act.wait_ge(y_full, y_at)
                act.wait_ge(dn_full, at)
                go(oT[n % 2], ps[2][:, :].rearrange("p (k t) -> p k t", k=KD), ACT.Copy).then_inc(oTs_ok, 1)

            def group(i):
                fixed = isinstance(i, int)
                for s in range(NES):
                    if not (fixed and i == NE // NES - 1 and s == NES - 1):
                        rows_out(s + 1, i * NES + (s + 2))
                    silu(s, i * NES + (s + 1))
                    if not (fixed and i * NES + s < 1):
                        outputs_out(s - 1, i * NES + s, None if fixed and i * NES + s < 3 else i * NES + (s - 2))

            rows_out(0, 1)
            group(0)
            with act.Fori(1, NE // NES - 1) as i:
                group(i)
            group(NE // NES - 1)
            outputs_out(NE - 1, NE, NE - 2)
            over = act.value_load(rti[0:1, N_OVER:N_OVER + 1], min_val=0, max_val=N_OVER)
            with act.If(over > 0):
                with act.Fori(0, N_OVER) as i:
                    rows_out(0, i + (NE + 1))
                    silu(0, i + (NE + 1))
                    outputs_out(0, i + (NE + 1), i + NE)
        @block.vector
        def _(dve):
            v = nc.vector
            steps = [0]

            def link(ins):
                steps[0] += 1
                ins.then_inc(dve_step, 1)
                dve.wait_ge(dve_step, steps[0])

            def rstd(out, total, width):
                x, y, w = total, out, newton[:, 0:out.shape[1]]
                link(v.tensor_scalar(x, x, 1.0 / width, EPS, ALU.mult, ALU.add))
                link(v.tensor_scalar(y.bitcast(I32), x.bitcast(I32), 1, None, ALU.logical_shift_right))
                link(v.tensor_scalar(y.bitcast(I32), y.bitcast(I32), -1.0, float(0x5f3759df), ALU.mult, ALU.add))
                for _ in range(3):
                    link(v.scalar_tensor_tensor(w, y, -0.5, y, ALU.mult, ALU.mult))
                    link(v.tensor_tensor(w, w, x, ALU.mult))
                    link(v.scalar_tensor_tensor(y, w, 1.5, y, ALU.add, ALU.mult))

            for q in range(2):
                dve.sem_inc(m_prod[q], 1)

            dve.wait_ge(g_norm_in, 32)
            for t in range(NT + NM):
                if t in (0, 2):
                    t1 = 2 if t == 0 else NT + NM
                    dve.wait_ge(ss_ok, t1)
                    rstd(rs0[:, t:t1], ss0[:, t:t1], D)
                v.scalar_tensor_tensor(xt[:, t, :], xt[:, t, :], rs0[:, t:t + 1], g_x if t < NT else g_mem,
                                       ALU.mult, ALU.mult).then_inc(xn_ok, 1)
            dve.wait_ge(xn_ok, NT + NM)
            v.memset(glrT[0:32, :], 1.0).then_inc(zero_ok, 1)

            dve.wait_ge(gain_in, 16 * N_GAINS)
            for t in range(NT):
                dve.wait_ge(kiss_ok, t + 1)
                rstd(rsk[:, t:t + 1], ssk[:, t:t + 1], DI)
                src = ps[2 + t % 2]
                for r in range(2):
                    v.scalar_tensor_tensor(kid[:, t, r * DI:(r + 1) * DI], src[:, 0:DI], rsk[:, t:t + 1], g_ki[:, 0:DI],
                                           ALU.mult, ALU.mult)
                v.tensor_scalar(wi[:, t, :], src[:, DI:DI + HI], HI ** -0.5 * DI ** -0.5, None, ALU.mult).then_inc(kid_ok, 1)
            dve.wait_ge(kid_ok, NT)
            dve.wait_ge(hT_ok, 2 * (NT + NM))
            dve.wait_ge(const_ok, N_CONST)
            for par in range(2):
                n8 = HI // 2
                last = v.tensor_tensor(wdiag[:, par * n8:(par + 1) * n8, :], ident.unsqueeze(1).to_broadcast([P, n8, P]),
                                       wi[:, NTP, par::2].unsqueeze(2).to_broadcast([P, n8, P]), ALU.mult)
            last.then_inc(wd_ok, 1)

            n = 0
            for t in range(1, NT):
                dst = work[t][:, PAST:KS] if t == NTP else work[t]
                w = TS if t == NTP else (t + 1) * P
                for h in range(HI):
                    dve.wait_ge(rel_ok[n % 3], n // 3 + 1)
                    if h == 0:
                        v.tensor_scalar(dst, rel[n % 3][:, 0:w], wi[:, t, 0:1], None, ALU.mult).then_inc(acc_ok, 1)
                    else:
                        dve.wait_ge(acc_ok, n)
                        v.scalar_tensor_tensor(dst, rel[n % 3][:, 0:w], wi[:, t, h:h + 1], dst, ALU.mult, ALU.add)\
                            .then_inc(acc_ok, 1)
                    n += 1
            dve.wait_ge(ciT_ok, 8)
            for b in range(B):
                dve.wait_ge(scs_full, b + 1)
                if b:
                    dve.wait_ge(scs_ok, b)
                for s in range(PB):
                    for par in range(2):
                        h8 = slice(par * HI // 2, (par + 1) * HI // 2)
                        src = ps[2 * (b % 2) + par][:, s * HI * TB // 2:(s + 1) * HI * TB // 2]
                        last = v.scalar_tensor_tensor(sct[s].rearrange("p (h t) -> p h t", h=HI)[:, h8, :],
                                                      src.rearrange("p (h t) -> p h t", t=TB),
                                                      0.0, wB[:, h8, b * TB:(b + 1) * TB], ALU.max, ALU.mult)
                link(last)
                for s in range(PB):
                    last = v.tensor_reduce(sT[:, s, b * TB:(b + 1) * TB], sct[s].rearrange("p (h t) -> p t h", h=HI), AX_X, ALU.add)
                last.then_inc(scs_ok, 1)
            dve.wait_ge(scs_full, B + 1)
            v.tensor_copy(work[NTP][:, 0:PAST], ps[2][:, 0:PAST]).then_inc(scs_ok, 1)

            dve.wait_ge(acc_ok, n)
            link(v.memset(work[0], 0.0))
            for t in range(NTP):
                v.memset(work[t][0:CHUNK, t * P + CHUNK:(t + 1) * P], NEG)
            link(v.tensor_tensor(work[NTP][:, PAST:KS], work[NTP][:, PAST:KS], other, ALU.add))
            dve.wait_ge(scs_ok, B + 1)

            for t in range(1, NT):
                left = TOPK_S if t == NTP else TOPK_P
                while left > 0:
                    link(v.max(top8, work[t]))
                    if left < 8:
                        link(v.memset(top8[:, left:8], TAKEN))
                    link(v.match_replace(work[t], top8, work[t], TAKEN))
                    left -= 8
                link(v.tensor_scalar(work[t], work[t], TAKEN / 2, NEG, ALU.is_gt, ALU.mult))

            for t in range(NT):
                dve.wait_ge(z_full, t + 1)
                link(v.tensor_scalar(la[:, t, :], ps[6 + t % 2][:, :], 0.0, None, ALU.min))
                v.scalar_tensor_tensor(zabs[:, t, :], la[:, t, :], -2.0, ps[6 + t % 2][:, :], ALU.mult, ALU.add)\
                    .then_inc(z_ok, 1)
            dve.wait_ge(act_step, 2)
            v.tensor_tensor(la, la, zabs, ALU.subtract).then_inc(la_ok, 1)
            dve.wait_ge(la_ok, 1)
            v.memset(state, 0.0).then_inc(state_ok, 1)

            def gla_gated(t):
                dve.wait_ge(oT_full, t + 1)
                for g in range(2):
                    for d in range(2):
                        dst = goT[:, 4 * g + d:4 * g + 4:2, t * P:(t + 1) * P]
                        last = v.scalar_tensor_tensor(dst, ps[6 + g][:, :].rearrange("p (k t) -> p k t", k=4)[:, d::2, :],
                                                      gcol_o[:, d:d + 1], dst, ALU.mult, ALU.mult)
                last.then_inc(og_ok, 1)

            dve.wait_ge(pool_step, 3)
            dve.wait_ge(early_out, 32)
            for t in range(NT):
                tok = slice(t * P, (t + 1) * P)
                cum, attm = (cum_p, attm_p) if t < NTP else (cum_s, attm_s)
                dve.wait_ge(eb_ok, t + 1)
                if t < NTP:
                    v.tensor_copy(dec[:, :, 0:2], eb[:, :, CHUNK - 1::CHUNK])
                else:
                    v.tensor_copy(dec[:, :, 0:B], eb[:, :, TB - 1::TB])
                v.scalar_tensor_tensor(qe, qkT[:, 0:HG, tok], DK ** -0.5, eb, ALU.mult, ALU.mult)
                v.tensor_tensor(ke, qkT[:, HG:2 * HG, tok], enb, ALU.mult).then_inc(qe_ok, 1)
                if t == NTP:
                    dve.wait_ge(qe_ok, t + 1)
                    diag = qem.rearrange("p (b x) -> p b x", b=B)[:, :, 0:HG * P].rearrange("p b (h c) -> p h b c", h=HG)
                    v.tensor_copy(diag[:, :, :, 0:TB], qe.rearrange("p h (b c) -> p h b c", b=B)).then_inc(qem_ok, 1)
                dve.wait_ge(kdf_ok, t + 1)
                dve.wait_ge(kt_full, t + 1)
                v.tensor_tensor(kd, ps[2][:, :].rearrange("p (h t) -> p h t", h=HG), kdf, ALU.mult).then_inc(kd_ok, 1)
                if t:
                    gla_gated(t - 1)
                dve.wait_ge(att_full, t + 1)
                v.copy_predicated(attm, cum.bitcast(U32).unsqueeze(1).to_broadcast([P, HG, P]),
                                  ps[3][:, :].rearrange("p (h t) -> p h t", h=HG)).then_inc(attm_ok, 1)
                if t < NTP:
                    dve.wait_ge(qe_ok, t + 1)
                    for c in range(2):
                        dve.wait_ge(kv_full, 2 * t + c + 1)
                        dve.wait_ge(state_ok, 2 * t + c + 1)
                        for h in range(HG):
                            last = v.scalar_tensor_tensor(state[:, h, :], state[:, h, :], dec[:, h, c:c + 1],
                                                          ps[2 + h // 2][:, (h % 2) * DV:(h % 2 + 1) * DV], ALU.mult, ALU.add)
                        last.then_inc(state_ok, 1)
                else:
                    for b in range(B):
                        dve.wait_ge(kvs_full, b + 1)
                        for h in range(HG):
                            last = v.scalar_tensor_tensor(state_s[b % 3][:, h, :], state_s[b % 3][:, h, :], dec[:, h, b:b + 1],
                                                          ps[2 + h // 2][:, (h % 2) * DV:(h % 2 + 1) * DV], ALU.mult, ALU.add)
                        last.then_inc(states_ok, 1)
                dve.wait_ge(oss_ok, t + 1)
                rstd(rso[:, 0:HG], sso[:, 0:HG], DV)
                for h in range(HG):
                    last = v.tensor_scalar(on[:, h * DV:(h + 1) * DV], ps[4 + h][:, 0:DV], rso[:, h:h + 1], None, ALU.mult)
                last.then_inc(on_ok, 1)
            gla_gated(NT - 1)

            def merge(u, m):
                with dve.Fori(0, 4) as i:
                    for q in range(2):
                        dve.wait_ge(sg_ok[q], i + (4 * m + 1))
                        dve.wait_ge(t_full[2 * q + 1], i + (u + 1))
                        sum_ = merged[:, bass.ds(i * 2 + q, 1), :]
                        dst = prod[q].unsqueeze(1) if m else sum_
                        v.tensor_tensor(dst[:, :, 0:TP], sg[q][:, 0:TP].unsqueeze(1), ps[4 * q][:, 0:TP].unsqueeze(1), ALU.mult)
                        v.tensor_tensor(dst[:, :, TP:T], sg[q][:, TP:T].unsqueeze(1), ps[4 * q + 2][:, 0:TS].unsqueeze(1), ALU.mult)\
                            .then_inc(m_prod[q], 1)
                        if m:
                            dve.wait_ge(m_prod[q], i + (4 * m + 2))
                            v.tensor_tensor(sum_, sum_, prod[q].unsqueeze(1), ALU.add).then_inc(merged_ok, 1)

            for n in range(3):
                dve.wait_ge(st_out[n], 16 * ((B + 2 - n) // 3))
            dve.wait_ge(early_out, 48)
            merge(U_MERGE[0], 0)

            def project_norm(kinds):
                for n in normed:
                    kind, f, t, c = items[n]
                    if kind not in kinds:
                        continue
                    j = normed.index(n)
                    hd = HDM if kind in ("mk", "qm") else HD
                    w = KV * HD if kind == "kv" else BANK
                    nh = w // hd
                    dve.wait_ge(sq_ok, j + 1)
                    link(v.tensor_reduce(ssn[:, 0:nh], sq[j % 2][:, 0:w].rearrange("p (h d) -> p h d", d=hd), AX_X, ALU.add))
                    rstd(rsn[:, 0:nh], ssn[:, 0:nh], hd)
                    if j >= 2:
                        dve.wait_ge(qT_full, j - 1)
                    q3 = qn[j % 2][:, 0:w].rearrange("p (h d) -> p h d", d=hd)
                    x = v.tensor_tensor(q3, ps[4 + n % 2][:, 0:w].rearrange("p (h d) -> p h d", d=hd),
                                        rsn[:, 0:nh].unsqueeze(2).to_broadcast([P, nh, hd]), ALU.mult)
                    if kind in ("qm", "qa"):
                        x.then_inc(qn_ok, 1)
                        continue
                    link(x)
                    dst, g = (mkn[:, t, c * BANK:(c + 1) * BANK], g_mk) if kind == "mk" else (kn[:, t, :], g_ka)
                    v.tensor_tensor(dst.rearrange("p (h d) -> p h d", d=hd), q3, g[:, 0:hd].unsqueeze(1).to_broadcast([P, nh, hd]),
                                    ALU.mult).then_inc(qn_ok, 1)

            project_norm(("mk", "qm"))

            def mem_max(j):
                dve.wait_ge(lm_full, j + 1)
                if j:
                    dve.wait_ge(pm_ok, j)
                for g in range(2):
                    last = v.tensor_reduce(mx[:, 2 * g:2 * g + 2], ps[2 * (j % 2) + g][:, :].rearrange("p (h m) -> p h m", h=2),
                                           AX_X, ALU.max)
                link(last)
                v.tensor_scalar(nmx[:, 0:HM], mx[:, 0:HM], -HDM ** -0.5, None, ALU.mult).then_inc(mmx_ok, 1)

            mem_max(0)
            for j in range(NT):
                if j + 1 < NT:
                    mem_max(j + 1)
                dve.wait_ge(pm_ok, j + 1)
                r = 4 * (j % 2)
                link(v.reciprocal(rsm[:, r:r + HM], sm[:, r:r + HM]))
                for h in range(HM):
                    last = v.tensor_scalar(pm[j % 2][:, h * M:(h + 1) * M], pm[j % 2][:, h * M:(h + 1) * M],
                                           rsm[:, r + h:r + h + 1], None, ALU.mult)
                last.then_inc(pmn_ok, 1)
            merge(U_MERGE[1], 1)

            project_norm(("kv", "qa"))

            def attend_max(n):
                t = s_tiles[n // HA]
                dve.wait_ge(lg_full, n + 1)
                if n >= 3:
                    dve.wait_ge(pr_ok, n - 2)
                link(v.tensor_tensor_reduce(lg[n % 3][:, 0:work_w[t]], ps[lg_bank[n % 3]][:, 0:work_w[t]], work[t], 1.0, TAKEN,
                                            ALU.add, ALU.max, mx[:, n % 4:n % 4 + 1]))
                v.tensor_scalar(nmx[:, n % 4:n % 4 + 1], mx[:, n % 4:n % 4 + 1], -HD ** -0.5, None, ALU.mult).then_inc(lg_ok, 1)

            def attend_out(w):
                t, k = s_tiles[w // KV], w % KV
                dve.wait_ge(oa_full, w + 1)
                v.tensor_copy(qaT[:, k * GQ:(k + 1) * GQ, t * P:(t + 1) * P], ps[4 + w % 2][:, :].rearrange("p (h t) -> p h t", h=GQ))\
                    .then_inc(oa_ok, 1)

            attend_max(0)
            for n in range(NT * HA):
                w = work_w[s_tiles[n // HA]]
                if n + 1 < NT * HA:
                    attend_max(n + 1)
                dve.wait_ge(pr_ok, n + 1)
                link(v.reciprocal(rsm[:, n % 4:n % 4 + 1], sm[:, n % 4:n % 4 + 1]))
                v.tensor_scalar(pr[n % 3][:, 0:w], pr[n % 3][:, 0:w], rsm[:, n % 4:n % 4 + 1], None, ALU.mult).then_inc(prn_ok, 1)
                if n >= GQ and n % GQ == 2:
                    attend_out(n // GQ - 1)
            attend_out(NT * KV - 1)
            merge(U_MERGE[2], 2)

            dve.wait_ge(kv_out, 64)
            dve.wait_ge(xr_in, 64)
            for n in index["out"]:
                _, f, t, c = items[n]
                dve.wait_ge(n_full, n + 1)
                v.tensor_tensor(x1[:, t, c * BANK:(c + 1) * BANK], ps[4 + n % 2][:, :], xr[:, t, c * BANK:(c + 1) * BANK], ALU.add)\
                    .then_inc(x1_ok, 1)
            dve.wait_ge(rtw_in, 80)
            dve.wait_ge(ssf_ok, NT)
            rstd(rsf[:, 0:NT], ssf[:, 0:NT], D)
            for t in range(NT):
                v.scalar_tensor_tensor(h2[:, t, :], x1[:, t, :], rsf[:, t:t + 1], g_ffn, ALU.mult, ALU.mult).then_inc(h2_ok, 1)

            def per(x, w):
                return x.unsqueeze(2).to_broadcast([P, NT, w])

            def first_index(out, x, top, w):
                c = r_tmp[:, :, 0:w]
                link(v.tensor_tensor(c, x, per(top, w), ALU.not_equal))
                link(v.scalar_tensor_tensor(c, c, 1000.0, iota_e[:, :, 0:w], ALU.mult, ALU.add))
                link(v.tensor_reduce(out, c, AX_X, ALU.min))

            dve.wait_ge(rt_full, 1)
            link(v.tensor_tensor(lt, ps[2][:, 0:NT * NR].rearrange("p (t c) -> p t c", t=NT),
                                 b_rt.unsqueeze(1).to_broadcast([P, NT, NR]), ALU.add))
            gmax, gsum, gw, gidx, m1, m2, dm, e2, i1, i2, den, rden, w0, w1, p0, p1 = rs5[0:16]
            link(v.tensor_reduce(gmax, lt[:, :, 0:NG], AX_X, ALU.max))
            v.tensor_tensor(gs5, lt[:, :, 0:NG], per(gmax, NG), ALU.subtract).then_inc(rt_step, 1)
            dve.wait_ge(pool_step, 3 + N_TABLES)
            first_index(gidx, lt[:, :, 0:NG], gmax, NG)
            link(v.tensor_tensor(r_tmp, iota_g, per(gidx, NE), ALU.not_equal))
            link(v.scalar_tensor_tensor(elm, r_tmp, NEG, lt[:, :, NG:NR], ALU.mult, ALU.add))
            link(v.tensor_reduce(m1, elm, AX_X, ALU.max))
            first_index(i1, elm, m1, NE)
            link(v.tensor_tensor(hot0, iota_e, per(i1, NE), ALU.is_equal))
            link(v.scalar_tensor_tensor(elm, hot0, 3 * NEG, elm, ALU.mult, ALU.add))
            link(v.tensor_reduce(m2, elm, AX_X, ALU.max))
            first_index(i2, elm, m2, NE)
            link(v.tensor_tensor(hot1, iota_e, per(i2, NE), ALU.is_equal))
            v.tensor_tensor(hot_both, hot0, hot1, ALU.add).then_inc(rt_step, 1)
            v.tensor_tensor(dm, m2, m1, ALU.subtract).then_inc(rt_step, 1)
            dve.wait_ge(act_step, 3)
            link(v.tensor_reduce(gsum, ge5, AX_X, ALU.add))
            link(v.reciprocal(gw, gsum))
            dve.wait_ge(act_step, 4)
            link(v.tensor_scalar(den, e2, 1.0, None, ALU.add))
            link(v.reciprocal(rden, den))
            link(v.tensor_tensor(w0, gw, rden, ALU.mult))
            link(v.tensor_tensor(w1, w0, e2, ALU.mult))

            dve.wait_ge(rank_full, 1)
            rank = ps[3][:, 0:NT * NE].rearrange("p (t e) -> p t e", t=NT)
            total = ps[3][:, NT * NE:(NT + 1) * NE]
            nov, incl, delta, zero_e = rsE[0], rsE[1], rsE[2], rsE[3]
            v.memset(zero_e, 0.0)
            link(v.tensor_tensor(nov_t, total.unsqueeze(2).to_broadcast([P, NE, M_OVER]),
                                 thr.unsqueeze(1).to_broadcast([P, NE, M_OVER]), ALU.is_gt))
            link(v.tensor_reduce(nov, nov_t, AX_X, ALU.add))
            link(v.tensor_tensor_scan(incl, nov, zero_e, 0.0, ALU.add, ALU.add))
            link(v.tensor_tensor(delta, incl, nov, ALU.subtract))
            link(v.tensor_tensor(delta, delta, iota_e[:, 0, :], ALU.subtract))
            link(v.tensor_scalar(delta, delta, float(NE - 1), float(CAP), ALU.add, ALU.mult))
            link(v.tensor_scalar(elm, rank, float(CAP), None, ALU.is_ge))
            link(v.tensor_tensor(elm, elm, delta.unsqueeze(1).to_broadcast([P, NT, NE]), ALU.mult))
            link(v.tensor_tensor(elm, elm, rank, ALU.add))
            link(v.scalar_tensor_tensor(elm, iota_e, float(CAP), elm, ALU.mult, ALU.add))
            for j, (hot, p) in enumerate(((hot0, p0), (hot1, p1))):
                link(v.tensor_tensor(r_tmp, hot, elm, ALU.mult))
                link(v.tensor_reduce(p, r_tmp, AX_X, ALU.add))
                link(v.tensor_copy(rows[:, :, j], p))
            big = rt[:, 0:N_OVER * NE].rearrange("p (s e) -> p s e", e=NE)
            link(v.tensor_tensor(big, incl.unsqueeze(1).to_broadcast([P, N_OVER, NE]),
                                 rowi.unsqueeze(2).to_broadcast([P, N_OVER, NE]), ALU.is_le))
            link(v.tensor_reduce(ovs, big, AX_X, ALU.add))
            link(v.tensor_scalar(ovs, ovs, float(NE - 1), None, ALU.min))
            v.tensor_copy(rti[0:1, 0:N_OVER], ovs[0:1, :])
            v.tensor_copy(rti[0:1, N_OVER:N_OVER + 1], incl[0:1, NE - 1:NE]).then_inc(pos_ok, 1)

            def hidden(n, at, last_down):
                if last_down is not None:
                    dve.wait_ge(dn_full, last_down)
                dve.wait_ge(silu_ok, at)
                v.tensor_tensor(hid[n % 2], act_g[n % 2], ps[1 + 2 * (n % 2)][:, DF // P * CAP:2 * (DF // P) * CAP], ALU.mult)\
                    .then_inc(hid_ok, 1)

            def slot_out(n, at, stored):
                if stored is not None:
                    dve.wait_ge(ysl_out[n % 2], stored)
                dve.wait_ge(y_full, at)
                b = 4 + 2 * (n % 2)
                v.tensor_copy(ysl[n % 2][0:CAP, 0:BANK], ps[b][0:CAP, :])
                v.tensor_copy(ysl[n % 2][0:CAP, BANK:D], ps[b + 1][0:CAP, :]).then_inc(ysl_ok, 1)

            def group(i):
                fixed = isinstance(i, int)
                for s in range(NES):
                    hidden(s, i * NES + (s + 1), None if fixed and i * NES + s < 2 else i * NES + (s - 1))
                    if not (fixed and i * NES + s < 2):
                        stored = i * 32 + ((s - 4) // 2 + 1) * 16
                        slot_out(s - 2, i * NES + (s - 1), None if fixed and i * NES + s < 4 else stored)

            group(0)
            with dve.Fori(1, NE // NES - 1) as i:
                group(i)
            group(NE // NES - 1)
            for n in (NE - 2, NE - 1):
                slot_out(n, n + 1, 16 * (n // 2))
            for q in range(2):
                dve.wait_ge(ysl_out[q], 16 * NE // 2)
            over = dve.value_load(rti[0:1, N_OVER:N_OVER + 1], min_val=0, max_val=N_OVER)
            with dve.If(over > 0):
                with dve.Fori(0, N_OVER) as i:
                    hidden(0, i + (NE + 1), i + NE)
                    slot_out(0, i + (NE + 1), i * 16 + 8 * NE)

            for t in range(NT):
                q = t % 2
                dve.wait_ge(yg_in[q], 32 * (t // 2 + 1))
                link(v.scalar_tensor_tensor(x1[:, t, :], yg[2 * q], w0[:, t:t + 1], x1[:, t, :], ALU.mult, ALU.add))
                v.scalar_tensor_tensor(x1[:, t, :], yg[2 * q + 1], w1[:, t:t + 1], x1[:, t, :], ALU.mult, ALU.add)\
                    .then_inc(yg_used, 1)

        @block.gpsimd
        def _(pool):
            g = nc.gpsimd
            made = [0]

            def made_const(ins):
                made[0] += 1
                ins.then_inc(const_ok, 1)
                pool.wait_ge(const_ok, made[0])

            def band(dst, value, tests, fill=0.0):
                made_const(g.memset(dst, value))
                for pattern, base, mult in tests:
                    made_const(g.affine_select(out=dst, in_=dst, compare_op=ALU.is_ge, fill=fill, base=base,
                                               pattern=pattern, channel_multiplier=mult))

            band(ident, 1.0, [([[-1, P]], 0, 1), ([[1, P]], 0, -1)])
            g.dma_start(g_x, a["attn_norm_g"].partition_broadcast(P)).then_inc(g_norm_in, 16)
            g.dma_start(g_mem, a["mem_norm_g"].partition_broadcast(P)).then_inc(g_norm_in, 16)
            gains = [(g_ki[:, :], "idx_k_norm_g"), (g_ka[:, :], "k_norm_g"),
                     (g_mk[:, :], "mem_k_norm_g")]
            for dst, name in gains:
                g.dma_start(dst, a[name].partition_broadcast(P)).then_inc(gain_in, 16)
            with nc.allow_non_contiguous_dma(reason="a few gains, one per partition"):
                g.dma_start(gcol_q, a["q_norm_g"].rearrange("l d -> d l")).then_inc(gain_in, 16)
                g.dma_start(gcol_o, a["gla_out_norm_g"][0].rearrange("(c d) -> d c", d=P)).then_inc(gain_in, 16)
                g.dma_start(gcol_qm, a["mem_q_norm_g"][0].rearrange("(c d) -> d c", d=P)).then_inc(gain_in, 16)

            g.dma_start(wga[0:RANK, :], a["w_gla_gate_up"][0]).then_inc(gain_in, 16)
            g.dma_start(wga[RANK:RANK + 1, :], a["b_gla_gate_up"]).then_inc(gain_in, 16)

            def result(t):
                pool.wait_ge(yg_used, t + 1)
                dst = o["y_s"].rearrange("b t d -> (b t) d") if t == NTP else o["y_p"][0, t * P:(t + 1) * P, :]
                g.dma_start(dst, x1[:, t, :]).then_inc(out_done, 16)

            band(ones, 1.0, [])
            for cum, suf, n in ((cum_p, suf_p, P // CHUNK), (cum_s, suf_s, B)):
                w = P // n
                band(cum, 1.0 / GATE_TEMP, [([[1, P]], 0, -1), ([[-w, n], [0, w]], 0, 1)])
                band(suf, 1.0 / GATE_TEMP, [([[-1, P]], -1, 1), ([[w, n], [0, w]], w - 1, -1)])
            band(before, 1.0, [([[1, P]], -1, -1)])
            band(other, 0.0, [([[-TB, B], [0, TB]], 0, 1), ([[TB, B], [0, TB]], TB - 1, -1)], NEG)
            band(bsel[:, :], 1.0, [([[-TB, B]], 0, 1), ([[TB, B]], TB - 1, -1)])
            assert made[0] == N_CONST

            for half in range(2):
                for b in range(B):
                    g.dma_start(ci[:, b, :, half * DI:(half + 1) * DI], a["cache_idx_k"][0, b].rearrange("(s p) d -> p s d", p=P))\
                     .then_inc(ci_in, 16)

            g.memset(zrow, 0.0).then_inc(pool_step, 1)
            pool.wait_ge(pool_step, 1)
            g.dma_start(slot_rows.rearrange("(p n) d -> p n d", p=CAP), zrow[0:CAP, :].unsqueeze(1).to_broadcast([CAP, N_SLOT, D]))\
             .then_inc(fill_ok, 16)

            pool.wait_ge(kid_ok, NT)
            g.dma_start(o["ki_p"][0, 0].rearrange("(t p) d -> p t d", p=P), kid[:, 0:NTP, 0:DI]).then_inc(early_out, 16)
            g.dma_start(o["ki_s"][0].rearrange("b t d -> (b t) d"), kid[:, NTP, 0:DI]).then_inc(early_out, 16)

            pool.wait_ge(n_full, len(index["vg"]))
            g.memset(qem, 0.0)
            g.memset(attm_p, 0.0).then_inc(pool_step, 1)
            g.memset(attm_s, 0.0).then_inc(pool_step, 1)
            pool.wait_ge(la_ok, 1)

            def state_in(b):
                g.dma_start(state_s[b % 3], a["state_gla"][0, b].rearrange("h k v -> k h v")).then_inc(st_in[b % 3], 16)

            for b in range(3):
                state_in(b)
            pool.wait_ge(state_ok, 2 * NTP + 1)
            g.dma_start(o["state_p"][0, 0].rearrange("h k v -> k h v"), state).then_inc(early_out, 16)
            for b in range(B):
                pool.wait_ge(states_ok, b + 1)
                g.dma_start(o["state_s"][0, b].rearrange("h k v -> k h v"), state_s[b % 3]).then_inc(st_out[b % 3], 16)
                if b + 3 < B:
                    pool.wait_ge(st_out[b % 3], 16 * (b // 3 + 1))
                    state_in(b + 3)

            def cached(n):
                name, b = ("cache_mem_k", n) if n < B else ("cache_mem_v", n - B)
                if n == 2:
                    pool.wait_ge(qn_ok, normed_before("qm"))
                    pool.wait_ge(qT_full, normed_before("qm"))
                elif 3 <= n < B + 3:
                    pool.wait_ge(kmT_full, 4 * (n - 2))
                elif n >= B + 3:
                    pool.wait_ge(mk_used, n - B - 2)
                g.dma_start(kvb[n % 3], a[name][0, b].rearrange("(m p) h d -> p m (h d)", p=P)).then_inc(kvb_in[n % 3], 16)

            pool.wait_ge(og_ok, NT)
            pool.wait_ge(kvs_full, B)
            for n in range(2):
                cached(n)
            pool.wait_ge(n_free_act, len(by_act))
            g.dma_start(o["mv_p"][0, 0].rearrange("(m p) h d -> p m (h d)", p=P), mv).then_inc(mem_out, 16)
            pool.wait_ge(qn_ok, normed_before("mk"))
            for m in range(NM):
                g.dma_start(o["mk_p"][0, 0].rearrange("(m p) h d -> m p (h d)", p=P)[m], mkn[:, m, :]).then_inc(mem_out, 16)
            for n in range(2, 2 * B):
                cached(n)

            for s in range(4):
                pool.wait_ge(t_full[s], U_MERGE[1] + 4)
            for b in range(B):
                g.dma_start(kc[:, b, :, :], a["cache_k"][0, b].rearrange("(s p) k d -> p s (k d)", p=P)).then_inc(kc_in, 16)
            pool.wait_ge(qn_ok, normed_before("kv"))
            for src, dp, ds in ((kn, "k_p", "k_s"), (va, "v_p", "v_s")):
                g.dma_start(o[dp][0, 0].rearrange("(t p) k d -> p t (k d)", p=P), src[:, 0:NTP, :]).then_inc(kv_out, 16)
                g.dma_start(o[ds][0].rearrange("b t k d -> (b t) (k d)"), src[:, NTP, :]).then_inc(kv_out, 16)
            pool.wait_ge(kcT_full, B)
            for b in range(B):
                g.dma_start(kc[:, b, :, :], a["cache_v"][0, b].rearrange("(s p) k d -> p s (k d)", p=P)).then_inc(vc_in, 16)

            for s in range(4):
                pool.wait_ge(t_full[s], U_MERGE[2] + 4)
            g.dma_start(xr[:, 0:NTP, :], a["x_prompt"][0].rearrange("(t p) d -> p t d", p=P)).then_inc(xr_in, 16)
            g.dma_start(xr[:, NTP, :], xs).then_inc(xr_in, 16)

            pool.wait_ge(x1_ok, 2 * NT)
            f32 = dict(allow_small_or_imprecise_dtypes=True)
            g.iota(iota_e, [[0, NT], [1, NE]], base=0, channel_multiplier=0, **f32)
            g.iota(iota_g, [[0, NT], [1, NG], [0, EPG]], base=0, channel_multiplier=0, **f32)
            g.iota(thr, [[CAP, M_OVER]], base=CAP, channel_multiplier=0, **f32)
            g.iota(rowi, [[1, N_OVER]], base=0, channel_multiplier=0, **f32).then_inc(pool_step, 1)

            pool.wait_ge(pos_ok, 1)
            pool.wait_ge(fill_ok, 16)
            for t in range(NT):
                for j in range(2):
                    g.indirect_dma_start(slot_rows, bass.IndirectOffsetOnAxis(ap=rows[:, t, j:j + 1].bitcast(U32), axis=0),
                                         h2[:, t, :], None).then_inc(scat, 16)

            with pool.Fori(0, NE // NES) as i:
                for s in range(NES):
                    pool.wait_ge(ysl_ok, i * NES + (s + 1))
                    g.dma_start(slot_rows[bass.ds(i * (NES * CAP) + s * CAP, CAP), :], ysl[s % 2][0:CAP, :]).then_inc(ysl_out[s % 2], 16)
            over = pool.value_load(rti[0:1, N_OVER:N_OVER + 1], min_val=0, max_val=N_OVER)
            with pool.If(over > 0):
                with pool.Fori(0, N_OVER) as i:
                    pool.wait_ge(ysl_ok, i + (NE + 1))
                    g.dma_start(slot_rows[bass.ds(i * CAP + NE * CAP, CAP), :], ysl[0][0:CAP, :]).then_inc(ysl_out[0], 16)
                pool.wait_ge(ysl_out[0], 16 * (NE // 2 + N_OVER))
            for q in range(2):
                pool.wait_ge(ysl_out[q], 16 * NE // 2)
            for t in range(NT):
                q = t % 2
                if t >= 2:
                    pool.wait_ge(yg_used, t - 1)
                for j in range(2):
                    g.indirect_dma_start(yg[2 * q + j], None, slot_rows,
                                         bass.IndirectOffsetOnAxis(ap=rows[:, t, j:j + 1].bitcast(U32), axis=0)).then_inc(yg_in[q], 16)
                if t:
                    result(t - 1)
            result(NT - 1)
            pool.wait_ge(out_done, 16 * NT)
            pool.wait_ge(mem_out, 48)
            pool.wait_ge(kv_out, 64)


_INS = ["x_prompt", "x_sample", "mem_prompt", "cache_k", "cache_v", "cache_idx_k", "state_gla", "cache_mem_k",
        "cache_mem_v", "attn_norm_g", "w_in", "q_norm_g", "k_norm_g", "idx_k_norm_g", "w_gla_gate_up", "b_gla_gate_up",
        "gla_out_norm_g", "mem_norm_g", "w_mem_kv", "mem_q_norm_g", "mem_k_norm_g", "w_branch_a", "w_branch_g",
        "w_branch_m", "w_out", "ffn_norm_g", "w_group_router", "b_group_router", "w_expert_router",
        "b_expert_router", "w_exp_gate", "w_exp_up", "w_exp_down"]
_OUTS = [("y_p", "x_prompt"), ("y_s", "x_sample"), ("k_p", None), ("v_p", None), ("ki_p", None), ("state_p", None),
         ("mk_p", None), ("mv_p", None), ("k_s", None), ("v_s", None), ("ki_s", None), ("state_s", "state_gla")]


def kernel(**inputs):
    import numpy as np
    import concourse.bacc as bacc
    from concourse.bass_utils import run_bass_kernel_spmd

    arrays = {n: np.ascontiguousarray(inputs[n]) for n in _INS}
    depth, db, past, kv, hd = arrays["cache_k"].shape
    _, tp, _ = arrays["x_prompt"].shape
    _, tb, _ = arrays["x_sample"].shape
    di = arrays["cache_idx_k"].shape[-1]
    hg, dk, dv = arrays["state_gla"].shape[2:]
    m, hm, hdm = arrays["cache_mem_k"].shape[2:]
    shapes = {"k_p": (depth, 1, tp, kv, hd), "v_p": (depth, 1, tp, kv, hd), "ki_p": (depth, 1, tp, di),
              "state_p": (depth, 1, hg, dk, dv), "mk_p": (depth, 1, m, hm, hdm), "mv_p": (depth, 1, m, hm, hdm),
              "k_s": (depth, db, tb, kv, hd), "v_s": (depth, db, tb, kv, hd), "ki_s": (depth, db, tb, di)}
    nc = bacc.Bacc("TRN2", target_bir_lowering=False, num_devices=1)
    a = {n: nc.dram_tensor(f"in_{n}", arrays[n].shape, F32, kind="ExternalInput").ap() for n in _INS}
    o = {}
    for n, like in _OUTS:
        shape = arrays[like].shape if like else shapes[n]
        o[n] = nc.dram_tensor(f"out_{n}", shape, F32, kind="ExternalOutput").ap()
    build(nc, a, o)
    r = run_bass_kernel_spmd(nc, [{f"in_{n}": x for n, x in arrays.items()}], core_ids=[0])
    return tuple(r.results[0][f"out_{n}"] for n, _ in _OUTS)
```
